# Optimizing a Trainium2 kernel written in Bass

```python
import math
import jax, jax.numpy as jnp
from jax import lax
import numpy as np

D_MODEL = 1024
BATCH = 1
SEQ = 512
DEPTH = 2

GRID_W = 64
CTX_LEN = 256
N_MIXERS = 3
A_HEADS = 8
A_KV_HEADS = 2
A_HEAD_DIM = 128
ROPE_THETA = 10000.0
Q_BLOCK = 128
B_CHUNK = 128
B_GROUPS = 8
B_WIDTH = D_MODEL
C_HEADS = 8
C_HEAD_DIM = D_MODEL // C_HEADS
C_CONV = 3
C_CHUNK = 64
N_EXPERTS = 16
N_GROUPS = 4
TOPK_GROUPS = 1
TOP_K = 2
D_EXPERT = 512
MOE_BLOCK = 256

EPS = 1e-6
DN_ALPHA = (2 * DEPTH) ** 0.25
DN_BETA = (8 * DEPTH) ** -0.25

kernel_name = "hybrid_interleaved_flow_backbone"

def layer_norm(x, g, b):
    xf = x.astype(jnp.float32)
    mu = jnp.mean(xf, -1, keepdims=True)
    var = jnp.mean(jnp.square(xf - mu), -1, keepdims=True)
    return ((xf - mu) * lax.rsqrt(var + EPS) * g + b).astype(x.dtype)

def rms_norm(x, g):
    xf = x.astype(jnp.float32)
    return (xf * lax.rsqrt(jnp.mean(xf * xf, -1, keepdims=True) + EPS) * g).astype(x.dtype)

def l2norm(x):
    return x * lax.rsqrt(jnp.sum(x * x, -1, keepdims=True) + EPS)

def modulate(x, shift, scale):
    return x * (1 + scale[:, None, :]) + shift[:, None, :]

def axial_rope(n):
    rows = n // GRID_W
    half = A_HEAD_DIM // 2
    inv = 1.0 / (ROPE_THETA ** (jnp.arange(0, half, 2, dtype=jnp.float32) / half))
    r = jnp.broadcast_to(jnp.arange(rows, dtype=jnp.float32)[:, None], (rows, GRID_W)).reshape(-1)
    col = jnp.broadcast_to(jnp.arange(GRID_W, dtype=jnp.float32)[None, :], (rows, GRID_W)).reshape(-1)
    ang = jnp.concatenate([r[:, None] * inv, col[:, None] * inv], -1)
    return jnp.cos(ang), jnp.sin(ang)

def apply_rope(x, cos, sin):
    xf = x.astype(jnp.float32).reshape(*x.shape[:-1], -1, 2)
    x1, x2 = xf[..., 0], xf[..., 1]
    c = cos[None, :, None, :]
    s = sin[None, :, None, :]
    return jnp.stack([x1 * c - x2 * s, x1 * s + x2 * c], -1).reshape(x.shape).astype(x.dtype)

def attention_mixer(u_lat, u_ctx, w_qkv, q_g, k_g, w_o, cos, sin, need_ctx):
    b, n, _ = u_lat.shape
    grp = A_HEADS // A_KV_HEADS
    scale = A_HEAD_DIM ** -0.5

    def proj(h):
        qkv = h @ w_qkv
        q, k, v = jnp.split(qkv, [A_HEADS * A_HEAD_DIM, (A_HEADS + A_KV_HEADS) * A_HEAD_DIM], -1)
        q = rms_norm(q.reshape(*h.shape[:2], A_HEADS, A_HEAD_DIM), q_g)
        k = rms_norm(k.reshape(*h.shape[:2], A_KV_HEADS, A_HEAD_DIM), k_g)
        return q, k, v.reshape(*h.shape[:2], A_KV_HEADS, A_HEAD_DIM)

    def attend(q, k, v):
        nq = q.shape[1]
        qg = q.reshape(b, nq, A_KV_HEADS, grp, A_HEAD_DIM)
        s = jnp.einsum("bqkgd,bskd->bkgqs", qg, k, preferred_element_type=jnp.float32) * scale
        p = jax.nn.softmax(s, axis=-1).astype(v.dtype)
        o = jnp.einsum("bkgqs,bskd->bqkgd", p, v)
        return o.reshape(b, nq, A_HEADS * A_HEAD_DIM)

    q_l, k_l, v_l = proj(u_lat)
    q_c, k_c, v_c = proj(u_ctx)
    q_l = apply_rope(q_l, cos, sin)
    k_l = apply_rope(k_l, cos, sin)
    k_all = jnp.concatenate([k_c, k_l], 1)
    v_all = jnp.concatenate([v_c, v_l], 1)
    nb = n // Q_BLOCK
    q_blocks = jnp.moveaxis(q_l.reshape(b, nb, Q_BLOCK, A_HEADS, A_HEAD_DIM), 1, 0)
    o_l = lax.map(lambda qb: attend(qb, k_all, v_all), q_blocks)
    y_lat = jnp.moveaxis(o_l, 0, 1).reshape(b, n, A_HEADS * A_HEAD_DIM) @ w_o
    y_ctx = attend(q_c, k_c, v_c) @ w_o if need_ctx else None
    return y_lat, y_ctx

def chunk_mlp(h, w_in, v_g, v_b, w_s, b_s, w_out):
    b, n, _ = h.shape
    z = jax.nn.gelu(h @ w_in)
    u, v = jnp.split(z, 2, -1)
    v = layer_norm(v, v_g, v_b)
    vg = v.reshape(b, n // B_CHUNK, B_CHUNK, B_GROUPS, B_WIDTH // B_GROUPS)
    mixed = jnp.einsum("gts,bcsgd->bctgd", w_s, vg) + b_s.T[None, None, :, :, None]
    return (u * mixed.reshape(b, n, B_WIDTH)) @ w_out

def short_conv(x, w):
    pad = C_CONV // 2
    return lax.conv_general_dilated(x, w[:, None, :], window_strides=(1,), padding=[(pad, pad)],
                                    dimension_numbers=("NWC", "WIO", "NWC"), feature_group_count=x.shape[-1])

def gated_delta_chunked(q, k, v, g, beta, s0):
    b, n, nh, dk = k.shape
    dv = v.shape[-1]
    nc = n // C_CHUNK

    def to_chunks(t):
        return jnp.moveaxis(t.reshape(b, nc, C_CHUNK, nh, *t.shape[3:]), (1, 2), (0, 3))

    qc, kc, vc = to_chunks(q), to_chunks(k), to_chunks(v)
    gc = jnp.cumsum(to_chunks(g), -1)
    bc = to_chunks(beta)
    idx = jnp.arange(C_CHUNK)
    tril = idx[:, None] >= idx[None, :]
    strict = idx[:, None] > idx[None, :]
    decay = jnp.exp(jnp.where(tril, gc[..., :, None] - gc[..., None, :], -jnp.inf))
    kb = kc * bc[..., None]
    a_mat = jnp.where(strict, jnp.einsum("...id,...jd->...ij", kb, kc) * decay, 0.0)
    eye = jnp.eye(C_CHUNK, dtype=jnp.float32)
    t_inv = lax.linalg.triangular_solve(a_mat + eye, jnp.broadcast_to(eye, a_mat.shape),
                                        left_side=True, lower=True)
    u = t_inv @ (vc * bc[..., None])
    w = t_inv @ (kb * jnp.exp(gc)[..., None])
    attn = jnp.where(tril, jnp.einsum("...id,...jd->...ij", qc, kc) * decay, 0.0)
    q_dec = qc * jnp.exp(gc)[..., None]
    k_dec = kc * jnp.exp(gc[..., -1:] - gc)[..., None]
    g_last = jnp.exp(gc[..., -1])

    def step(s, xs):
        u_i, w_i, attn_i, qd_i, kd_i, gl_i = xs
        v_new = u_i - w_i @ s
        o = qd_i @ s + attn_i @ v_new
        s = s * gl_i[..., None, None] + jnp.swapaxes(kd_i, -1, -2) @ v_new
        return s, o

    s_fin, o = lax.scan(step, s0, (u, w, attn, q_dec, k_dec, g_last))
    o = jnp.moveaxis(o, (0, 3), (1, 2)).reshape(b, n, nh, dv)
    return o, s_fin

def deltanet_mixer(u_lat, u_ctx, w_in, conv_w, a_log, dt_bias, norm_g, w_out, need_ctx):
    cw = C_HEADS * C_HEAD_DIM
    f32 = jnp.float32

    def prep(h):
        b, n, _ = h.shape
        proj = h @ w_in
        qkv = jax.nn.silu(short_conv(proj[..., :3 * cw], conv_w)).astype(f32)
        q, k, v = [t.reshape(b, n, C_HEADS, C_HEAD_DIM) for t in jnp.split(qkv, 3, -1)]
        q = l2norm(q) * (C_HEAD_DIM ** -0.5)
        k = l2norm(k)
        z = proj[..., 3 * cw:4 * cw].astype(f32).reshape(b, n, C_HEADS, C_HEAD_DIM)
        ab = proj[..., 4 * cw:].astype(f32).reshape(b, n, 2, 2, C_HEADS)
        g = -jnp.exp(a_log.astype(f32)) * jax.nn.softplus(ab[:, :, 0] + dt_bias.astype(f32))
        beta = jax.nn.sigmoid(ab[:, :, 1])
        return q, k, v, g, beta, z

    def bidir(q, k, v, g, beta, s_f, s_b):
        flip = lambda t: jnp.flip(t, 1)
        o_f, s_f = gated_delta_chunked(q, k, v, g[:, :, 0], beta[:, :, 0], s_f)
        o_b, s_b = gated_delta_chunked(flip(q), flip(k), flip(v), flip(g[:, :, 1]), flip(beta[:, :, 1]), s_b)
        return o_f + flip(o_b), s_f, s_b

    def out(o, z, dtype):
        y = rms_norm(o, norm_g) * jax.nn.silu(z)
        return y.reshape(*y.shape[:2], cw).astype(dtype) @ w_out

    qc, kc, vc, gc, bc, zc = prep(u_ctx)
    s0 = jnp.zeros((u_ctx.shape[0], C_HEADS, C_HEAD_DIM, C_HEAD_DIM), f32)
    o_ctx, s_f, s_b = bidir(qc, kc, vc, gc, bc, s0, s0)
    ql, kl, vl, gl, bl, zl = prep(u_lat)
    o_lat, _, _ = bidir(ql, kl, vl, gl, bl, s_f, s_b)
    y_lat = out(o_lat, zl, u_lat.dtype)
    y_ctx = out(o_ctx, zc, u_ctx.dtype) if need_ctx else None
    return y_lat, y_ctx

def moe_ffn(t, w_router, router_bias, w_gate, w_up, w_down):
    n_tok, d = t.shape
    per = N_EXPERTS // N_GROUPS
    scores = jax.nn.sigmoid((t @ w_router).astype(jnp.float32))
    sel = scores + router_bias.astype(jnp.float32)
    grp_score = lax.top_k(sel.reshape(n_tok, N_GROUPS, per), 2)[0].sum(-1)
    _, gidx = lax.top_k(grp_score, TOPK_GROUPS)
    gmask = jnp.any(gidx[..., None] == jnp.arange(N_GROUPS), axis=1)
    emask = jnp.repeat(gmask, per, axis=1)
    _, eidx = lax.top_k(jnp.where(emask, sel, -jnp.inf), TOP_K)
    wts = jnp.take_along_axis(scores, eidx, 1)
    wts = wts / jnp.sum(wts, -1, keepdims=True)
    n_asg = n_tok * TOP_K
    e_flat = eidx.reshape(-1)
    tok_flat = jnp.repeat(jnp.arange(n_tok, dtype=jnp.int32), TOP_K)
    order = jnp.argsort(e_flat)
    e_s, tok_s, w_s = e_flat[order], tok_flat[order], wts.reshape(-1)[order]
    counts = jnp.zeros((N_EXPERTS,), jnp.int32).at[e_flat].add(1)
    padded = (counts + MOE_BLOCK - 1) // MOE_BLOCK * MOE_BLOCK
    start = jnp.cumsum(counts) - counts
    pend = jnp.cumsum(padded)
    pstart = pend - padded
    dest = pstart[e_s] + jnp.arange(n_asg, dtype=jnp.int32) - start[e_s]
    n_blocks = -(-(n_asg + N_EXPERTS * (MOE_BLOCK - 1)) // MOE_BLOCK)
    n_rows = n_blocks * MOE_BLOCK
    row_tok = jnp.full((n_rows,), n_tok, jnp.int32).at[dest].set(tok_s)
    row_w = jnp.zeros((n_rows,), jnp.float32).at[dest].set(w_s)
    block_e = jnp.minimum(jnp.searchsorted(pend, jnp.arange(n_blocks) * MOE_BLOCK, side="right"), N_EXPERTS - 1)
    t_pad = jnp.concatenate([t, jnp.zeros((1, d), t.dtype)], 0)
    xb = t_pad[row_tok].reshape(n_blocks, MOE_BLOCK, d)

    def expert_block(args):
        xblk, e = args
        hid = jax.nn.silu(xblk @ w_gate[e]) * (xblk @ w_up[e])
        return hid @ w_down[e]

    yb = lax.map(expert_block, (xb, block_e)).reshape(n_rows, d)
    y = jnp.zeros((n_tok + 1, d), jnp.float32).at[row_tok].add(yb.astype(jnp.float32) * row_w[:, None])
    return y[:n_tok].astype(t.dtype)

def setup_inputs(seed: int = 0) -> dict:
    key = jax.random.key(seed)
    keys = jax.random.split(key, 40)
    ctr = [0]
    f32 = jnp.float32

    def nxt():
        ctr[0] += 1
        return keys[ctr[0] - 1]

    def nrm(shape, scale=1.0):
        return jax.random.normal(nxt(), shape, f32) * scale

    d = D_MODEL
    n_a = len(range(0, DEPTH, N_MIXERS))
    n_b = len(range(1, DEPTH, N_MIXERS))
    n_c = len(range(2, DEPTH, N_MIXERS))
    a_cols = (A_HEADS + 2 * A_KV_HEADS) * A_HEAD_DIM
    a_w = A_HEADS * A_HEAD_DIM
    cw = C_HEADS * C_HEAD_DIM
    dt = jnp.exp(jax.random.uniform(nxt(), (n_c, 2, C_HEADS), f32, math.log(1e-3), math.log(1e-1)))
    return {
        "x": nrm((BATCH, SEQ, d)),
        "c": nrm((BATCH, d)),
        "ctx": nrm((BATCH, CTX_LEN, d)),
        "c_ctx": nrm((d,)),
        "w_ada": nrm((DEPTH, d, 6 * d), d ** -0.5),
        "b_ada": nrm((DEPTH, 6 * d), 0.02),
        "ln_g": 1.0 + nrm((DEPTH, 2, d), 0.02),
        "ln_b": nrm((DEPTH, 2, d), 0.02),
        "a_wqkv": nrm((n_a, d, a_cols), d ** -0.5),
        "a_qg": 1.0 + nrm((n_a, A_HEAD_DIM), 0.02),
        "a_kg": 1.0 + nrm((n_a, A_HEAD_DIM), 0.02),
        "a_wo": nrm((n_a, a_w, d), a_w ** -0.5 * DN_BETA),
        "b_win": nrm((n_b, d, 2 * B_WIDTH), d ** -0.5),
        "b_vg": 1.0 + nrm((n_b, B_WIDTH), 0.02),
        "b_vb": nrm((n_b, B_WIDTH), 0.02),
        "b_ws": nrm((n_b, B_GROUPS, B_CHUNK, B_CHUNK), B_CHUNK ** -0.5),
        "b_bs": 1.0 + nrm((n_b, B_GROUPS, B_CHUNK), 0.02),
        "b_wout": nrm((n_b, B_WIDTH, d), B_WIDTH ** -0.5 * DN_BETA),
        "c_win": nrm((n_c, d, 4 * cw + 4 * C_HEADS), d ** -0.5),
        "c_conv": nrm((n_c, C_CONV, 3 * cw), C_CONV ** -0.5),
        "c_alog": jnp.log(jax.random.uniform(nxt(), (n_c, 2, C_HEADS), f32, 1.0, 16.0)),
        "c_dtb": dt + jnp.log(-jnp.expm1(-dt)),
        "c_ng": 1.0 + nrm((n_c, C_HEAD_DIM), 0.02),
        "c_wout": nrm((n_c, cw, d), cw ** -0.5 * DN_BETA),
        "w_router": nrm((d, N_EXPERTS), d ** -0.5),
        "router_bias": nrm((N_EXPERTS,), 0.01),
        "e_gate": nrm((DEPTH, N_EXPERTS, d, D_EXPERT), d ** -0.5),
        "e_up": nrm((DEPTH, N_EXPERTS, d, D_EXPERT), d ** -0.5),
        "e_down": nrm((DEPTH, N_EXPERTS, D_EXPERT, d), D_EXPERT ** -0.5 * DN_BETA),
    }

def reference(x, c, ctx, c_ctx, w_ada, b_ada, ln_g, ln_b,
              a_wqkv, a_qg, a_kg, a_wo,
              b_win, b_vg, b_vb, b_ws, b_bs, b_wout,
              c_win, c_conv, c_alog, c_dtb, c_ng, c_wout,
              w_router, router_bias, e_gate, e_up, e_down):
    d = x.shape[-1]
    cos, sin = axial_rope(x.shape[1])
    s_lat = jax.nn.silu(c)
    s_ctx = jax.nn.silu(c_ctx)[None]
    h, hc = x, ctx
    for i in range(DEPTH):
        last = i == DEPTH - 1
        m, j = i % N_MIXERS, i // N_MIXERS
        sh1, sc1, g1, sh2, sc2, g2 = jnp.split(s_lat @ w_ada[i] + b_ada[i], 6, -1)
        csh1, csc1, cg1, csh2, csc2, cg2 = jnp.split(s_ctx @ w_ada[i] + b_ada[i], 6, -1)
        u = modulate(h, sh1, sc1)
        uc = modulate(hc, csh1, csc1)
        if m == 0:
            y, yc = attention_mixer(u, uc, a_wqkv[j], a_qg[j], a_kg[j], a_wo[j], cos, sin, not last)
        elif m == 1:
            y = chunk_mlp(u, b_win[j], b_vg[j], b_vb[j], b_ws[j], b_bs[j], b_wout[j])
            yc = None if last else chunk_mlp(uc, b_win[j], b_vg[j], b_vb[j], b_ws[j], b_bs[j], b_wout[j])
        else:
            y, yc = deltanet_mixer(u, uc, c_win[j], c_conv[j], c_alog[j], c_dtb[j], c_ng[j], c_wout[j], not last)
        h = layer_norm(DN_ALPHA * h + g1[:, None, :] * y, ln_g[i, 0], ln_b[i, 0])
        if not last:
            hc = layer_norm(DN_ALPHA * hc + cg1[:, None, :] * yc, ln_g[i, 0], ln_b[i, 0])
        u = modulate(h, sh2, sc2)
        if last:
            y = moe_ffn(u.reshape(-1, d), w_router, router_bias, e_gate[i], e_up[i], e_down[i]).reshape(h.shape)
            h = layer_norm(DN_ALPHA * h + g2[:, None, :] * y, ln_g[i, 1], ln_b[i, 1])
        else:
            uc = modulate(hc, csh2, csc2)
            n_lat_tok = u.shape[0] * u.shape[1]
            yt = moe_ffn(jnp.concatenate([u.reshape(-1, d), uc.reshape(-1, d)], 0),
                         w_router, router_bias, e_gate[i], e_up[i], e_down[i])
            y = yt[:n_lat_tok].reshape(h.shape)
            yc = yt[n_lat_tok:].reshape(hc.shape)
            h = layer_norm(DN_ALPHA * h + g2[:, None, :] * y, ln_g[i, 1], ln_b[i, 1])
            hc = layer_norm(DN_ALPHA * hc + cg2[:, None, :] * yc, ln_g[i, 1], ln_b[i, 1])
    return h


_drawn_inputs = setup_inputs


def setup_inputs(seed=0):
    import zlib

    import numpy as np

    out = dict(_drawn_inputs(seed))
    spreads = {}
    factors = {'a_qg': 5.042, 'a_kg': 8.0, 'b_vg': 8.0, 'b_vb': 17.096, 'b_bs': 15.942}
    for name, (base, spread) in spreads.items():
        noise = np.random.default_rng([zlib.crc32(name.encode()), seed]).standard_normal(out[name].shape)
        drawn = base * np.exp(spread * noise) if base else spread * noise
        out[name] = __import__('jax').numpy.asarray(drawn.astype(out[name].dtype))
    for name, factor in factors.items():
        out[name] = (out[name] * factor).astype(out[name].dtype)
    return out
```

```python
from contextlib import ExitStack

import concourse.bass as bass
from concourse import mybir

ALU = mybir.AluOpType
ACT = mybir.ActivationFunctionType
AX = mybir.AxisListType
F32 = mybir.dt.float32
I32 = mybir.dt.int32

P = 128
EPS = 1e-6
RING = 6
BLK = 64
BIG = 1e30


def backbone(nc, x, c, ctx_tok, c_ctx, w_ada, b_ada, ln_g, ln_b, a_wqkv, a_qg, a_kg, a_wo, b_win, b_vg, b_vb, b_ws,
             b_bs, b_wout, w_router, router_bias, e_gate, e_up, e_down, rope_cos, rope_sin, out):
    D = x.shape[2]
    NT = x.shape[1] // P
    NX = ctx_tok.shape[1] // P
    DC = D // P
    DEPTH = w_ada.shape[0]
    ALPHA = float((2 * DEPTH) ** 0.25)
    HD = a_qg.shape[1]
    NH = a_wo.shape[1] // HD
    NKV = (a_wqkv.shape[2] // HD - NH) // 2
    NKT = NX + NT
    SCALE = float(HD) ** -0.5
    NE = w_router.shape[1]
    NG = 4
    PER = NE // NG
    FE = e_gate.shape[3]
    FC = FE // P
    TOK = NT * P
    MAXB = NE + (2 * TOK - NE) // BLK
    ROWB = MAXB + 2
    SH1, SC1, G1, SH2, SC2, G2 = range(0, 6 * DC, DC)
    assert D == 1024 and NT == 4 and NX == 2 and HD == P and NH == 8 and NKV == 2 and FE == 512 and DEPTH == 2

    hscr = [nc.dram_tensor(f"tokens_{l}", [TOK, D], F32).ap() for l in range(DEPTH)]
    yscr = [nc.dram_tensor(f"expert_rows_{l}", [ROWB * BLK, D], F32).ap() for l in range(DEPTH)]

    with ExitStack() as st:
        def sb(name, shape, dt=F32):
            return st.enter_context(nc.sbuf_tensor(name, shape, dt))

        def sem(name):
            return st.enter_context(nc.semaphore(name))

        ring = sb("ring", [P, RING, 4096])
        H = sb("H", [P, NT, D])
        uT = sb("uT", [P, DC, TOK])
        RD = sb("RD", [P, 4096])
        RE = sb("RE", [P, 4096])
        RF = sb("RF", [P, 3072])
        RW = sb("RW", [P, 3072])
        LG = sb("LG", [P, D])
        LB = sb("LB", [P, D])
        G = sb("G", [P, D])
        ident = sb("ident", [P, P])
        ones = sb("ones", [P, P])
        tri = sb("tri", [P, P])
        ctxn = RD[:, 0:2048].rearrange("p (t d) -> p t d", t=NX)
        ucT = RD[:, 2048:4096].rearrange("p (c t) -> p c t", c=DC)
        PT = RD[:, 0:NKT * TOK].rearrange("p (k q) -> p k q", k=NKT)
        zu = RD[:, :].rearrange("p (t d) -> p t d", t=NT)
        yg = RD[:, :].rearrange("p (b k d) -> p b k d", b=2, k=2)
        qT = RE[:, :].rearrange("p (h q) -> p h q", h=NH)
        zv = RE[:, :].rearrange("p (t d) -> p t d", t=NT)
        kT = RF[:, 0:1536].rearrange("p (h k) -> p h k", h=NKV)
        V = RF[:, 1536:3072].rearrange("p (k d) -> p k d", k=NKT)
        ws = RF[:, 0:1024].rearrange("p (g s) -> p g s", g=8)
        wsT = RF[:, 1024:2048].rearrange("p (g s) -> p g s", g=8)
        xn, t1, t2, rot, junk = (RW[:, 512 * i:512 * i + 512] for i in range(5))
        Pb = RW[:, 0:2304].rearrange("p (b k) -> p b k", b=3)
        gcb = RW[:, 0:1024].rearrange("p (c m) -> p c m", c=DC)
        lt = RW[:, 0:2048].rearrange("p (b d) -> p b d", b=2)
        ropeC = LG[:, 0:512].rearrange("p (t d) -> p t d", t=NT)
        ropeS = LG[:, 512:1024].rearrange("p (t d) -> p t d", t=NT)
        xg = RE[0:BLK, 0:1024]
        xT = RE[:, 1024:1536].rearrange("p (c s) -> p c s", c=DC)
        xTt = RE[:, 1536:2048].rearrange("p (c s) -> p c s", c=DC)
        gs = RE[0:BLK, 2048:2560]
        hid = RE[0:BLK, 2560:3072]
        hidT = RE[:, 3072:3328].rearrange("p (k s) -> p k s", k=FC)
        ysb = RE[:, 3328:3840]
        oh = RW[:, 2048:2304].rearrange("p (t s) -> p t s", t=NT)
        oh2t = RW[:, 2304:2560].rearrange("p (t s) -> p t s", t=NT)

        silu_c = sb("silu_c", [P, DC, 2])
        craw = sb("craw", [P, 2, DC])
        brow = sb("brow", [96, P])
        bsrow = sb("bsrow", [8, P])
        badaT = sb("badaT", [P, 2, 48])
        bsT = sb("bsT", [P, 8])
        mod = [sb(f"mod{l}", [P, 48]) for l in range(DEPTH)]
        modc = sb("modc", [P, 16])
        qg = sb("qg", [P, HD])
        kg = sb("kg", [P, HD])
        wr = sb("wr", [P, DC, NE])
        rb = sb("rb", [P, NE])
        ss = sb("ss", [P, 4])
        ms = sb("ms", [P, 4])
        rt = sb("rt", [P, 4])
        rs = sb("rs", [P, 4])
        nt = sb("nt", [P, 4])
        mx = sb("mx", [P, 4])
        nmx = sb("nmx", [P, 4])
        den = sb("den", [P, 4])
        rden = sb("rden", [P, 4])
        st6 = sb("st6", [P, 2, 6])
        mv = sb("mv", [P, 2])
        sc_ = sb("sc_", [P, NT, NE])
        sel = sb("sel", [P, NT, NE])
        s6 = sb("s6", [P, 16, 6])
        g4 = sb("g4", [P, NT, NG])
        gm1 = sb("gm1", [P, NT])
        gmask = sb("gmask", [P, NT, NG])
        cand = sb("cand", [P, NT, NE])
        o1 = sb("o1", [P, NT, NE])
        o2 = sb("o2", [P, NT, NE])
        MP = sb("MP", [P, NT + 1, NE])
        wts = sb("wts", [P, 2, NT])
        wsum = sb("wsum", [P, NT])
        gt7 = sb("gt7", [P, NE, 7])
        nbk = sb("nbk", [P, NE])
        bs = sb("bs", [P, NE + 2])
        bs64 = sb("bs64", [P, NE + 1])
        smap = sb("smap", [P, NT, NE])
        slot = sb("slot", [P, 2, NT])
        srel = sb("srel", [P, 2, NT])
        yidx = sb("yidx", [P, 2, NT], I32)
        table = [sb(f"table{l}", [1, NE + 2], I32) for l in range(DEPTH)]
        gidx = sb("gidx", [P, 1], I32)
        ic = sb("ic", [P, 64 + 16 + 4 + 4 + 7], I32)
        fc = sb("fc", [P, 64 + 16 + 4 + 4 + 7])
        iota64, dec16, dec4, tokid, thr = fc[:, 0:64], fc[:, 64:80], fc[:, 80:84], fc[:, 84:88], fc[:, 88:95]

        PS = st.enter_context(nc.psum_tensor("PS", [P, 8, 512], F32))

        static0 = ([("ada", 0, q) for q in range(4)] + [("qkv", 0, n) for n in (2, 0, 1)]
                   + [("ada", 0, q) for q in range(4, 12)] + [("ada", 1, q) for q in range(12)]
                   + [("wo", 0, 0), ("wo", 0, 1)])
        static1 = [("win", 0, n) for n in (2, 3, 0, 1)] + [("wout", 0, 0), ("wout", 0, 1)]
        S0, S1 = len(static0), len(static1)
        base_moe = [S0, S0 + 3 * NE + S1]
        base_s1 = S0 + 3 * NE

        def slot_of(n):
            return ring[:, n % RING, :]

        w_in = [sem(f"weights_in_{b}") for b in range(RING)]
        s_c = sem("cond_loaded")
        s_x = sem("x_loaded")
        s_ctx = sem("ctx_loaded")
        s_small = sem("small_loaded")
        s_lnw = sem("ln_weights_loaded")
        s_ws = sem("spatial_weights_loaded")
        s_const = sem("constants_ready")
        s_ic = sem("iota_ready")
        s_silu = sem("silu_c_ready")
        s_bT_pe = sem("bias_rows_turned")
        s_bT = sem("bias_cols_ready")
        ada_pe, ada_ev = sem("ada_in_psum"), sem("ada_ready")
        tr_pe, tr_act, tr_dve = sem("turned_in_psum"), sem("turned_by_act"), sem("turned_by_dve")
        qkv_pe, sq_done, ms_done, sqrt_done = sem("qkv_in_psum"), sem("squares_done"), sem("meansq_ready"), sem("sqrt_ready")
        xn_done, t1_done, rot_done = sem("normed"), sem("rope_cos_part"), sem("rotated")
        qkT_pe, qk_ev = sem("qk_turned_in_psum"), sem("qkT_ready")
        s_pe, nm, exp_done, p_norm = sem("scores_in_psum"), sem("negmax_ready"), sem("exp_done"), sem("probs_ready")
        t_pe, pt_act, pt_dve = sem("probs_turned_in_psum"), sem("probsT_by_act"), sem("probsT_by_dve")
        pv_pe, o_ev = sem("attn_out_in_psum"), sem("attn_out_ready")
        gc_rd, gb_pe, gb_ev = sem("gate_cols_spread"), sem("gate_rows_in_psum"), sem("gate_rows_ready")
        y_pe = [sem(f"mixer_out_in_psum_{l}") for l in range(DEPTH)]
        var_rd, std_rd, ln_nrm, ln_rd = sem("ln_var_ready"), sem("ln_std_ready"), sem("ln_normed"), sem("ln_tile_ready")
        pgl = sem("ln_gain_applied")
        z_pe, z_ev = sem("mlp_in_psum"), sem("gelu_done")
        vn, vg1, v_rd = sem("v_normed"), sem("v_gain_applied"), sem("v_ready")
        wsT_pe, wsT_ev = sem("spatial_turned_in_psum"), sem("spatialT_ready")
        mix_pe, mix_ev = sem("mixed_in_psum"), sem("gated_ready")
        s_hw = [sem(f"tokens_stored_{l}") for l in range(DEPTH)]
        lg_pe, sig_rd, m_rd, rk_pe, tab_rd = (sem("logits_in_psum"), sem("scores_ready"), sem("choice_ready"),
                                              sem("ranks_in_psum"), sem("table_ready"))
        L = range(DEPTH)
        oh_rd = [sem(f"onehot_ready_{l}") for l in L]
        ix_pe = [sem(f"index_in_psum_{l}") for l in L]
        ix_rd = [sem(f"index_ready_{l}") for l in L]
        xg_in = [sem(f"gathered_{l}") for l in L]
        xt_pe = [sem(f"gathered_turned_{l}") for l in L]
        xT_rd = [sem(f"block_xT_ready_{l}") for l in L]
        gu = [[sem(f"gate_up_{h}_in_psum_{l}") for h in range(2)] for l in L]
        silu_rd = [[sem(f"silu_{h}_ready_{l}") for h in range(2)] for l in L]
        hid_rd = [[sem(f"hidden_{h}_ready_{l}") for h in range(2)] for l in L]
        ht_pe = [[sem(f"hidden_{h}_turned_{l}") for h in range(2)] for l in L]
        ht_rd = [[sem(f"hiddenT_{h}_ready_{l}") for h in range(2)] for l in L]
        dn_pe = [sem(f"block_out_in_psum_{l}") for l in L]
        y_ev = [sem(f"block_out_ready_{l}") for l in L]
        y_st = [sem(f"block_out_stored_{l}") for l in L]
        y_fill = [sem(f"unused_rows_filled_{l}") for l in L]
        dlp = [sem(f"dve_loop_chain_{l}") for l in L]
        fg = [[sem(f"expert_rows_in_{l}_{b}") for b in range(2)] for l in L]
        fg_used = sem("expert_rows_used")
        s_out = sem("out_stored")
        chain = sem("dve_chain")
        pchain = sem("pool_chain")
        achain = sem("act_chain")

        block = st.enter_context(nc.Block())

        def tr_wait(eng, i):
            eng.wait_ge(tr_dve if i % 2 else tr_act, i // 2 + 1)

        TR_X, TR_C, TR_R0, TR_M1, TR_P1, TR_R1 = 0, 8, 16, 24, 32, 40

        @block.sync
        def _(sp):
            wqkv = a_wqkv[0].rearrange("(k p) n -> p k n", p=P)
            wo = a_wo[0].rearrange("(k p) n -> p k n", p=P)
            win = b_win[0].rearrange("(k p) n -> p k n", p=P)
            wout = b_wout[0].rearrange("(k p) n -> p k n", p=P)
            ada = [w_ada[l].rearrange("(p k) n -> p k n", k=DC) for l in range(DEPTH)]
            view = {"qkv": wqkv, "wo": wo, "win": win, "wout": wout}

            def load_static(n, kind, l, q):
                src = (ada[l] if kind == "ada" else view[kind])[:, :, 512 * q:512 * q + 512]
                sp.dma_start(slot_of(n).rearrange("p (k n) -> p k n", k=DC), src).then_inc(w_in[n % RING], 16)

            def load_expert(n, l, e, j):
                dst = slot_of(n)
                if j < 2:
                    src = (e_gate, e_up)[j][l, e].rearrange("(k p) n -> p k n", p=P)
                    dst = dst.rearrange("p (k n) -> p k n", k=DC)
                else:
                    src = e_down[l, e].rearrange("(k p) n -> p k n", p=P)
                    dst = dst.rearrange("p (k n) -> p k n", k=FC)
                sp.dma_start(dst, src).then_inc(w_in[n % RING], 16)

            def wait_used(ch):
                kind, l, q = ch
                if kind == "ada":
                    sp.wait_ge(ada_pe, 12 * l + q + 1)
                elif kind == "qkv":
                    sp.wait_ge(qkv_pe, {2: NKT, 0: NKT + NT, 1: NKT + 2 * NT}[q])
                elif kind == "win":
                    sp.wait_ge(z_pe, NT * ((q + 2) % 4 + 1))
                else:
                    sp.wait_ge(y_pe[0 if kind == "wo" else 1], NT * (q + 1))

            for l in range(DEPTH):
                if l == 0:
                    for n, ch in enumerate(static0):
                        if n >= RING:
                            wait_used(static0[n - RING])
                        load_static(n, *ch)
                else:
                    for i, ch in enumerate(static1):
                        e_last, j = NE - 2 + i // 3, i % 3
                        last = sp.value_load(table[l - 1][0:1, e_last + 1:e_last + 2], min_val=1, max_val=MAXB)
                        sp.wait_ge(dn_pe[l - 1] if j == 2 else gu[l - 1][1], last)
                        load_static(base_s1 + i, *ch)
                for i in range(RING):
                    wait_used((static0, static1)[l][i - RING])
                    load_expert(base_moe[l] + i, l, i // 3, i % 3)
                sp.wait_ge(tab_rd, l + 1)
                total = sp.value_load(table[l][0:1, NE:NE + 1], min_val=1, max_val=MAXB)
                with sp.Fori(total, ROWB - 1) as b:
                    sp.dma_start(yscr[l][bass.ds(b * BLK, BLK), :], H[0:BLK, 0, :]).then_inc(y_fill[l], 16)
                with sp.Fori(1, NE // 2) as pair:
                    for par in range(2):
                        e = pair * 2 + par
                        last = sp.value_load(table[l][0:1, bass.ds(pair * 2 + (par - 1), 1)], min_val=1, max_val=MAXB)
                        for j in range(3):
                            sp.wait_ge(dn_pe[l] if j == 2 else gu[l][1], last)
                            load_expert(base_moe[l] + 3 * par + j, l, e, j)

        @block.gpsimd
        def _(pool):
            nchain = [0]

            def link(ins):
                nchain[0] += 1
                ins.then_inc(pchain, 1)
                pool.wait_ge(pchain, nchain[0])

            nc.gpsimd.memset(ident[:, :], 0.0).then_inc(pchain, 1)
            nc.gpsimd.memset(ones[:, :], 1.0).then_inc(pchain, 1)
            nchain[0] = 2
            pool.wait_ge(pchain, 2)
            nc.gpsimd.affine_select(out=ident[:, :], in_=ident[:, :], compare_op=ALU.not_equal, fill=1.0, base=0,
                                    pattern=[[-1, P]], channel_multiplier=1).then_inc(s_const, 1)
            nc.gpsimd.affine_select(out=tri[:, :], in_=ones[:, :], compare_op=ALU.is_gt, fill=0.0, base=0,
                                    pattern=[[1, P]], channel_multiplier=-1).then_inc(s_const, 1)
            nc.gpsimd.iota(ic[:, 0:64], pattern=[[1, 64]], base=0, channel_multiplier=0)
            nc.gpsimd.iota(ic[:, 64:80], pattern=[[-1, 16]], base=16, channel_multiplier=0)
            nc.gpsimd.iota(ic[:, 80:84], pattern=[[-1, 4]], base=4, channel_multiplier=0)
            nc.gpsimd.iota(ic[:, 84:88], pattern=[[P, 4]], base=0, channel_multiplier=1)
            nc.gpsimd.iota(ic[:, 88:95], pattern=[[BLK, 7]], base=BLK, channel_multiplier=0).then_inc(s_ic, 1)

            pool.wait_ge(s_small, 16 * 9)
            for i in range(14):
                if i < NX:
                    continue
                nh = NKV if i < NKT else 4
                j = (i - NX) % NT
                pool.wait_ge(xn_done, i + 1)
                if i > NX:
                    pool.wait_ge(rot_done, i)
                nc.gpsimd.tensor_tensor(t1[:, 0:nh * HD].rearrange("p (h d) -> p h d", h=nh),
                                        xn[:, 0:nh * HD].rearrange("p (h d) -> p h d", h=nh),
                                        ropeC[:, j:j + 1, :].broadcast_to([P, nh, HD]), ALU.mult).then_inc(t1_done, 1)

            def ln_affine(k):
                pool.wait_ge(s_lnw, 32 * (k + 1) if k < 2 else 32 * (k + 2))
                for j in range(NT):
                    pool.wait_ge(ln_nrm, NT * k + j + 1)
                    nc.gpsimd.tensor_tensor(H[:, j, :], H[:, j, :], LG[:, :], ALU.mult).then_inc(pgl, 1)
                    pool.wait_ge(pgl, NT * k + j + 1)
                    nc.gpsimd.tensor_tensor(H[:, j, :], H[:, j, :], LB[:, :], ALU.add).then_inc(ln_rd, 1)

            def moe(l):
                pool.wait_ge(s_hw[l], 16 * NT)
                pool.wait_ge(tab_rd, l + 1)

                def gather():
                    nc.gpsimd.indirect_dma_start(
                        out=xg, out_offset=None, in_=hscr[l],
                        in_offset=bass.IndirectOffsetOnAxis(ap=gidx[0:BLK, 0:1], axis=0)).then_inc(xg_in[l], 16)

                pool.wait_ge(ix_rd[l], 1)
                gather()
                pool.wait_ge(ix_rd[l], 2)
                pool.wait_ge(xt_pe[l], 1)
                gather()
                total = pool.value_load(table[l][0:1, NE:NE + 1], min_val=1, max_val=MAXB)
                with pool.Fori(0, total) as g:
                    pool.wait_ge(ix_rd[l], g + 3)
                    pool.nop(nofuse=True)
                    pool.wait_ge(xt_pe[l], g + 2)
                    pool.nop(nofuse=True)
                    gather()
                total = pool.value_load(table[l][0:1, NE:NE + 1], min_val=1, max_val=MAXB)
                pool.wait_ge(y_st[l], total * 32 + 32)
                pool.nop(nofuse=True)
                unused = pool.value_load(table[l][0:1, NE + 1:NE + 2], min_val=1, max_val=ROWB)
                pool.wait_ge(y_fill[l], unused * 16)
                pool.nop(nofuse=True)
                pool.wait_ge(xg_in[l], total * 16 + 32)
                pool.nop(nofuse=True)
                for j in range(NT):
                    if l * NT + j >= 2:
                        pool.wait_ge(fg_used, l * NT + j - 1)
                    for k in range(2):
                        nc.gpsimd.indirect_dma_start(
                            out=yg[:, j % 2, k, :], out_offset=None, in_=yscr[l],
                            in_offset=bass.IndirectOffsetOnAxis(ap=yidx[:, k, j:j + 1], axis=0),
                        ).then_inc(fg[l][j % 2], 16)
                ln_affine(2 * l + 1)

            ln_affine(0)
            moe(0)
            pool.wait_ge(s_lnw, 32 * 3)
            for j in range(NT):
                pool.wait_ge(vn, j + 1)
                nc.gpsimd.tensor_tensor(zv[:, j, :], zv[:, j, :], LG[:, :], ALU.mult).then_inc(vg1, 1)
                pool.wait_ge(vg1, j + 1)
                nc.gpsimd.tensor_tensor(zv[:, j, :], zv[:, j, :], LB[:, :], ALU.add).then_inc(v_rd, 1)
            ln_affine(2)
            moe(1)

        @block.scalar
        def _(act):
            A = nc.scalar.activation
            act.dma_start(craw[:, 0, :], c[0].rearrange("(p k) -> p k", k=DC)).then_inc(s_c, 16)
            act.dma_start(craw[:, 1, :], c_ctx.rearrange("(p k) -> p k", k=DC)).then_inc(s_c, 16)
            act.dma_start(brow[:, :], b_ada.rearrange("l (m p) -> (l m) p", p=P)).then_inc(s_small, 16)
            act.dma_start(bsrow[:, :], b_bs[0]).then_inc(s_small, 16)
            act.dma_start(qg[:, :], a_qg[0:1, :].broadcast_to([P, HD])).then_inc(s_small, 16)
            act.dma_start(kg[:, :], a_kg[0:1, :].broadcast_to([P, HD])).then_inc(s_small, 16)
            act.dma_start(wr[:, :, :], w_router.rearrange("(k p) n -> p k n", p=P)).then_inc(s_small, 16)
            act.dma_start(rb[:, :], router_bias.rearrange("(o n) -> o n", o=1).broadcast_to([P, NE])).then_inc(s_small, 16)
            act.dma_start(ropeC, rope_cos.rearrange("(t p) d -> p t d", p=P)).then_inc(s_small, 16)
            act.dma_start(ropeS, rope_sin.rearrange("(t p) d -> p t d", p=P)).then_inc(s_small, 16)
            act.dma_start(ctxn, ctx_tok[0].rearrange("(t p) d -> p t d", p=P)).then_inc(s_ctx, 16)
            act.dma_start(H[:, :, :], x[0].rearrange("(t p) d -> p t d", p=P)).then_inc(s_x, 16)
            act.dma_start(junk[:, 0:P], b_vg[0:1, 0:P].broadcast_to([P, P])).then_inc(s_small, 16)
            act.wait_ge(s_c, 32)
            A(silu_c[:, :, :], craw[:, :, :].rearrange("p v k -> p k v"), ACT.Silu).then_inc(s_silu, 1)
            act.wait_ge(s_small, 16 * 9)

            def load_row(dst, src):
                act.dma_start(dst[:, :], src.broadcast_to([P, D])).then_inc(s_lnw, 16)

            def tr_evac(first, dst, src_n, l, sc, sh):
                for q in range(0, DC, 2):
                    i = first + q
                    act.wait_ge(tr_pe, i + 1)
                    src = PS[:, i % 4, 0:src_n]
                    if sc is None:
                        A(dst[:, q, :], src, ACT.Copy).then_inc(tr_act, 1)
                    else:
                        A(dst[:, q, :], src, ACT.Identity, bias=sh[:, q:q + 1], scale=sc[:, q:q + 1]).then_inc(tr_act, 1)

            def m(t, o):
                return t[:, o:o + DC]

            act.wait_ge(ada_ev, 4)
            tr_evac(TR_X, uT, TOK, 0, m(mod[0], SC1), m(mod[0], SH1))
            tr_evac(TR_C, ucT, NX * P, 0, m(modc, SC1), m(modc, SH1))

            def qk_evac(i):
                act.wait_ge(qkT_pe, i + 1)
                if i < NKT:
                    A(kT[:, :, i * P:(i + 1) * P], PS[:, i % 2, 0:NKV * P].rearrange("p (h q) -> p h q", h=NKV),
                      ACT.Copy).then_inc(qk_ev, 1)
                else:
                    h0, j = 4 * ((i - NKT) // NT), (i - NKT) % NT
                    A(qT[:, h0:h0 + 4, j * P:(j + 1) * P], PS[:, i % 2, :].rearrange("p (h q) -> p h q", h=4),
                      ACT.Copy).then_inc(qk_ev, 1)

            for i in range(14):
                bank = PS[:, 4 + i % 3, :]
                nh = NKV if i < NKT else 4
                act.wait_ge(qkv_pe, i + 1)
                if i < NKT:
                    A(V[:, i, :], bank[:, NKV * HD:2 * NKV * HD], ACT.Copy)
                if i:
                    act.wait_ge(ms_done, i)
                for h in range(nh):
                    ins = A(junk[:, h * HD:(h + 1) * HD], bank[:, h * HD:(h + 1) * HD], ACT.Square, accum_out=ss[:, h:h + 1])
                ins.then_inc(sq_done, 1)
                act.wait_ge(ms_done, i + 1)
                A(rt[:, 0:nh], ms[:, 0:nh], ACT.Sqrt).then_inc(sqrt_done, 1)
                if i:
                    qk_evac(i - 1)
            qk_evac(13)
            load_row(LG, ln_g[0, 0:1, :])
            load_row(LB, ln_b[0, 0:1, :])

            LAG = 2
            NU = NH * NT
            for u in range(NU + LAG):
                if u < NU:
                    act.wait_ge(nm, u + 1)
                    if u >= 3:
                        act.wait_ge(t_pe, u - 2)
                    if u >= 4:
                        act.wait_ge(p_norm, u - 3)
                    A(Pb[:, u % 3, :], PS[:, 2 * (u % 2):2 * (u % 2) + 2, :].rearrange("p b n -> p (b n)")[:, 0:NKT * P],
                      ACT.Exp, bias=nmx[:, u % 4:u % 4 + 1], scale=SCALE, accum_out=den[:, u % 4:u % 4 + 1]
                      ).then_inc(exp_done, 1)
                v = u - LAG
                if v >= 0:
                    if v % NT == 0 and v:
                        h = v // NT - 1
                        act.wait_ge(pv_pe, h + 1)
                        A(uT[:, h, :], PS[:, 6, :], ACT.Copy).then_inc(o_ev, 1)
                    act.wait_ge(t_pe, v + 1)
                    qb = v % NT
                    A(PT[:, 0:3, qb * P:(qb + 1) * P], PS[:, 4, 0:3 * P].rearrange("p (k q) -> p k q", k=3),
                      ACT.Copy).then_inc(pt_act, 1)
            act.wait_ge(pv_pe, NH)
            A(uT[:, NH - 1, :], PS[:, 6, :], ACT.Copy).then_inc(o_ev, 1)

            def gate_rows(n):
                act.wait_ge(gb_pe, n + 1)
                A(G[:, :], PS[:, 6:8, :].rearrange("p b n -> p (b n)"), ACT.Copy).then_inc(gb_ev, 1)

            def ln_sqrt(n):
                act.wait_ge(var_rd, n + 1)
                A(rt[:, 0:1], ms[:, 0:1], ACT.Sqrt).then_inc(std_rd, 1)

            def moe(l):
                for j in range(NT):
                    act.wait_ge(ln_rd, 2 * NT * l + j + 1)
                    act.dma_start(hscr[l][j * P:(j + 1) * P, :], H[:, j, :]).then_inc(s_hw[l], 16)
                for half in range(2):
                    act.dma_start(yscr[l][(ROWB - 1) * BLK:, half * 512:half * 512 + 512], H[0:BLK, 0, 0:512]).then_inc(y_st[l], 16)
                if l == 0:
                    load_row(LG, ln_g[l, 1:2, :])
                    load_row(LB, ln_b[l, 1:2, :])
                else:
                    load_row(LG, ln_g[l, 1:2, :])
                    load_row(LB, ln_b[l, 1:2, :])
                tr_evac(TR_R0 if l == 0 else TR_R1, uT, TOK, l, m(mod[l], SC2), m(mod[l], SH2))
                gate_rows(2 * l + 1)
                act.wait_ge(lg_pe, l + 1)
                A(sc_[:, :, :].rearrange("p t e -> p (t e)"), PS[:, 4, 0:NT * NE], ACT.Sigmoid).then_inc(sig_rd, 1)
                act.wait_ge(tab_rd, l + 1)
                total = act.value_load(table[l][0:1, NE:NE + 1], min_val=1, max_val=MAXB)
                with act.Fori(0, total) as g:
                    for h in range(2):
                        act.wait_ge(gu[l][h], g + 1)
                        A(gs[:, 256 * h:256 * h + 256], PS[0:BLK, h, 0:256], ACT.Silu).then_inc(silu_rd[l][h], 1)
                    for h in range(2):
                        act.wait_ge(ht_pe[l][h], g + 1)
                        A(hidT[:, 2 * h:2 * h + 2, :], PS[:, 3 + h, 0:2 * BLK].rearrange("p (k s) -> p k s", k=2),
                          ACT.Copy).then_inc(ht_rd[l][h], 1)
                    act.wait_ge(y_st[l], g * 32 + 32)
                    act.wait_ge(dn_pe[l], g + 1)
                    A(ysb, PS[:, 5, :], ACT.Copy).then_inc(y_ev[l], 1)
                    act.wait_ge(y_ev[l], g + 1)
                    act.dma_start(yscr[l][bass.ds(g * BLK, BLK), 0:512], ysb[0:BLK, :]).then_inc(y_st[l], 16)
                    act.dma_start(yscr[l][bass.ds(g * BLK, BLK), 512:1024], ysb[BLK:P, :]).then_inc(y_st[l], 16)
                for j in range(NT):
                    ln_sqrt(ln_no[2 * l + 1] + j)

            ln_no = [0, NT, 3 * NT, 4 * NT]
            v_no = 2 * NT
            gate_rows(0)
            for j in range(NT):
                ln_sqrt(ln_no[0] + j)
            moe(0)
            act.wait_ge(ln_rd, 2 * NT)
            load_row(LG, b_vg[0:1, :])
            load_row(LB, b_vb[0:1, :])
            act.dma_start(ws, b_ws[0].rearrange("g t s -> t g s")).then_inc(s_ws, 16)
            tr_evac(TR_M1, uT, TOK, 1, m(mod[1], SC1), m(mod[1], SH1))
            act.wait_ge(xg_in[0], 16)
            for i in range(16):
                half, n, j = i // 8, (i // 4) % 2, i % 4
                act.wait_ge(z_pe, i + 1)
                dst = (zv, zu)[half]
                A(dst[:, j, 512 * n:512 * n + 512], PS[:, 4 + i % 4, :], ACT.Gelu_apprx_tanh).then_inc(z_ev, 1)
            for j in range(NT):
                ln_sqrt(v_no + j)
            act.wait_ge(v_rd, NT)
            load_row(LG, ln_g[1, 0:1, :])
            load_row(LB, ln_b[1, 0:1, :])
            tr_evac(TR_P1, uT, TOK, 1, None, None)
            gate_rows(2)
            for j in range(NT):
                ln_sqrt(ln_no[2] + j)
            moe(1)
            for j in range(NT):
                act.wait_ge(ln_rd, 3 * NT + j + 1)
                act.dma_start(out[0, j * P:(j + 1) * P, :], H[:, j, :]).then_inc(s_out, 16)
            act.wait_ge(s_out, 16 * NT)

        @block.vector
        def _(dve):
            V_ = nc.vector
            nchain = [0]

            def link(ins):
                nchain[0] += 1
                ins.then_inc(chain, 1)
                dve.wait_ge(chain, nchain[0])

            def rsqrt(n, wait_sem, wait_val):
                dve.wait_ge(wait_sem, wait_val)
                link(V_.reciprocal(rs[:, 0:n], rt[:, 0:n]))
                link(V_.tensor_tensor(nt[:, 0:n], rs[:, 0:n], rs[:, 0:n], ALU.mult))
                link(V_.tensor_tensor(nt[:, 0:n], nt[:, 0:n], ms[:, 0:n], ALU.mult))
                link(V_.tensor_scalar(nt[:, 0:n], nt[:, 0:n], -0.5, 1.5, ALU.mult, ALU.add))
                link(V_.tensor_tensor(rs[:, 0:n], rs[:, 0:n], nt[:, 0:n], ALU.mult))

            dve.wait_ge(s_ic, 1)
            link(V_.tensor_copy(fc[:, :], ic[:, :]))
            dve.wait_ge(s_bT_pe, 1)
            link(V_.tensor_copy(badaT[:, :, :].rearrange("p l m -> p (l m)"), PS[:, 6, 0:96]))
            link(V_.tensor_copy(bsT[:, :], PS[:, 6, 96:104]))
            for l in range(DEPTH):
                for o in (SC1, SC2):
                    link(V_.tensor_scalar(badaT[:, l, o:o + DC], badaT[:, l, o:o + DC], 1.0, None, ALU.add))

            def ada_evac(q):
                dve.wait_ge(ada_pe, q + 1)
                if q < 4:
                    ps = PS[:, 7, 8 * q:8 * q + 8].rearrange("p (m v) -> p m v", v=2)
                    link(V_.tensor_tensor(mod[0][:, 4 * q:4 * q + 4], ps[:, :, 0], badaT[:, 0, 4 * q:4 * q + 4], ALU.add))
                    V_.tensor_tensor(modc[:, 4 * q:4 * q + 4], ps[:, :, 1], badaT[:, 0, 4 * q:4 * q + 4],
                                     ALU.add).then_inc(ada_ev, 1)
                else:
                    l, qq = divmod(q, 12)
                    V_.tensor_tensor(mod[l][:, 4 * qq:4 * qq + 4], PS[:, 7, 32 + 4 * (q - 4):36 + 4 * (q - 4)],
                                     badaT[:, l, 4 * qq:4 * qq + 4], ALU.add).then_inc(ada_ev, 1)

            for q in range(4):
                ada_evac(q)
            dve.wait_ge(ada_ev, 4)

            def tr_evac(first, dst, src_n, sc, sh):
                for q in range(1, DC, 2):
                    i = first + q
                    dve.wait_ge(tr_pe, i + 1)
                    src = PS[:, i % 4, 0:src_n]
                    if sc is None:
                        V_.tensor_copy(dst[:, q, :], src).then_inc(tr_dve, 1)
                    else:
                        V_.tensor_scalar(dst[:, q, :], src, sc[:, q:q + 1], sh[:, q:q + 1], ALU.mult,
                                         ALU.add).then_inc(tr_dve, 1)

            def m(t, o):
                return t[:, o:o + DC]

            tr_evac(TR_X, uT, TOK, m(mod[0], SC1), m(mod[0], SH1))
            tr_evac(TR_C, ucT, NX * P, m(modc, SC1), m(modc, SH1))

            dve.wait_ge(s_small, 16 * 9)
            for i in range(14):
                bank = PS[:, 4 + i % 3, :]
                nh = NKV if i < NKT else 4
                gain = kg if i < NKT else qg
                dve.wait_ge(sq_done, i + 1)
                V_.tensor_scalar(ms[:, 0:nh], ss[:, 0:nh], 1.0 / HD, EPS, ALU.mult, ALU.add).then_inc(ms_done, 1)
                rsqrt(nh, sqrt_done, i + 1)
                to = rot if i < NX else xn
                if i and i < NX:
                    dve.wait_ge(qkT_pe, i)
                for h in range(nh):
                    ins = V_.scalar_tensor_tensor(out=to[:, h * HD:(h + 1) * HD], in0=bank[:, h * HD:(h + 1) * HD],
                                                  scalar=rs[:, h:h + 1], in1=gain[:, :], op0=ALU.mult, op1=ALU.mult)
                if i < NX:
                    link(ins)
                    V_.tensor_copy(nt[:, 0:1], rs[:, 0:1]).then_inc(xn_done, 1)
                    V_.tensor_copy(nt[:, 1:2], rs[:, 0:1]).then_inc(rot_done, 1)
                    continue
                ins.then_inc(xn_done, 1)
                dve.wait_ge(xn_done, i + 1)
                j = (i - NX) % NT
                xv = xn[:, 0:nh * HD].rearrange("p (h d) -> p h d", h=nh)
                tv = t2[:, 0:nh * HD].rearrange("p (h d) -> p h d", h=nh)
                for par in range(2):
                    ins = V_.tensor_tensor(tv[:, :, par::2], xv[:, :, 1 - par::2],
                                           ropeS[:, j:j + 1, par::2].broadcast_to([P, nh, HD // 2]), ALU.mult)
                link(ins)
                dve.wait_ge(t1_done, i - NX + 1)
                dve.wait_ge(qkT_pe, i)
                V_.tensor_tensor(rot[:, 0:nh * HD], t1[:, 0:nh * HD], t2[:, 0:nh * HD], ALU.add).then_inc(rot_done, 1)

            LAG = 2
            NU = NH * NT
            for u in range(NU + LAG):
                if u < NU:
                    dve.wait_ge(s_pe, u + 1)
                    if u == 0:
                        dve.wait_ge(qkT_pe, 14)
                    link(V_.tensor_reduce(mx[:, u % 4:u % 4 + 1],
                                          PS[:, 2 * (u % 2):2 * (u % 2) + 2, :].rearrange("p b n -> p (b n)")[:, 0:NKT * P],
                                          AX.X, ALU.max))
                    if u >= 4:
                        dve.wait_ge(exp_done, u - 3)
                    V_.tensor_scalar(nmx[:, u % 4:u % 4 + 1], mx[:, u % 4:u % 4 + 1], -SCALE, None,
                                     ALU.mult).then_inc(nm, 1)
                v = u - LAG
                if v >= 0:
                    dve.wait_ge(t_pe, v + 1)
                    qb = v % NT
                    V_.tensor_copy(PT[:, 3:6, qb * P:(qb + 1) * P],
                                   PS[:, 5, 0:3 * P].rearrange("p (k q) -> p k q", k=3)).then_inc(pt_dve, 1)
                if u < NU:
                    dve.wait_ge(exp_done, u + 1)
                    link(V_.reciprocal(rden[:, u % 4:u % 4 + 1], den[:, u % 4:u % 4 + 1]))
                    V_.tensor_scalar(Pb[:, u % 3, :], Pb[:, u % 3, :], rden[:, u % 4:u % 4 + 1], None,
                                     ALU.mult).then_inc(p_norm, 1)
                if 1 <= u <= 20:
                    ada_evac(u + 3)
            dve.wait_ge(ada_ev, 24)

            def gate_cols(col, n):
                V_.tensor_copy(gcb, col.unsqueeze(2).broadcast_to([P, DC, P])).then_inc(gc_rd, 1)

            def norm_stats(r, no):
                V_.bn_stats(st6[:, 0, :], r[:, 0:512])
                link(V_.bn_stats(st6[:, 1, :], r[:, 512:1024]))
                link(V_.bn_aggr(mv[:, :], st6[:, :, :].rearrange("p a b -> p (a b)")))
                V_.tensor_scalar(ms[:, 0:1], mv[:, 1:2], EPS, None, ALU.add).then_inc(var_rd, 1)
                rsqrt(1, std_rd, no + 1)

            def residual_norm(j, r, no):
                link(V_.scalar_tensor_tensor(out=r, in0=H[:, j, :], scalar=ALPHA, in1=r, op0=ALU.mult, op1=ALU.add))
                norm_stats(r, no)
                V_.tensor_scalar(H[:, j, :], r, mv[:, 0:1], rs[:, 0:1], ALU.subtract, ALU.mult).then_inc(ln_nrm, 1)

            def mixer_out(l, no):
                for j in range(NT):
                    r = lt[:, j % 2, :]
                    dve.wait_ge(y_pe[l], NT + j + 1)
                    for n in range(2):
                        ins = V_.tensor_tensor(r[:, 512 * n:512 * n + 512], PS[:, 4 * n + j, :],
                                               G[:, 512 * n:512 * n + 512], ALU.mult)
                    link(ins)
                    residual_norm(j, r, no + j)

            def first_max(one, v, tmp, dec, mx1, n):
                link(V_.tensor_reduce(mx1, v, AX.X, ALU.max))
                link(V_.tensor_tensor(tmp, v, mx1.unsqueeze(2).broadcast_to([P, NT, n]), ALU.is_equal))
                link(V_.tensor_tensor(tmp, tmp, dec.unsqueeze(1).broadcast_to([P, NT, n]), ALU.mult))
                link(V_.tensor_reduce(mx1, tmp, AX.X, ALU.max))
                link(V_.tensor_tensor(one, tmp, mx1.unsqueeze(2).broadcast_to([P, NT, n]), ALU.is_equal))

            def moe(l):
                dve.wait_ge(ln_nrm, NT * (2 * l + 1))
                gate_cols(m(mod[l], G2), 2 * l + 1)
                tr_evac(TR_R0 if l == 0 else TR_R1, uT, TOK, m(mod[l], SC2), m(mod[l], SH2))
                dve.wait_ge(sig_rd, l + 1)
                link(V_.tensor_tensor(sel[:, :, :], sc_[:, :, :], rb[:, :].unsqueeze(1).broadcast_to([P, NT, NE]), ALU.add))
                sv = sel[:, :, :].rearrange("p t (g e) -> p (t g) e", g=NG)
                V_.tensor_tensor(s6[:, :, 0:2], sv[:, :, 0:4:2], sv[:, :, 1:4:2], ALU.add)
                V_.tensor_tensor(s6[:, :, 2:4], sv[:, :, 0:2], sv[:, :, 2:4], ALU.add)
                V_.tensor_tensor(s6[:, :, 4:5], sv[:, :, 0:1], sv[:, :, 3:4], ALU.add)
                link(V_.tensor_tensor(s6[:, :, 5:6], sv[:, :, 1:2], sv[:, :, 2:3], ALU.add))
                link(V_.tensor_reduce(g4[:, :, :].rearrange("p t g -> p (t g)"), s6[:, :, :], AX.X, ALU.max))
                first_max(gmask[:, :, :], g4[:, :, :], cand[:, :, 0:NG], dec4, gm1[:, :], NG)
                gv = gmask[:, :, :].rearrange("p t g -> p (t g)").unsqueeze(2).broadcast_to([P, NT * NG, PER])
                link(V_.tensor_tensor(sv, sv, gv, ALU.mult))
                link(V_.tensor_scalar(g4[:, :, :], gmask[:, :, :], BIG, -BIG, ALU.mult, ALU.add))
                pv = g4[:, :, :].rearrange("p t g -> p (t g)").unsqueeze(2).broadcast_to([P, NT * NG, PER])
                link(V_.tensor_tensor(sv, sv, pv, ALU.add))
                first_max(o1[:, :, :], sel[:, :, :], cand[:, :, :], dec16, gm1[:, :], NE)
                link(V_.scalar_tensor_tensor(out=sel[:, :, :], in0=o1[:, :, :], scalar=-3e38, in1=sel[:, :, :],
                                             op0=ALU.mult, op1=ALU.add))
                first_max(o2[:, :, :], sel[:, :, :], cand[:, :, :], dec16, gm1[:, :], NE)
                V_.memset(MP[:, 0, :], 0.0)
                link(V_.tensor_tensor(cand[:, :, :], o1[:, :, :], o2[:, :, :], ALU.add))
                link(V_.tensor_copy(MP[:, 1, :], cand[:, 0, :]))
                for j in range(1, NT):
                    ins = V_.tensor_tensor(MP[:, j + 1, :], MP[:, j, :], cand[:, j, :], ALU.add)
                    if j < NT - 1:
                        link(ins)
                ins.then_inc(m_rd, 1)
                for k, o in enumerate((o1, o2)):
                    link(V_.tensor_tensor(smap[:, :, :], sc_[:, :, :], o[:, :, :], ALU.mult))
                    link(V_.tensor_reduce(wts[:, k, :], smap[:, :, :], AX.X, ALU.add))
                link(V_.tensor_tensor(wsum[:, :], wts[:, 0, :], wts[:, 1, :], ALU.add))
                link(V_.reciprocal(wsum[:, :], wsum[:, :]))
                link(V_.tensor_tensor(wts[:, :, :], wts[:, :, :], wsum[:, :].unsqueeze(1).broadcast_to([P, 2, NT]), ALU.mult))
                dve.wait_ge(rk_pe, l + 1)
                link(V_.tensor_tensor(gt7[:, :, :], PS[:, 5, 64:80].unsqueeze(2).broadcast_to([P, NE, 7]),
                                      thr.unsqueeze(1).broadcast_to([P, NE, 7]), ALU.is_gt))
                link(V_.tensor_reduce(nbk[:, :], gt7[:, :, :], AX.X, ALU.add))
                link(V_.tensor_scalar(nbk[:, :], nbk[:, :], 1.0, None, ALU.add))
                V_.memset(bs[:, 0:1], 0.0)
                link(V_.tensor_tensor_scan(bs[:, 1:NE + 1], ones[:, 0:NE], nbk[:, :], 0.0, ALU.mult, ALU.add))
                link(V_.tensor_scalar(bs[:, NE + 1:NE + 2], bs[:, NE:NE + 1], -1.0, float(ROWB - 1), ALU.mult, ALU.add))
                link(V_.tensor_scalar(bs64[:, :], bs[:, 0:NE + 1], float(BLK), None, ALU.mult))
                V_.tensor_copy(table[l][:, :], bs[0:1, :]).then_inc(tab_rd, 1)
                link(V_.tensor_tensor(smap[:, :, :], PS[:, 5, 0:64].rearrange("p (t e) -> p t e", t=NT),
                                      bs64[:, 0:NE].unsqueeze(1).broadcast_to([P, NT, NE]), ALU.add))
                for k, o in enumerate((o1, o2)):
                    link(V_.tensor_tensor(cand[:, :, :], smap[:, :, :], o[:, :, :], ALU.mult))
                    link(V_.tensor_reduce(slot[:, k, :], cand[:, :, :], AX.X, ALU.add))
                V_.tensor_copy(yidx[:, :, :], slot[:, :, :])
                link(V_.tensor_copy(srel[:, :, :], slot[:, :, :]))

                STEPS = 7
                loop = dlp[l]

                def onehot(lnk):
                    it = iota64.unsqueeze(1).broadcast_to([P, NT, BLK])
                    V_.tensor_tensor(oh, srel[:, 0, :].unsqueeze(2).broadcast_to([P, NT, BLK]), it, ALU.is_equal)
                    lnk(V_.tensor_tensor(oh2t, srel[:, 1, :].unsqueeze(2).broadcast_to([P, NT, BLK]), it, ALU.is_equal))
                    V_.tensor_tensor(oh, oh, oh2t, ALU.add).then_inc(oh_rd[l], 1)
                    lnk(V_.tensor_scalar(srel[:, :, :], srel[:, :, :], -float(BLK), None, ALU.add))

                def index():
                    V_.tensor_copy(gidx[0:BLK, :], PS[0:BLK, 6, 0:1]).then_inc(ix_rd[l], 1)

                def x_evac(lnk):
                    lnk(V_.tensor_tensor(xTt, PS[:, 2, :].rearrange("p (c s) -> p c s", c=DC),
                                         m(mod[l], SC2).unsqueeze(2).broadcast_to([P, DC, BLK]), ALU.mult))
                    V_.tensor_tensor(xT, xTt, m(mod[l], SH2).unsqueeze(2).broadcast_to([P, DC, BLK]),
                                     ALU.add).then_inc(xT_rd[l], 1)

                onehot(link)
                dve.wait_ge(ix_pe[l], 1)
                index()
                onehot(link)
                dve.wait_ge(xg_in[l], 16)
                dve.wait_ge(ix_pe[l], 2)
                index()
                onehot(link)
                dve.wait_ge(xt_pe[l], 1)
                x_evac(link)
                total = dve.value_load(table[l][0:1, NE:NE + 1], min_val=1, max_val=MAXB)
                with dve.Fori(0, total) as g:
                    k = [0]

                    def lnk(ins):
                        k[0] += 1
                        ins.then_inc(loop, 1)
                        dve.wait_ge(loop, g * 3 + k[0])

                    for h in range(2):
                        dve.wait_ge(silu_rd[l][h], g + 1)
                        V_.tensor_tensor(hid[:, 256 * h:256 * h + 256], gs[:, 256 * h:256 * h + 256],
                                         PS[BLK:P, h, 0:256], ALU.mult).then_inc(hid_rd[l][h], 1)
                    dve.wait_ge(xt_pe[l], g + 2)
                    x_evac(lnk)
                    dve.wait_ge(ix_pe[l], g + 3)
                    index()
                    onehot(lnk)
                    assert k[0] == 3

                for j in range(NT):
                    r = lt[:, j % 2, :]
                    dve.wait_ge(fg[l][j % 2], 32 * (j // 2 + 1))
                    link(V_.tensor_scalar(r, yg[:, j % 2, 0, :], wts[:, 0, j:j + 1], None, ALU.mult))
                    ins = V_.scalar_tensor_tensor(out=r, in0=yg[:, j % 2, 1, :], scalar=wts[:, 1, j:j + 1], in1=r,
                                                  op0=ALU.mult, op1=ALU.add)
                    ins.then_inc(fg_used, 1)
                    dve.wait_ge(fg_used, l * NT + j + 1)
                    if j == 0:
                        dve.wait_ge(gb_ev, 2 * l + 2)
                    link(V_.tensor_tensor(r, r, G[:, :], ALU.mult))
                    residual_norm(j, r, ln_no[2 * l + 1] + j)

            ln_no = [0, NT, 3 * NT, 4 * NT]
            v_no = 2 * NT
            dve.wait_ge(pv_pe, NH)
            gate_cols(m(mod[0], G1), 0)
            dve.wait_ge(gb_ev, 1)
            mixer_out(0, ln_no[0])
            moe(0)
            tr_evac(TR_M1, uT, TOK, m(mod[1], SC1), m(mod[1], SH1))
            dve.wait_ge(wsT_pe, 1)
            V_.tensor_copy(wsT, PS[:, 0:2, :].rearrange("p b (g t) -> p (b g) t", g=4)).then_inc(wsT_ev, 1)
            for j in range(NT):
                dve.wait_ge(z_ev, 4 + j + 1)
                norm_stats(zv[:, j, :], v_no + j)
                V_.tensor_scalar(zv[:, j, :], zv[:, j, :], mv[:, 0:1], rs[:, 0:1], ALU.subtract, ALU.mult).then_inc(vn, 1)
            dve.wait_ge(z_ev, 16)
            for g in range(8):
                dve.wait_ge(mix_pe, g + 1)
                o = zu[:, :, g * P:(g + 1) * P]
                V_.scalar_tensor_tensor(out=o, in0=PS[:, g % 4, :].rearrange("p (t d) -> p t d", t=NT),
                                        scalar=bsT[:, g:g + 1], in1=o, op0=ALU.add, op1=ALU.mult).then_inc(mix_ev, 1)
            gate_cols(m(mod[1], G1), 2)
            tr_evac(TR_P1, uT, TOK, None, None)
            dve.wait_ge(gb_ev, 3)
            mixer_out(1, ln_no[2])
            moe(1)

        @block.tensor
        def _(pe):
            mm = nc.tensor.matmul

            def weights(n):
                pe.wait_ge(w_in[n % RING], 16 * (n // RING + 1))

            def ada(q, n):
                weights(n)
                if q:
                    pe.wait_ge(ada_ev, q)
                w = slot_of(n).rearrange("p (k n) -> p k n", k=DC)
                for t in range(4):
                    o = PS[:, 7, 8 * q + 2 * t:8 * q + 2 * t + 2] if q < 4 else \
                        PS[:, 7, 32 + 4 * (q - 4) + t:33 + 4 * (q - 4) + t]
                    for k in range(DC):
                        ins = mm(o, w[:, k, t * P:(t + 1) * P], silu_c[:, k, 0:2 if q < 4 else 1],
                                 start=(k == 0), stop=(k == DC - 1))
                ins.then_inc(ada_pe, 1)

            pe.wait_ge(s_const, 2)
            pe.wait_ge(s_small, 16 * 9)
            nc.tensor.transpose(PS[:, 6, 0:96], brow[:, :], ident[0:96, 0:96])
            nc.tensor.transpose(PS[:, 6, 96:104], bsrow[:, :], ident[0:8, 0:8]).then_inc(s_bT_pe, 1)
            pe.wait_ge(s_silu, 1)

            n = 0
            for q in range(4):
                ada(q, n)
                n += 1

            def tr_items(first, srcs):
                for q in range(DC):
                    i = first + q
                    if i >= 4:
                        tr_wait(pe, i - 4)
                    for j, s in enumerate(srcs):
                        ins = nc.tensor.transpose(PS[:, i % 4, j * P:(j + 1) * P], s[:, q * P:(q + 1) * P], ident[:, :])
                    ins.then_inc(tr_pe, 1)

            pe.wait_ge(s_x, 16)
            tr_items(TR_X, [H[:, j, :] for j in range(NT)])
            pe.wait_ge(s_ctx, 16)
            tr_items(TR_C, [ctxn[:, j, :] for j in range(NX)])
            tr_wait(pe, TR_C + DC - 2)
            tr_wait(pe, TR_C + DC - 1)

            def qk_turn(i):
                nh = NKV if i < NKT else 4
                pe.wait_ge(rot_done, i + 1)
                if i >= 2:
                    pe.wait_ge(qk_ev, i - 1)
                for h in range(nh):
                    ins = nc.tensor.transpose(PS[:, i % 2, h * P:(h + 1) * P], rot[:, h * HD:(h + 1) * HD], ident[:, :])
                ins.then_inc(qkT_pe, 1)

            for i in range(14):
                ctx_item = i < NX
                if i in (0, NKT, NKT + NT):
                    weights(n)
                    w = slot_of(n).rearrange("p (k n) -> p k n", k=DC)
                if i >= 3:
                    pe.wait_ge(xn_done, i - 2)
                j = i if ctx_item else (i - NX) % NT
                a = ucT if ctx_item else uT
                for k in range(DC):
                    ins = mm(PS[:, 4 + i % 3, :], a[:, k, j * P:(j + 1) * P], w[:, k, :], start=(k == 0), stop=(k == DC - 1))
                ins.then_inc(qkv_pe, 1)
                if i in (NKT - 1, NKT + NT - 1, NKT + 2 * NT - 1):
                    n += 1
                if i:
                    qk_turn(i - 1)
            qk_turn(13)
            pe.wait_ge(qk_ev, 14)

            LAG = 2
            NU = NH * NT

            def pv(h):
                pe.wait_ge(pt_act, NT * (h + 1))
                pe.wait_ge(pt_dve, NT * (h + 1))
                if h:
                    pe.wait_ge(o_ev, h)
                kv = h // (NH // NKV)
                for k in range(NKT):
                    ins = mm(PS[:, 6, :], V[:, k, kv * HD:(kv + 1) * HD], PT[:, k, :], start=(k == 0), stop=(k == NKT - 1))
                ins.then_inc(pv_pe, 1)

            for u in range(NU + LAG):
                if u < NU:
                    h, qb = u // NT, u % NT
                    kv = h // (NH // NKV)
                    if u >= 2:
                        pe.wait_ge(exp_done, u - 1)
                    b = 2 * (u % 2)
                    q = qT[:, h, qb * P:(qb + 1) * P]
                    mm(PS[:, b, :], q, kT[:, kv, 0:512], start=True, stop=True)
                    mm(PS[:, b + 1, 0:NKT * P - 512], q, kT[:, kv, 512:NKT * P], start=True, stop=True).then_inc(s_pe, 1)
                v = u - LAG
                if v >= 0:
                    if v % NT == 0 and v:
                        pv(v // NT - 1)
                    pe.wait_ge(p_norm, v + 1)
                    if v:
                        pe.wait_ge(pt_act, v)
                        pe.wait_ge(pt_dve, v)
                    for k in range(NKT):
                        ins = nc.tensor.transpose(PS[:, 4 + k // 3, (k % 3) * P:(k % 3 + 1) * P],
                                                  Pb[:, v % 3, k * P:(k + 1) * P], ident[:, :])
                    ins.then_inc(t_pe, 1)
                if 1 <= u <= 20:
                    ada(u + 3, n)
                    n += 1
            pv(NH - 1)
            pe.wait_ge(o_ev, NH)

            def gate_rows(k):
                pe.wait_ge(gc_rd, k + 1)
                for f in range(DC):
                    ins = mm(PS[:, 6 + f // 4, (f % 4) * P:(f % 4 + 1) * P], gcb[:, f, :], ident[:, :], start=True, stop=True)
                ins.then_inc(gb_pe, 1)
                pe.wait_ge(gb_ev, k + 1)

            def project(l, n):
                for half in range(2):
                    weights(n)
                    w = slot_of(n).rearrange("p (k n) -> p k n", k=DC)
                    for j in range(NT):
                        for k in range(DC):
                            ins = mm(PS[:, 4 * half + j, :], uT[:, k, j * P:(j + 1) * P], w[:, k, :],
                                     start=(k == 0), stop=(k == DC - 1))
                        ins.then_inc(y_pe[l], 1)
                    n += 1
                return n

            def moe(l):
                pe.wait_ge(ln_rd, NT * (2 * l + 1))
                tr_items(TR_R0 if l == 0 else TR_R1, [H[:, j, :] for j in range(NT)])
                gate_rows(2 * l + 1)
                last = (TR_R0 if l == 0 else TR_R1) + DC - 1
                tr_wait(pe, last - 1)
                tr_wait(pe, last)
                for j in range(NT):
                    for k in range(DC):
                        ins = mm(PS[:, 4, j * NE:(j + 1) * NE], uT[:, k, j * P:(j + 1) * P], wr[:, k, :],
                                 start=(k == 0), stop=(k == DC - 1))
                ins.then_inc(lg_pe, 1)
                pe.wait_ge(m_rd, l + 1)
                mflat = cand[:, :, :].rearrange("p t e -> p (t e)")
                mm(PS[:, 5, 0:64], tri[:, :], mflat, start=True, stop=False)
                mm(PS[:, 5, 0:64], ones[:, :], MP[:, 0:NT, :].rearrange("p t e -> p (t e)"), start=False, stop=True)
                mm(PS[:, 5, 64:80], ones[:, :], MP[:, NT, :], start=True, stop=True).then_inc(rk_pe, 1)

                def index():
                    for j in range(NT):
                        ins = mm(PS[0:BLK, 6, 0:1], oh[:, j, :], tokid[:, j:j + 1], start=(j == 0), stop=(j == NT - 1))
                    ins.then_inc(ix_pe[l], 1)

                def turn_x():
                    for f in range(DC):
                        ins = nc.tensor.transpose(PS[:, 2, f * BLK:(f + 1) * BLK], xg[:, f * P:(f + 1) * P],
                                                  ident[0:BLK, 0:BLK])
                    ins.then_inc(xt_pe[l], 1)

                pe.wait_ge(oh_rd[l], 1)
                index()
                pe.wait_ge(oh_rd[l], 2)
                pe.wait_ge(ix_rd[l], 1)
                index()
                pe.wait_ge(xg_in[l], 16)
                turn_x()
                base = base_moe[l]
                pe.wait_ge(tab_rd, l + 1)
                with pe.Fori(0, NE // 2) as pair:
                    for par in range(2):
                        lo = pe.value_load(table[l][0:1, bass.ds(pair * 2 + par, 1)], min_val=0, max_val=MAXB)
                        hi = pe.value_load(table[l][0:1, bass.ds(pair * 2 + (par + 1), 1)], min_val=1, max_val=MAXB)
                        nn = base + 3 * par

                        def landed(j):
                            pe.wait_ge(w_in[(nn + j) % RING], pair * 16 + 16 * ((nn + j) // RING + 1))

                        wg = slot_of(nn).rearrange("p (k n) -> p k n", k=DC)
                        wu = slot_of(nn + 1).rearrange("p (k n) -> p k n", k=DC)
                        wd = slot_of(nn + 2).rearrange("p (k n) -> p k n", k=FC)
                        with pe.Fori(lo, hi) as g:
                            pe.wait_ge(xT_rd[l], g + 1)
                            landed(0)
                            landed(1)
                            for h in range(2):
                                for k in range(DC):
                                    mm(PS[0:BLK, h, 0:256], xT[:, k, :], wg[:, k, 256 * h:256 * h + 256],
                                       start=(k == 0), stop=(k == DC - 1))
                                    ins = mm(PS[BLK:P, h, 0:256], xT[:, k, :], wu[:, k, 256 * h:256 * h + 256],
                                             start=(k == 0), stop=(k == DC - 1))
                                ins.then_inc(gu[l][h], 1)

                            def turn_hidden(h):
                                pe.wait_ge(hid_rd[l][h], g + 1)
                                pe.nop(nofuse=True)
                                for f in range(2):
                                    ins = nc.tensor.transpose(PS[:, 3 + h, f * BLK:(f + 1) * BLK],
                                                              hid[:, (2 * h + f) * P:(2 * h + f + 1) * P],
                                                              ident[0:BLK, 0:BLK])
                                ins.then_inc(ht_pe[l][h], 1)

                            turn_hidden(0)
                            pe.wait_ge(xg_in[l], g * 16 + 32)
                            pe.nop(nofuse=True)
                            turn_x()
                            landed(2)

                            def down(h):
                                pe.wait_ge(ht_rd[l][h], g + 1)
                                for k in (2 * h, 2 * h + 1):
                                    for half in range(2):
                                        ins = mm(PS[BLK * half:BLK * half + BLK, 5, :], hidT[:, k, :],
                                                 wd[:, k, 512 * half:512 * half + 512],
                                                 start=(k == 0), stop=(k == FC - 1))
                                return ins

                            down(0)
                            turn_hidden(1)
                            pe.wait_ge(oh_rd[l], g + 3)
                            pe.wait_ge(ix_rd[l], g + 2)
                            index()
                            down(1).then_inc(dn_pe[l], 1)

            gate_rows(0)
            n = project(0, n)
            moe(0)
            pe.wait_ge(ln_rd, 2 * NT)
            tr_items(TR_M1, [H[:, j, :] for j in range(NT)])
            tr_wait(pe, TR_M1 + DC - 2)
            tr_wait(pe, TR_M1 + DC - 1)
            pe.wait_ge(s_ws, 16)
            for g in range(8):
                ins = nc.tensor.transpose(PS[:, g // 4, (g % 4) * P:(g % 4 + 1) * P], ws[:, g, :], ident[:, :])
            ins.then_inc(wsT_pe, 1)
            n = base_s1
            for i in range(16):
                if i % 4 == 0:
                    weights(n)
                    w = slot_of(n).rearrange("p (k n) -> p k n", k=DC)
                if i >= 4:
                    pe.wait_ge(z_ev, i - 3)
                j = i % 4
                for k in range(DC):
                    ins = mm(PS[:, 4 + i % 4, :], uT[:, k, j * P:(j + 1) * P], w[:, k, :], start=(k == 0), stop=(k == DC - 1))
                ins.then_inc(z_pe, 1)
                if i % 4 == 3:
                    n += 1
            pe.wait_ge(wsT_ev, 1)
            pe.wait_ge(v_rd, NT)
            for g in range(8):
                if g >= 4:
                    pe.wait_ge(mix_ev, g - 3)
                mm(PS[:, g % 4, :], wsT[:, g, :], zv[:, :, g * P:(g + 1) * P], start=True, stop=True).then_inc(mix_pe, 1)
            pe.wait_ge(mix_ev, 8)
            tr_items(TR_P1, [zu[:, j, :] for j in range(NT)])
            gate_rows(2)
            tr_wait(pe, TR_P1 + DC - 2)
            tr_wait(pe, TR_P1 + DC - 1)
            n = project(1, n)
            moe(1)


_INS = ['x', 'c', 'ctx', 'c_ctx', 'w_ada', 'b_ada', 'ln_g', 'ln_b', 'a_wqkv', 'a_qg', 'a_kg', 'a_wo', 'b_win', 'b_vg',
        'b_vb', 'b_ws', 'b_bs', 'b_wout', 'w_router', 'router_bias', 'e_gate', 'e_up', 'e_down']
_OUT = ((1, 512, 1024), 'float32')
GRID_W, HEAD_DIM, ROPE_THETA = 64, 128, 10000.0


def rope_tables(n):
    import numpy as np
    half = HEAD_DIM // 2
    inv = (np.float32(1.0) / (np.float32(ROPE_THETA) ** (np.arange(0, half, 2, dtype=np.float32) / np.float32(half))))
    t = np.arange(n)
    ang = np.concatenate([(t // GRID_W).astype(np.float32)[:, None] * inv,
                          (t % GRID_W).astype(np.float32)[:, None] * inv], -1)
    cos, sin = np.cos(ang), np.sin(ang)
    return (np.repeat(cos, 2, axis=1).astype(np.float32),
            np.stack([-sin, sin], -1).reshape(n, HEAD_DIM).astype(np.float32))


def kernel(**inputs):
    import numpy as _np
    import concourse.bacc as _bacc
    from concourse import mybir as _mybir
    from concourse.bass_utils import run_bass_kernel_spmd as _run

    nc = _bacc.Bacc("TRN2", target_bir_lowering=False, num_devices=1)
    arrays, args = {}, []
    for name in _INS:
        a = _np.ascontiguousarray(inputs[name])
        arrays[f"in_{name}_dram"] = a
        args.append(nc.dram_tensor(f"in_{name}_dram", a.shape, _mybir.dt.from_np(a.dtype), kind="ExternalInput").ap())
    for name, a in zip(("rope_cos", "rope_sin"), rope_tables(512)):
        arrays[f"{name}_dram"] = a
        args.append(nc.dram_tensor(f"{name}_dram", a.shape, _mybir.dt.from_np(a.dtype), kind="ExternalInput").ap())
    shape, dtype = _OUT
    args.append(nc.dram_tensor("out_0_dram", shape, _mybir.dt.from_np(_np.dtype(dtype)), kind="ExternalOutput").ap())
    backbone(nc, *args)
    r = _run(nc, [arrays], core_ids=[0])
    return r.results[0]["out_0_dram"]
```

```python
from contextlib import ExitStack

import concourse.bass as bass
from concourse import mybir

ALU = mybir.AluOpType
ACT = mybir.ActivationFunctionType
AX = mybir.AxisListType
F32 = mybir.dt.float32
I32 = mybir.dt.int32

P = 128
EPS = 1e-6
RING = 6
BLK = 64
BIG = 1e30


def backbone(nc, x, c, ctx_tok, c_ctx, w_ada, b_ada, ln_g, ln_b, a_wqkv, a_qg, a_kg, a_wo, b_win, b_vg, b_vb, b_ws,
             b_bs, b_wout, w_router, router_bias, e_gate, e_up, e_down, rope_cos, rope_sin, out):
    D = x.shape[2]
    NT = x.shape[1] // P
    NX = ctx_tok.shape[1] // P
    DC = D // P
    DEPTH = w_ada.shape[0]
    ALPHA = float((2 * DEPTH) ** 0.25)
    HD = a_qg.shape[1]
    NH = a_wo.shape[1] // HD
    NKV = (a_wqkv.shape[2] // HD - NH) // 2
    NKT = NX + NT
    SCALE = float(HD) ** -0.5
    NE = w_router.shape[1]
    NG = 4
    PER = NE // NG
    FE = e_gate.shape[3]
    FC = FE // P
    TOK = NT * P
    MAXB = NE + (2 * TOK - NE) // BLK
    ROWB = MAXB + 2
    SH1, SC1, G1, SH2, SC2, G2 = range(0, 6 * DC, DC)
    assert D == 1024 and NT == 4 and NX == 2 and HD == P and NH == 8 and NKV == 2 and FE == 512 and DEPTH == 2

    hscr = [nc.dram_tensor(f"tokens_{l}", [TOK, D], F32).ap() for l in range(DEPTH)]
    yscr = [nc.dram_tensor(f"expert_rows_{l}", [ROWB * BLK, D], F32).ap() for l in range(DEPTH)]

    with ExitStack() as st:
        def sb(name, shape, dt=F32):
            return st.enter_context(nc.sbuf_tensor(name, shape, dt))

        def sem(name):
            return st.enter_context(nc.semaphore(name))

        ring = sb("ring", [P, RING, 4096])
        H = sb("H", [P, NT, D])
        uT = sb("uT", [P, DC, TOK])
        RD = sb("RD", [P, 4096])
        RE = sb("RE", [P, 4096])
        RF = sb("RF", [P, 3072])
        RW = sb("RW", [P, 3072])
        LG = sb("LG", [P, D])
        LB = sb("LB", [P, D])
        G = sb("G", [P, D])
        ident = sb("ident", [P, P])
        ones = sb("ones", [P, P])
        tri = sb("tri", [P, P])
        ctxn = RD[:, 0:2048].rearrange("p (t d) -> p t d", t=NX)
        ucT = RD[:, 2048:4096].rearrange("p (c t) -> p c t", c=DC)
        PT = RD[:, 0:NKT * TOK].rearrange("p (k q) -> p k q", k=NKT)
        zu = RD[:, :].rearrange("p (t d) -> p t d", t=NT)
        yg = RD[:, :].rearrange("p (b k d) -> p b k d", b=2, k=2)
        qT = RE[:, :].rearrange("p (h q) -> p h q", h=NH)
        zv = RE[:, :].rearrange("p (t d) -> p t d", t=NT)
        kT = RF[:, 0:1536].rearrange("p (h k) -> p h k", h=NKV)
        V = RF[:, 1536:3072].rearrange("p (k d) -> p k d", k=NKT)
        ws = RF[:, 0:1024].rearrange("p (g s) -> p g s", g=8)
        wsT = RF[:, 1024:2048].rearrange("p (g s) -> p g s", g=8)
        xn, t1, t2, rot, junk = (RW[:, 512 * i:512 * i + 512] for i in range(5))
        Pb = RW[:, 0:2304].rearrange("p (b k) -> p b k", b=3)
        arow = RW[:, 0:2048].rearrange("p (q n) -> p q n", q=4)
        arow1 = RW[:, 2304:2816]
        lrow = RW[:, 1024:1536]
        gcb = RW[:, 0:1024].rearrange("p (c m) -> p c m", c=DC)
        lt = RW[:, 1024:3072].rearrange("p (b d) -> p b d", b=2)
        ropeC = LG[:, 0:512].rearrange("p (t d) -> p t d", t=NT)
        ropeS = LG[:, 512:1024].rearrange("p (t d) -> p t d", t=NT)
        xg = RE[0:BLK, 0:1024]
        xT = RE[:, 1024:1536].rearrange("p (c s) -> p c s", c=DC)
        xTt = RE[:, 1536:2048].rearrange("p (c s) -> p c s", c=DC)
        gs = RE[0:BLK, 2048:2560]
        hid = RE[0:BLK, 2560:3072]
        hidT = RE[:, 3072:3328].rearrange("p (k s) -> p k s", k=FC)
        ysb = RE[:, 3328:3840]
        oh = RW[:, 2048:2304].rearrange("p (t s) -> p t s", t=NT)
        oh2t = RW[:, 2304:2560].rearrange("p (t s) -> p t s", t=NT)

        silu_c = sb("silu_c", [P, DC, 32])
        craw = sb("craw", [P, 2, DC])
        rows1 = RE[:, 0:P]
        rows2 = RE[0:40, P:2 * P]
        cols = sb("cols", [P, 168])
        badaT = cols[:, 0:96].rearrange("p (l m) -> p l m", l=2)
        lngT = cols[:, 96:128].rearrange("p (k c) -> p k c", k=4)
        lnbT = cols[:, 128:160].rearrange("p (k c) -> p k c", k=4)
        bsT = cols[:, 160:168]
        fsc = sb("fsc", [P, 3, DC])
        fsh = sb("fsh", [P, 3, DC])
        mod = [sb(f"mod{l}", [P, 48]) for l in range(DEPTH)]
        modc = sb("modc", [P, 16])
        qg = sb("qg", [P, HD])
        kg = sb("kg", [P, HD])
        wr = sb("wr", [P, DC, 32])
        atmp = sb("atmp", [P, 4, 2])
        rb = sb("rb", [P, NE])
        ss = sb("ss", [P, 4])
        ms = sb("ms", [P, 4])
        rt = sb("rt", [P, 4])
        rs = sb("rs", [P, 4])
        nt = sb("nt", [P, 4])
        mx = sb("mx", [P, 4])
        nmx = sb("nmx", [P, 4])
        den = sb("den", [P, 4])
        rden = sb("rden", [P, 4])
        st6 = sb("st6", [P, NT, 12])
        mv = sb("mv", [P, NT, 2])
        nb = sb("nb", [P, NT])
        sc_ = sb("sc_", [P, NT, NE])
        sel = sb("sel", [P, NT, NE])
        s6 = sb("s6", [P, 16, 6])
        g4 = sb("g4", [P, NT, NG])
        gm1 = sb("gm1", [P, NT])
        gmask = sb("gmask", [P, NT, NG])
        cand = sb("cand", [P, NT, NE])
        o1 = sb("o1", [P, NT, NE])
        o2 = sb("o2", [P, NT, NE])
        MP = sb("MP", [P, NT + 1, NE])
        wts = sb("wts", [P, 2, NT])
        wsum = sb("wsum", [P, NT])
        gt7 = sb("gt7", [P, NE, 7])
        nbk = sb("nbk", [P, NE])
        bs = sb("bs", [P, NE + 2])
        bs64 = sb("bs64", [P, NE + 1])
        smap = sb("smap", [P, NT, NE])
        slot = sb("slot", [P, 2, NT])
        srel = sb("srel", [P, 2, NT])
        yidx = sb("yidx", [P, 2, NT], I32)
        table = [sb(f"table{l}", [1, NE + 2], I32) for l in range(DEPTH)]
        gidx = sb("gidx", [P, 1], I32)
        ic = sb("ic", [P, 64 + 16 + 4 + 4 + 7], I32)
        fc = sb("fc", [P, 64 + 16 + 4 + 4 + 7])
        iota64, dec16, dec4, tokid, thr = fc[:, 0:64], fc[:, 64:80], fc[:, 80:84], fc[:, 84:88], fc[:, 88:95]

        PS = st.enter_context(nc.psum_tensor("PS", [P, 8, 512], F32))

        static0 = ([("ada", 0, q) for q in range(4)] + [("qkv", 0, n) for n in (2, 0, 1)]
                   + [("ada", 0, q) for q in range(4, 12)] + [("ada", 1, q) for q in range(12)]
                   + [("wo", 0, 0), ("wo", 0, 1)])
        static1 = [("win", 0, n) for n in (2, 3, 0, 1)] + [("wout", 0, 0), ("wout", 0, 1)]
        S0, S1 = len(static0), len(static1)
        base_moe = [S0, S0 + 3 * NE + S1]
        base_s1 = S0 + 3 * NE

        def slot_of(n):
            return ring[:, n % RING, :]

        w_in = [sem(f"weights_in_{b}") for b in range(RING)]
        s_c = sem("cond_loaded")
        s_x = sem("x_loaded")
        s_ctx = sem("ctx_loaded")
        s_small = sem("small_loaded")
        s_rope = sem("rope_loaded")
        s_lnw = sem("ln_weights_loaded")
        s_ws = sem("spatial_weights_loaded")
        s_const = sem("constants_ready")
        s_ic = sem("iota_ready")
        s_silu = sem("silu_c_ready")
        s_bT_pe = sem("bias_rows_turned")
        s_bT = sem("bias_cols_ready")
        ada_pe, ar_ev, at_pe, ada_ev = (sem("ada_rows_in_psum"), sem("ada_rows_ready"), sem("ada_cols_in_psum"),
                                        sem("ada_ready"))
        s_zero, s_fold, lr_pe, lr_ev, lg_rd = (sem("pads_zeroed"), sem("folded_ready"), sem("logit_rows_in_psum"),
                                               sem("logit_rows_ready"), sem("logits_ready"))
        ab_rd, lnw_sc = sem("norm_scale_ready"), sem("ln_rows_scaled")
        nrm_act = sem("ln_normed_by_act")
        tr_pe, tr_act, tr_dve = sem("turned_in_psum"), sem("turned_by_act"), sem("turned_by_dve")
        qkv_pe, sq_done, ms_done, sqrt_done = sem("qkv_in_psum"), sem("squares_done"), sem("meansq_ready"), sem("sqrt_ready")
        xn_done, t1_done, rot_done = sem("normed"), sem("rope_cos_part"), sem("rotated")
        qkT_pe, qk_ev = sem("qk_turned_in_psum"), sem("qkT_ready")
        s_pe, nm, exp_done, p_norm = sem("scores_in_psum"), sem("negmax_ready"), sem("exp_done"), sem("probs_ready")
        t_pe, pt_act, pt_dve = sem("probs_turned_in_psum"), sem("probsT_by_act"), sem("probsT_by_dve")
        pv_pe, o_ev = sem("attn_out_in_psum"), sem("attn_out_ready")
        gc_rd, gb_pe, gb_ev = sem("gate_cols_spread"), sem("gate_rows_in_psum"), sem("gate_rows_ready")
        y_pe = [sem(f"mixer_out_in_psum_{l}") for l in range(DEPTH)]
        var_rd, std_rd, ln_nrm, ln_rd = sem("ln_var_ready"), sem("ln_std_ready"), sem("ln_normed"), sem("ln_tile_ready")
        pgl = sem("ln_gain_applied")
        z_pe, z_ev = sem("mlp_in_psum"), sem("gelu_done")
        vn, vg1, v_rd = sem("v_normed"), sem("v_gain_applied"), sem("v_ready")
        wsT_pe, wsT_ev = sem("spatial_turned_in_psum"), sem("spatialT_ready")
        mix_pe, mix_ev = sem("mixed_in_psum"), sem("gated_ready")
        s_hw = [sem(f"tokens_stored_{l}") for l in range(DEPTH)]
        lg_pe, sig_rd, m_rd, rk_pe, tab_rd = (sem("logits_in_psum"), sem("scores_ready"), sem("choice_ready"),
                                              sem("ranks_in_psum"), sem("table_ready"))
        L = range(DEPTH)
        oh_rd = [sem(f"onehot_ready_{l}") for l in L]
        ix_pe = [sem(f"index_in_psum_{l}") for l in L]
        ix_rd = [sem(f"index_ready_{l}") for l in L]
        xg_in = [sem(f"gathered_{l}") for l in L]
        xt_pe = [sem(f"gathered_turned_{l}") for l in L]
        xT_rd = [sem(f"block_xT_ready_{l}") for l in L]
        gu = [[sem(f"gate_up_{h}_in_psum_{l}") for h in range(2)] for l in L]
        silu_rd = [[sem(f"silu_{h}_ready_{l}") for h in range(2)] for l in L]
        hid_rd = [[sem(f"hidden_{h}_ready_{l}") for h in range(2)] for l in L]
        ht_pe = [[sem(f"hidden_{h}_turned_{l}") for h in range(2)] for l in L]
        ht_rd = [[sem(f"hiddenT_{h}_ready_{l}") for h in range(2)] for l in L]
        dn_pe = [sem(f"block_out_in_psum_{l}") for l in L]
        y_ev = [sem(f"block_out_ready_{l}") for l in L]
        y_st = [sem(f"block_out_stored_{l}") for l in L]
        y_fill = [sem(f"unused_rows_filled_{l}") for l in L]
        dlp = [sem(f"dve_loop_chain_{l}") for l in L]
        fg = [[sem(f"expert_rows_in_{l}_{b}") for b in range(2)] for l in L]
        fg_used = sem("expert_rows_used")
        s_out = sem("out_stored")
        chain = sem("dve_chain")
        pchain = sem("pool_chain")
        achain = sem("act_chain")

        block = st.enter_context(nc.Block())

        def tr_wait(eng, i):
            eng.wait_ge(tr_dve if i % 2 else tr_act, i // 2 + 1)

        TR_X, TR_C, TR_R0, TR_M1, TR_P1, TR_R1 = 0, 8, 16, 24, 32, 40

        @block.sync
        def _(sp):
            wqkv = a_wqkv[0].rearrange("(k p) n -> p k n", p=P)
            wo = a_wo[0].rearrange("(k p) n -> p k n", p=P)
            win = b_win[0].rearrange("(k p) n -> p k n", p=P)
            wout = b_wout[0].rearrange("(k p) n -> p k n", p=P)
            ada = [w_ada[l].rearrange("(p k) n -> p k n", k=DC) for l in range(DEPTH)]
            view = {"qkv": wqkv, "wo": wo, "win": win, "wout": wout}

            def load_static(n, kind, l, q):
                src = (ada[l] if kind == "ada" else view[kind])[:, :, 512 * q:512 * q + 512]
                sp.dma_start(slot_of(n).rearrange("p (k n) -> p k n", k=DC), src).then_inc(w_in[n % RING], 16)

            def load_expert(n, l, e, j):
                dst = slot_of(n)
                if j < 2:
                    src = (e_gate, e_up)[j][l, e].rearrange("(k p) n -> p k n", p=P)
                    dst = dst.rearrange("p (k n) -> p k n", k=DC)
                else:
                    src = e_down[l, e].rearrange("(k p) n -> p k n", p=P)
                    dst = dst.rearrange("p (k n) -> p k n", k=FC)
                sp.dma_start(dst, src).then_inc(w_in[n % RING], 16)

            def wait_used(ch):
                kind, l, q = ch
                if kind == "ada":
                    sp.wait_ge(ada_pe, 12 * l + q + 1)
                elif kind == "qkv":
                    sp.wait_ge(qkv_pe, {2: NKT, 0: NKT + NT, 1: NKT + 2 * NT}[q])
                elif kind == "win":
                    sp.wait_ge(z_pe, NT * ((q + 2) % 4 + 1))
                else:
                    sp.wait_ge(y_pe[0 if kind == "wo" else 1], NT * (q + 1))

            for l in range(DEPTH):
                if l == 0:
                    sp.dma_start(craw[:, 0, :], c[0].rearrange("(p k) -> p k", k=DC)).then_inc(s_c, 16)
                    sp.dma_start(craw[:, 1, :], c_ctx.rearrange("(p k) -> p k", k=DC)).then_inc(s_c, 16)
                    for n, ch in enumerate(static0):
                        if n == 3:
                            sp.dma_start(H[:, :, :], x[0].rearrange("(t p) d -> p t d", p=P)).then_inc(s_x, 16)
                        if n == 4:
                            sp.dma_start(ctxn, ctx_tok[0].rearrange("(t p) d -> p t d", p=P)).then_inc(s_ctx, 16)
                        if n == 5:
                            sp.dma_start(ropeC, rope_cos.rearrange("(t p) d -> p t d", p=P)).then_inc(s_rope, 16)
                            sp.dma_start(ropeS, rope_sin.rearrange("(t p) d -> p t d", p=P)).then_inc(s_rope, 16)
                        if n >= RING:
                            wait_used(static0[n - RING])
                        load_static(n, *ch)
                else:
                    for i, ch in enumerate(static1):
                        e_last, j = NE - 2 + i // 3, i % 3
                        last = sp.value_load(table[l - 1][0:1, e_last + 1:e_last + 2], min_val=1, max_val=MAXB)
                        sp.wait_ge(dn_pe[l - 1] if j == 2 else gu[l - 1][1], last)
                        load_static(base_s1 + i, *ch)
                for i in range(RING):
                    wait_used((static0, static1)[l][i - RING])
                    load_expert(base_moe[l] + i, l, i // 3, i % 3)
                sp.wait_ge(tab_rd, l + 1)
                sp.wait_ge(ln_rd, NT * (2 * l + 1))
                total = sp.value_load(table[l][0:1, NE:NE + 1], min_val=1, max_val=MAXB)
                with sp.Fori(total, ROWB - 1) as b:
                    sp.dma_start(yscr[l][bass.ds(b * BLK, BLK), :], H[0:BLK, 0, :]).then_inc(y_fill[l], 16)
                with sp.Fori(1, NE // 2) as pair:
                    for par in range(2):
                        e = pair * 2 + par
                        last = sp.value_load(table[l][0:1, bass.ds(pair * 2 + (par - 1), 1)], min_val=1, max_val=MAXB)
                        for j in range(3):
                            sp.wait_ge(dn_pe[l] if j == 2 else gu[l][1], last)
                            load_expert(base_moe[l] + 3 * par + j, l, e, j)

        @block.gpsimd
        def _(pool):
            nchain = [0]

            def link(ins):
                nchain[0] += 1
                ins.then_inc(pchain, 1)
                pool.wait_ge(pchain, nchain[0])

            nc.gpsimd.memset(silu_c[:, :, :], 0.0).then_inc(s_zero, 1)
            nc.gpsimd.memset(wr[:, :, :], 0.0).then_inc(s_zero, 1)
            nc.gpsimd.memset(ident[:, :], 0.0).then_inc(pchain, 1)
            nc.gpsimd.memset(ones[:, :], 1.0).then_inc(pchain, 1)
            nchain[0] = 2
            pool.wait_ge(pchain, 2)
            nc.gpsimd.affine_select(out=ident[:, :], in_=ident[:, :], compare_op=ALU.not_equal, fill=1.0, base=0,
                                    pattern=[[-1, P]], channel_multiplier=1).then_inc(s_const, 1)
            nc.gpsimd.affine_select(out=tri[:, :], in_=ones[:, :], compare_op=ALU.is_gt, fill=0.0, base=0,
                                    pattern=[[1, P]], channel_multiplier=-1).then_inc(s_const, 1)
            nc.gpsimd.iota(ic[:, 0:64], pattern=[[1, 64]], base=0, channel_multiplier=0)
            nc.gpsimd.iota(ic[:, 64:80], pattern=[[-1, 16]], base=16, channel_multiplier=0)
            nc.gpsimd.iota(ic[:, 80:84], pattern=[[-1, 4]], base=4, channel_multiplier=0)
            nc.gpsimd.iota(ic[:, 84:88], pattern=[[P, 4]], base=0, channel_multiplier=1)
            nc.gpsimd.iota(ic[:, 88:95], pattern=[[BLK, 7]], base=BLK, channel_multiplier=0).then_inc(s_ic, 1)

            pool.wait_ge(s_rope, 32)
            for i in range(14):
                if i < NX:
                    continue
                nh = NKV if i < NKT else 4
                j = (i - NX) % NT
                pool.wait_ge(xn_done, i + 1)
                if i > NX:
                    pool.wait_ge(rot_done, i)
                nc.gpsimd.tensor_tensor(t1[:, 0:nh * HD].rearrange("p (h d) -> p h d", h=nh),
                                        xn[:, 0:nh * HD].rearrange("p (h d) -> p h d", h=nh),
                                        ropeC[:, j:j + 1, :].broadcast_to([P, nh, HD]), ALU.mult).then_inc(t1_done, 1)

            def ln_affine(k):
                for j in range(NT):
                    nc.gpsimd.tensor_tensor(H[:, j, :], H[:, j, :], LG[:, :], ALU.mult).then_inc(pgl, 1)
                for j in range(NT):
                    pool.wait_ge(pgl, NT * k + j + 1)
                    nc.gpsimd.tensor_tensor(H[:, j, :], H[:, j, :], LB[:, :], ALU.add).then_inc(ln_rd, 1)

            def moe(l):
                pool.wait_ge(s_hw[l], 16 * NT)
                pool.wait_ge(tr_pe, (TR_R0 if l == 0 else TR_R1) + DC)
                pool.wait_ge(lnw_sc, 2 if l == 0 else 6)
                ln_affine(2 * l)
                pool.wait_ge(tab_rd, l + 1)

                def gather():
                    nc.gpsimd.indirect_dma_start(
                        out=xg, out_offset=None, in_=hscr[l],
                        in_offset=bass.IndirectOffsetOnAxis(ap=gidx[0:BLK, 0:1], axis=0)).then_inc(xg_in[l], 16)

                pool.wait_ge(ix_rd[l], 1)
                gather()
                pool.wait_ge(ix_rd[l], 2)
                pool.wait_ge(xt_pe[l], 1)
                gather()
                total = pool.value_load(table[l][0:1, NE:NE + 1], min_val=1, max_val=MAXB)
                with pool.Fori(0, total) as g:
                    pool.wait_ge(ix_rd[l], g + 3)
                    pool.nop(nofuse=True)
                    pool.wait_ge(xt_pe[l], g + 2)
                    pool.nop(nofuse=True)
                    gather()
                total = pool.value_load(table[l][0:1, NE:NE + 1], min_val=1, max_val=MAXB)
                pool.wait_ge(y_st[l], total * 32 + 32)
                pool.nop(nofuse=True)
                unused = pool.value_load(table[l][0:1, NE + 1:NE + 2], min_val=1, max_val=ROWB)
                pool.wait_ge(y_fill[l], unused * 16)
                pool.nop(nofuse=True)
                pool.wait_ge(xg_in[l], total * 16 + 32)
                pool.nop(nofuse=True)
                for j in range(NT):
                    if l * NT + j >= 2:
                        pool.wait_ge(fg_used, l * NT + j - 1)
                    for k in range(2):
                        nc.gpsimd.indirect_dma_start(
                            out=yg[:, j % 2, k, :], out_offset=None, in_=yscr[l],
                            in_offset=bass.IndirectOffsetOnAxis(ap=yidx[:, k, j:j + 1], axis=0),
                        ).then_inc(fg[l][j % 2], 16)

            moe(0)
            pool.wait_ge(tr_pe, TR_M1 + DC)
            pool.wait_ge(lnw_sc, 4)
            ln_affine(1)
            pool.wait_ge(s_lnw, 32 * 3)
            for j in range(NT):
                pool.wait_ge(vn, j + 1)
                nc.gpsimd.tensor_tensor(zv[:, j, :], zv[:, j, :], LG[:, :], ALU.mult).then_inc(vg1, 1)
                pool.wait_ge(vg1, j + 1)
                nc.gpsimd.tensor_tensor(zv[:, j, :], zv[:, j, :], LB[:, :], ALU.add).then_inc(v_rd, 1)
            moe(1)
            pool.wait_ge(s_lnw, 32 * 5)
            for j in range(NT):
                pool.wait_ge(pgl, 3 * NT + j + 1)
                nc.gpsimd.tensor_tensor(H[:, j, :], H[:, j, :], LB[:, :], ALU.add).then_inc(ln_rd, 1)

        @block.scalar
        def _(act):
            A = nc.scalar.activation
            act.dma_start(rows1[0:96, :], b_ada.rearrange("l (m p) -> (l m) p", p=P)).then_inc(s_small, 16)
            act.dma_start(rows1[96:128, :], ln_g.rearrange("l k (c p) -> (l k c) p", p=P)).then_inc(s_small, 16)
            act.dma_start(rows2[0:32, :], ln_b.rearrange("l k (c p) -> (l k c) p", p=P)).then_inc(s_small, 16)
            act.dma_start(rows2[32:40, :], b_bs[0]).then_inc(s_small, 16)
            act.dma_start(qg[:, :], a_qg[0:1, :].broadcast_to([P, HD])).then_inc(s_small, 16)
            act.dma_start(kg[:, :], a_kg[0:1, :].broadcast_to([P, HD])).then_inc(s_small, 16)
            act.dma_start(rb[:, :], router_bias.rearrange("(o n) -> o n", o=1).broadcast_to([P, NE])).then_inc(s_small, 16)
            act.wait_ge(s_zero, 2)
            act.dma_start(wr[:, :, 0:NE], w_router.rearrange("(k p) n -> p k n", p=P)).then_inc(s_small, 16)
            act.wait_ge(s_c, 32)
            A(silu_c[:, :, 0:2], craw[:, :, :].rearrange("p v k -> p k v"), ACT.Silu).then_inc(s_silu, 1)
            for q in range(4):
                act.wait_ge(ada_pe, q + 1)
                A(arow[:, q, :], PS[:, 4 + q, :], ACT.Copy).then_inc(ar_ev, 1)
            act.wait_ge(s_small, 16 * 8)

            nload = [0]

            def load_rows(g, b, scaled):
                nload[0] += 1
                act.dma_start(LG[:, :], g.broadcast_to([P, D])).then_inc(s_lnw, 16)
                act.dma_start(LB[:, :], b.broadcast_to([P, D])).then_inc(s_lnw, 16)
                if scaled:
                    act.wait_ge(s_lnw, 32 * nload[0])
                    A(LG[:, :], LG[:, :], ACT.Copy, scale=ALPHA).then_inc(lnw_sc, 1)
                    A(LB[:, :], LB[:, :], ACT.Copy, scale=ALPHA).then_inc(lnw_sc, 1)

            def tr_evac(first, dst, src_n, l, sc, sh):
                for q in range(0, DC, 2):
                    i = first + q
                    act.wait_ge(tr_pe, i + 1)
                    src = PS[:, i % 4, 0:src_n]
                    if sc is None:
                        A(dst[:, q, :], src, ACT.Copy).then_inc(tr_act, 1)
                    else:
                        A(dst[:, q, :], src, ACT.Identity, bias=sh[:, q:q + 1], scale=sc[:, q:q + 1]).then_inc(tr_act, 1)

            def m(t, o):
                return t[:, o:o + DC]

            act.wait_ge(ada_ev, 4)
            tr_evac(TR_X, uT, TOK, 0, m(mod[0], SC1), m(mod[0], SH1))
            tr_evac(TR_C, ucT, NX * P, 0, m(modc, SC1), m(modc, SH1))

            def qk_evac(i):
                act.wait_ge(qkT_pe, i + 1)
                if i < NKT:
                    A(kT[:, :, i * P:(i + 1) * P], PS[:, i % 2, 0:NKV * P].rearrange("p (h q) -> p h q", h=NKV),
                      ACT.Copy).then_inc(qk_ev, 1)
                else:
                    h0, j = 4 * ((i - NKT) // NT), (i - NKT) % NT
                    A(qT[:, h0:h0 + 4, j * P:(j + 1) * P], PS[:, i % 2, :].rearrange("p (h q) -> p h q", h=4),
                      ACT.Copy).then_inc(qk_ev, 1)

            for i in range(14):
                bank = PS[:, 4 + i % 3, :]
                nh = NKV if i < NKT else 4
                act.wait_ge(qkv_pe, i + 1)
                if i < NKT:
                    A(V[:, i, :], bank[:, NKV * HD:2 * NKV * HD], ACT.Copy)
                if i:
                    act.wait_ge(ms_done, i)
                for h in range(nh):
                    ins = A(junk[:, h * HD:(h + 1) * HD], bank[:, h * HD:(h + 1) * HD], ACT.Square, accum_out=ss[:, h:h + 1])
                ins.then_inc(sq_done, 1)
                act.wait_ge(ms_done, i + 1)
                A(rt[:, 0:nh], ms[:, 0:nh], ACT.Sqrt).then_inc(sqrt_done, 1)
                if i:
                    qk_evac(i - 1)
            qk_evac(13)
            load_rows(ln_g[0, 0:1, :], ln_b[0, 0:1, :], True)

            LAG = 2
            NU = NH * NT
            for u in range(NU + LAG):
                if u < NU:
                    act.wait_ge(nm, u + 1)
                    if u >= 3:
                        act.wait_ge(t_pe, u - 2)
                    if u >= 4:
                        act.wait_ge(p_norm, u - 3)
                    A(Pb[:, u % 3, :], PS[:, 2 * (u % 2):2 * (u % 2) + 2, :].rearrange("p b n -> p (b n)")[:, 0:NKT * P],
                      ACT.Exp, bias=nmx[:, u % 4:u % 4 + 1], scale=SCALE, accum_out=den[:, u % 4:u % 4 + 1]
                      ).then_inc(exp_done, 1)
                v = u - LAG
                if v >= 0:
                    if v % NT == 0 and v:
                        h = v // NT - 1
                        act.wait_ge(pv_pe, h + 1)
                        A(uT[:, h, :], PS[:, 6, :], ACT.Copy).then_inc(o_ev, 1)
                    act.wait_ge(t_pe, v + 1)
                    qb = v % NT
                    A(PT[:, 0:3, qb * P:(qb + 1) * P], PS[:, 4, 0:3 * P].rearrange("p (k q) -> p k q", k=3),
                      ACT.Copy).then_inc(pt_act, 1)
                if 1 <= u <= 20:
                    act.wait_ge(ada_pe, u + 4)
                    if u > 1:
                        act.wait_ge(at_pe, u + 3)
                    A(arow1, PS[:, 7, :], ACT.Copy).then_inc(ar_ev, 1)
            act.wait_ge(pv_pe, NH)
            A(uT[:, NH - 1, :], PS[:, 6, :], ACT.Copy).then_inc(o_ev, 1)

            def gate_rows(n):
                act.wait_ge(gb_pe, n + 1)
                A(G[:, :], PS[:, 6:8, :].rearrange("p b n -> p (b n)"), ACT.Copy).then_inc(gb_ev, 1)

            def norm_part(k, tiles, t):
                act.wait_ge(var_rd, k + 1)
                A(rt[:, 0:NT], ms[:, 0:NT], ACT.Sqrt).then_inc(std_rd, 1)
                act.wait_ge(ab_rd, k + 1)
                for j in tiles:
                    A(t[:, j, :], t[:, j, :], ACT.Identity, bias=nb[:, j:j + 1], scale=rs[:, j:j + 1]).then_inc(nrm_act, 1)

            def moe(l):
                act.wait_ge(nrm_act, 4 * l + 2)
                for j in (0, 2):
                    act.dma_start(hscr[l][j * P:(j + 1) * P, :], H[:, j, :]).then_inc(s_hw[l], 16)
                act.wait_ge(ln_nrm, 4 * l + 2)
                for j in (1, 3):
                    act.dma_start(hscr[l][j * P:(j + 1) * P, :], H[:, j, :]).then_inc(s_hw[l], 16)
                tr_evac(TR_R0 if l == 0 else TR_R1, uT, TOK, l, fsc[:, 2 * l, :], fsh[:, 2 * l, :])
                act.wait_ge(lr_pe, l + 1)
                A(lrow, PS[:, 4, :], ACT.Copy).then_inc(lr_ev, 1)
                act.wait_ge(lg_rd, l + 1)
                A(sc_[:, :, :], sel[:, :, :], ACT.Sigmoid).then_inc(sig_rd, 1)
                act.wait_ge(gb_pe, 2 * l + 2)
                A(G[:, 0:512], PS[:, 7, :], ACT.Copy).then_inc(gb_ev, 1)
                act.wait_ge(ln_rd, NT * (2 * l + 1))
                for half in range(2):
                    act.dma_start(yscr[l][(ROWB - 1) * BLK:, half * 512:half * 512 + 512], H[0:BLK, 0, 0:512]).then_inc(y_st[l], 16)
                load_rows(ln_g[l, 1:2, :], ln_b[l, 1:2, :], l == 0)
                act.wait_ge(tab_rd, l + 1)
                total = act.value_load(table[l][0:1, NE:NE + 1], min_val=1, max_val=MAXB)
                with act.Fori(0, total) as g:
                    for h in range(2):
                        act.wait_ge(gu[l][h], g + 1)
                        A(gs[:, 256 * h:256 * h + 256], PS[0:BLK, h, 0:256], ACT.Silu).then_inc(silu_rd[l][h], 1)
                    for h in range(2):
                        act.wait_ge(ht_pe[l][h], g + 1)
                        A(hidT[:, 2 * h:2 * h + 2, :], PS[:, 3 + h, 0:2 * BLK].rearrange("p (k s) -> p k s", k=2),
                          ACT.Copy).then_inc(ht_rd[l][h], 1)
                    act.wait_ge(y_ev[l], g + 1)
                    act.nop(nofuse=True)
                    act.dma_start(yscr[l][bass.ds(g * BLK, BLK), 0:512], ysb[0:BLK, :]).then_inc(y_st[l], 16)
                    act.dma_start(yscr[l][bass.ds(g * BLK, BLK), 512:1024], ysb[BLK:P, :]).then_inc(y_st[l], 16)
                norm_part((1, 4)[l], (0, 2), H)

            gate_rows(0)
            norm_part(0, (0, 2), H)
            moe(0)
            act.dma_start(ws, b_ws[0].rearrange("g t s -> t g s")).then_inc(s_ws, 16)
            tr_evac(TR_M1, uT, TOK, 1, fsc[:, 1, :], fsh[:, 1, :])
            act.wait_ge(ln_rd, 2 * NT)
            load_rows(b_vg[0:1, :], b_vb[0:1, :], False)
            for i in range(16):
                half, n, j = i // 8, (i // 4) % 2, i % 4
                act.wait_ge(z_pe, i + 1)
                dst = (zv, zu)[half]
                A(dst[:, j, 512 * n:512 * n + 512], PS[:, 4 + i % 4, :], ACT.Gelu_apprx_tanh).then_inc(z_ev, 1)
                if i == 8:
                    norm_part(2, (), zv)
            gate_rows(2)
            act.wait_ge(v_rd, NT)
            load_rows(ln_g[1, 0:1, :], ln_b[1, 0:1, :], True)
            tr_evac(TR_P1, uT, TOK, 1, None, None)
            norm_part(3, (0, 2), H)
            moe(1)
            for j in range(NT):
                act.wait_ge(ln_rd, 3 * NT + j + 1)
                act.dma_start(out[0, j * P:(j + 1) * P, :], H[:, j, :]).then_inc(s_out, 16)
            act.wait_ge(s_out, 16 * NT)

        @block.vector
        def _(dve):
            V_ = nc.vector
            nchain = [0]

            def link(ins):
                nchain[0] += 1
                ins.then_inc(chain, 1)
                dve.wait_ge(chain, nchain[0])

            def rsqrt(n, wait_sem, wait_val):
                dve.wait_ge(wait_sem, wait_val)
                link(V_.reciprocal(rs[:, 0:n], rt[:, 0:n]))
                link(V_.tensor_tensor(nt[:, 0:n], rs[:, 0:n], rs[:, 0:n], ALU.mult))
                link(V_.tensor_tensor(nt[:, 0:n], nt[:, 0:n], ms[:, 0:n], ALU.mult))
                link(V_.tensor_scalar(nt[:, 0:n], nt[:, 0:n], -0.5, 1.5, ALU.mult, ALU.add))
                link(V_.tensor_tensor(rs[:, 0:n], rs[:, 0:n], nt[:, 0:n], ALU.mult))

            dve.wait_ge(s_ic, 1)
            link(V_.tensor_copy(fc[:, :], ic[:, :]))
            dve.wait_ge(s_bT_pe, 1)
            link(V_.tensor_copy(cols[:, :], PS[:, 0, 0:168]))
            for l in range(DEPTH):
                for o in (SC1, SC2):
                    link(V_.tensor_scalar(badaT[:, l, o:o + DC], badaT[:, l, o:o + DC], 1.0, None, ALU.add))

            def ada_evac(q):
                dve.wait_ge(at_pe, q + 1)
                l, qq = divmod(q, 12)
                ps = PS[:, 4 + q if q < 4 else 7, :].rearrange("p (t g v) -> p t v g", t=4, g=4)
                nv = 2 if q < 4 else 1
                link(V_.tensor_reduce(atmp[:, :, 0:nv], ps[:, :, 0:nv, :], AX.X, ALU.add))
                if q < 4:
                    V_.tensor_tensor(modc[:, 4 * q:4 * q + 4], atmp[:, :, 1], badaT[:, 0, 4 * q:4 * q + 4], ALU.add)
                V_.tensor_tensor(mod[l][:, 4 * qq:4 * qq + 4], atmp[:, :, 0],
                                 badaT[:, l, 4 * qq:4 * qq + 4], ALU.add).then_inc(ada_ev, 1)
                dve.wait_ge(ada_ev, q + 1)

            for q in range(4):
                ada_evac(q)

            def tr_evac(first, dst, src_n, sc, sh):
                for q in range(1, DC, 2):
                    i = first + q
                    dve.wait_ge(tr_pe, i + 1)
                    src = PS[:, i % 4, 0:src_n]
                    if sc is None:
                        V_.tensor_copy(dst[:, q, :], src).then_inc(tr_dve, 1)
                    else:
                        V_.tensor_scalar(dst[:, q, :], src, sc[:, q:q + 1], sh[:, q:q + 1], ALU.mult,
                                         ALU.add).then_inc(tr_dve, 1)

            def m(t, o):
                return t[:, o:o + DC]

            tr_evac(TR_X, uT, TOK, m(mod[0], SC1), m(mod[0], SH1))
            tr_evac(TR_C, ucT, NX * P, m(modc, SC1), m(modc, SH1))

            dve.wait_ge(s_small, 16 * 8)
            dve.wait_ge(s_rope, 32)
            for i in range(14):
                bank = PS[:, 4 + i % 3, :]
                nh = NKV if i < NKT else 4
                gain = kg if i < NKT else qg
                dve.wait_ge(sq_done, i + 1)
                V_.tensor_scalar(ms[:, 0:nh], ss[:, 0:nh], 1.0 / HD, EPS, ALU.mult, ALU.add).then_inc(ms_done, 1)
                rsqrt(nh, sqrt_done, i + 1)
                to = rot if i < NX else xn
                if i and i < NX:
                    dve.wait_ge(qkT_pe, i)
                for h in range(nh):
                    ins = V_.scalar_tensor_tensor(out=to[:, h * HD:(h + 1) * HD], in0=bank[:, h * HD:(h + 1) * HD],
                                                  scalar=rs[:, h:h + 1], in1=gain[:, :], op0=ALU.mult, op1=ALU.mult)
                if i < NX:
                    link(ins)
                    V_.tensor_copy(nt[:, 0:1], rs[:, 0:1]).then_inc(xn_done, 1)
                    V_.tensor_copy(nt[:, 1:2], rs[:, 0:1]).then_inc(rot_done, 1)
                    continue
                ins.then_inc(xn_done, 1)
                dve.wait_ge(xn_done, i + 1)
                j = (i - NX) % NT
                xv = xn[:, 0:nh * HD].rearrange("p (h d) -> p h d", h=nh)
                tv = t2[:, 0:nh * HD].rearrange("p (h d) -> p h d", h=nh)
                for par in range(2):
                    ins = V_.tensor_tensor(tv[:, :, par::2], xv[:, :, 1 - par::2],
                                           ropeS[:, j:j + 1, par::2].broadcast_to([P, nh, HD // 2]), ALU.mult)
                link(ins)
                dve.wait_ge(t1_done, i - NX + 1)
                dve.wait_ge(qkT_pe, i)
                V_.tensor_tensor(rot[:, 0:nh * HD], t1[:, 0:nh * HD], t2[:, 0:nh * HD], ALU.add).then_inc(rot_done, 1)

            LAG = 2
            NU = NH * NT
            for u in range(NU + LAG):
                if u < NU:
                    dve.wait_ge(s_pe, u + 1)
                    if u == 0:
                        dve.wait_ge(qkT_pe, 14)
                    link(V_.tensor_reduce(mx[:, u % 4:u % 4 + 1],
                                          PS[:, 2 * (u % 2):2 * (u % 2) + 2, :].rearrange("p b n -> p (b n)")[:, 0:NKT * P],
                                          AX.X, ALU.max))
                    if u >= 4:
                        dve.wait_ge(exp_done, u - 3)
                    V_.tensor_scalar(nmx[:, u % 4:u % 4 + 1], mx[:, u % 4:u % 4 + 1], -SCALE, None,
                                     ALU.mult).then_inc(nm, 1)
                if 2 <= u <= 21:
                    ada_evac(u + 2)
                v = u - LAG
                if v >= 0:
                    dve.wait_ge(t_pe, v + 1)
                    qb = v % NT
                    V_.tensor_copy(PT[:, 3:6, qb * P:(qb + 1) * P],
                                   PS[:, 5, 0:3 * P].rearrange("p (k q) -> p k q", k=3)).then_inc(pt_dve, 1)
                if u < NU:
                    dve.wait_ge(exp_done, u + 1)
                    link(V_.reciprocal(rden[:, u % 4:u % 4 + 1], den[:, u % 4:u % 4 + 1]))
                    V_.tensor_scalar(Pb[:, u % 3, :], Pb[:, u % 3, :], rden[:, u % 4:u % 4 + 1], None,
                                     ALU.mult).then_inc(p_norm, 1)
            for k, (l, o_sc, o_sh) in enumerate(((0, SC2, SH2), (1, SC1, SH1), (1, SC2, SH2))):
                sc, sh = mod[l][:, o_sc:o_sc + DC], mod[l][:, o_sh:o_sh + DC]
                V_.tensor_tensor(fsc[:, k, :], lngT[:, k, :], sc, ALU.mult)
                link(V_.tensor_tensor(fsh[:, k, :], lnbT[:, k, :], sc, ALU.mult))
                V_.tensor_tensor(fsh[:, k, :], fsh[:, k, :], sh, ALU.add).then_inc(s_fold, 1)
            dve.wait_ge(s_fold, 3)

            def gate_cols(col, n):
                V_.tensor_copy(gcb, col.unsqueeze(2).broadcast_to([P, DC, P])).then_inc(gc_rd, 1)

            def norm_stats(j, r):
                V_.bn_stats(st6[:, j, 0:6], r[:, 0:512])
                link(V_.bn_stats(st6[:, j, 6:12], r[:, 512:1024]))

            def norm_scale(k):
                for j in range(NT):
                    ins = V_.bn_aggr(mv[:, j, :], st6[:, j, :])
                link(ins)
                V_.tensor_scalar(ms[:, 0:NT], mv[:, :, 1], EPS, None, ALU.add).then_inc(var_rd, 1)
                rsqrt(NT, std_rd, k + 1)
                V_.scalar_tensor_tensor(out=nb[:, :], in0=mv[:, :, 0], scalar=-1.0, in1=rs[:, 0:NT], op0=ALU.mult,
                                        op1=ALU.mult).then_inc(ab_rd, 1)

            def norm_tile(t, j, done):
                V_.tensor_scalar(t[:, j, :], t[:, j, :], mv[:, j, 0:1], rs[:, j:j + 1], ALU.subtract,
                                 ALU.mult).then_inc(done, 1)

            def mixer_out(l, k):
                if l:
                    dve.wait_ge(ln_rd, 2 * NT)
                for j in range(NT):
                    r = lt[:, j % 2, :]
                    dve.wait_ge(y_pe[l], NT + j + 1)
                    for n in range(2):
                        ins = V_.tensor_tensor(r[:, 512 * n:512 * n + 512], PS[:, 4 * n + j, :],
                                               G[:, 512 * n:512 * n + 512], ALU.mult)
                    link(ins)
                    link(V_.scalar_tensor_tensor(out=H[:, j, :], in0=H[:, j, :], scalar=ALPHA if l == 0 else 1.0, in1=r,
                                                 op0=ALU.mult, op1=ALU.add))
                    norm_stats(j, H[:, j, :])
                norm_scale(k)
                for j in (1, 3):
                    norm_tile(H, j, ln_nrm)

            def first_max(one, v, tmp, dec, mx1, n):
                link(V_.tensor_reduce(mx1, v, AX.X, ALU.max))
                link(V_.tensor_tensor(tmp, v, mx1.unsqueeze(2).broadcast_to([P, NT, n]), ALU.is_equal))
                link(V_.tensor_tensor(tmp, tmp, dec.unsqueeze(1).broadcast_to([P, NT, n]), ALU.mult))
                link(V_.tensor_reduce(mx1, tmp, AX.X, ALU.max))
                link(V_.tensor_tensor(one, tmp, mx1.unsqueeze(2).broadcast_to([P, NT, n]), ALU.is_equal))

            def moe(l):
                tr_evac(TR_R0 if l == 0 else TR_R1, uT, TOK, fsc[:, 2 * l, :], fsh[:, 2 * l, :])
                gate_cols(m(mod[l], G2), 2 * l + 1)
                dve.wait_ge(lg_pe, l + 1)
                V_.tensor_reduce(sel[:, :, :], PS[:, 5, :].rearrange("p (t g e) -> p t e g", t=NT, g=4)[:, :, 0:NE, :],
                                 AX.X, ALU.add).then_inc(lg_rd, 1)
                dve.wait_ge(sig_rd, l + 1)
                link(V_.tensor_tensor(sel[:, :, :], sc_[:, :, :], rb[:, :].unsqueeze(1).broadcast_to([P, NT, NE]), ALU.add))
                sv = sel[:, :, :].rearrange("p t (g e) -> p (t g) e", g=NG)
                V_.tensor_tensor(s6[:, :, 0:2], sv[:, :, 0:4:2], sv[:, :, 1:4:2], ALU.add)
                V_.tensor_tensor(s6[:, :, 2:4], sv[:, :, 0:2], sv[:, :, 2:4], ALU.add)
                V_.tensor_tensor(s6[:, :, 4:5], sv[:, :, 0:1], sv[:, :, 3:4], ALU.add)
                link(V_.tensor_tensor(s6[:, :, 5:6], sv[:, :, 1:2], sv[:, :, 2:3], ALU.add))
                link(V_.tensor_reduce(g4[:, :, :].rearrange("p t g -> p (t g)"), s6[:, :, :], AX.X, ALU.max))
                first_max(gmask[:, :, :], g4[:, :, :], cand[:, :, 0:NG], dec4, gm1[:, :], NG)
                gv = gmask[:, :, :].rearrange("p t g -> p (t g)").unsqueeze(2).broadcast_to([P, NT * NG, PER])
                link(V_.tensor_tensor(sv, sv, gv, ALU.mult))
                link(V_.tensor_scalar(g4[:, :, :], gmask[:, :, :], BIG, -BIG, ALU.mult, ALU.add))
                pv = g4[:, :, :].rearrange("p t g -> p (t g)").unsqueeze(2).broadcast_to([P, NT * NG, PER])
                link(V_.tensor_tensor(sv, sv, pv, ALU.add))
                first_max(o1[:, :, :], sel[:, :, :], cand[:, :, :], dec16, gm1[:, :], NE)
                link(V_.scalar_tensor_tensor(out=sel[:, :, :], in0=o1[:, :, :], scalar=-3e38, in1=sel[:, :, :],
                                             op0=ALU.mult, op1=ALU.add))
                first_max(o2[:, :, :], sel[:, :, :], cand[:, :, :], dec16, gm1[:, :], NE)
                V_.memset(MP[:, 0, :], 0.0)
                link(V_.tensor_tensor(cand[:, :, :], o1[:, :, :], o2[:, :, :], ALU.add))
                link(V_.tensor_copy(MP[:, 1, :], cand[:, 0, :]))
                for j in range(1, NT):
                    ins = V_.tensor_tensor(MP[:, j + 1, :], MP[:, j, :], cand[:, j, :], ALU.add)
                    if j < NT - 1:
                        link(ins)
                ins.then_inc(m_rd, 1)
                for k, o in enumerate((o1, o2)):
                    link(V_.tensor_tensor(smap[:, :, :], sc_[:, :, :], o[:, :, :], ALU.mult))
                    link(V_.tensor_reduce(wts[:, k, :], smap[:, :, :], AX.X, ALU.add))
                link(V_.tensor_tensor(wsum[:, :], wts[:, 0, :], wts[:, 1, :], ALU.add))
                link(V_.reciprocal(wsum[:, :], wsum[:, :]))
                link(V_.tensor_tensor(wts[:, :, :], wts[:, :, :], wsum[:, :].unsqueeze(1).broadcast_to([P, 2, NT]), ALU.mult))
                dve.wait_ge(rk_pe, l + 1)
                link(V_.tensor_tensor(gt7[:, :, :], PS[:, 5, 64:80].unsqueeze(2).broadcast_to([P, NE, 7]),
                                      thr.unsqueeze(1).broadcast_to([P, NE, 7]), ALU.is_gt))
                link(V_.tensor_reduce(nbk[:, :], gt7[:, :, :], AX.X, ALU.add))
                link(V_.tensor_scalar(nbk[:, :], nbk[:, :], 1.0, None, ALU.add))
                V_.memset(bs[:, 0:1], 0.0)
                link(V_.tensor_tensor_scan(bs[:, 1:NE + 1], ones[:, 0:NE], nbk[:, :], 0.0, ALU.mult, ALU.add))
                link(V_.tensor_scalar(bs[:, NE + 1:NE + 2], bs[:, NE:NE + 1], -1.0, float(ROWB - 1), ALU.mult, ALU.add))
                link(V_.tensor_scalar(bs64[:, :], bs[:, 0:NE + 1], float(BLK), None, ALU.mult))
                V_.tensor_copy(table[l][:, :], bs[0:1, :]).then_inc(tab_rd, 1)
                link(V_.tensor_tensor(smap[:, :, :], PS[:, 5, 0:64].rearrange("p (t e) -> p t e", t=NT),
                                      bs64[:, 0:NE].unsqueeze(1).broadcast_to([P, NT, NE]), ALU.add))
                for k, o in enumerate((o1, o2)):
                    link(V_.tensor_tensor(cand[:, :, :], smap[:, :, :], o[:, :, :], ALU.mult))
                    link(V_.tensor_reduce(slot[:, k, :], cand[:, :, :], AX.X, ALU.add))
                V_.tensor_copy(yidx[:, :, :], slot[:, :, :])
                link(V_.tensor_copy(srel[:, :, :], slot[:, :, :]))

                STEPS = 7
                loop = dlp[l]

                def onehot(lnk):
                    it = iota64.unsqueeze(1).broadcast_to([P, NT, BLK])
                    V_.tensor_tensor(oh, srel[:, 0, :].unsqueeze(2).broadcast_to([P, NT, BLK]), it, ALU.is_equal)
                    lnk(V_.tensor_tensor(oh2t, srel[:, 1, :].unsqueeze(2).broadcast_to([P, NT, BLK]), it, ALU.is_equal))
                    V_.tensor_tensor(oh, oh, oh2t, ALU.add).then_inc(oh_rd[l], 1)
                    lnk(V_.tensor_scalar(srel[:, :, :], srel[:, :, :], -float(BLK), None, ALU.add))

                def index():
                    V_.tensor_copy(gidx[0:BLK, :], PS[0:BLK, 6, 0:1]).then_inc(ix_rd[l], 1)

                def x_evac(lnk):
                    lnk(V_.tensor_tensor(xTt, PS[:, 2, :].rearrange("p (c s) -> p c s", c=DC),
                                         fsc[:, 2 * l, :].unsqueeze(2).broadcast_to([P, DC, BLK]), ALU.mult))
                    V_.tensor_tensor(xT, xTt, fsh[:, 2 * l, :].unsqueeze(2).broadcast_to([P, DC, BLK]),
                                     ALU.add).then_inc(xT_rd[l], 1)

                onehot(link)
                dve.wait_ge(ix_pe[l], 1)
                index()
                onehot(link)
                dve.wait_ge(xg_in[l], 16)
                dve.wait_ge(ix_pe[l], 2)
                index()
                onehot(link)
                dve.wait_ge(xt_pe[l], 1)
                x_evac(link)
                dve.wait_ge(gb_ev, 2 * l + 2)
                total = dve.value_load(table[l][0:1, NE:NE + 1], min_val=1, max_val=MAXB)
                with dve.Fori(0, total) as g:
                    k = [0]

                    def lnk(ins):
                        k[0] += 1
                        ins.then_inc(loop, 1)
                        dve.wait_ge(loop, g * 3 + k[0])

                    for h in range(2):
                        dve.wait_ge(silu_rd[l][h], g + 1)
                        V_.tensor_tensor(hid[:, 256 * h:256 * h + 256], gs[:, 256 * h:256 * h + 256],
                                         PS[BLK:P, h, 0:256], ALU.mult).then_inc(hid_rd[l][h], 1)
                    dve.wait_ge(xt_pe[l], g + 2)
                    x_evac(lnk)
                    dve.wait_ge(ix_pe[l], g + 3)
                    index()
                    onehot(lnk)
                    assert k[0] == 3
                    dve.wait_ge(y_st[l], g * 32 + 32)
                    dve.wait_ge(dn_pe[l], g + 1)
                    V_.tensor_tensor(ysb, PS[:, 5, :], G[:, 0:512], ALU.mult).then_inc(y_ev[l], 1)

                dve.wait_ge(ln_rd, NT * (2 * l + 1))
                for j in range(NT):
                    h = H[:, j, :]
                    dve.wait_ge(fg[l][j % 2], 32 * (j // 2 + 1))
                    link(V_.scalar_tensor_tensor(out=h, in0=yg[:, j % 2, 0, :], scalar=wts[:, 0, j:j + 1], in1=h,
                                                 op0=ALU.mult, op1=ALU.add))
                    V_.scalar_tensor_tensor(out=h, in0=yg[:, j % 2, 1, :], scalar=wts[:, 1, j:j + 1], in1=h,
                                            op0=ALU.mult, op1=ALU.add).then_inc(fg_used, 1)
                    dve.wait_ge(fg_used, l * NT + j + 1)
                    norm_stats(j, h)
                norm_scale((1, 4)[l])
                for j in (1, 3):
                    norm_tile(H, j, ln_nrm)

            dve.wait_ge(pv_pe, NH)
            gate_cols(m(mod[0], G1), 0)
            dve.wait_ge(gb_ev, 1)
            mixer_out(0, 0)
            moe(0)
            tr_evac(TR_M1, uT, TOK, fsc[:, 1, :], fsh[:, 1, :])
            gate_cols(m(mod[1], G1), 2)
            dve.wait_ge(wsT_pe, 1)
            V_.tensor_copy(wsT, PS[:, 0:2, :].rearrange("p b (g t) -> p (b g) t", g=4)).then_inc(wsT_ev, 1)
            for j in range(NT):
                dve.wait_ge(z_ev, 4 + j + 1)
                norm_stats(j, zv[:, j, :])
            norm_scale(2)
            for j in range(NT):
                norm_tile(zv, j, vn)
            dve.wait_ge(z_ev, 16)
            for g in range(8):
                dve.wait_ge(mix_pe, g + 1)
                o = zu[:, :, g * P:(g + 1) * P]
                V_.scalar_tensor_tensor(out=o, in0=PS[:, g % 4, :].rearrange("p (t d) -> p t d", t=NT),
                                        scalar=bsT[:, g:g + 1], in1=o, op0=ALU.add, op1=ALU.mult).then_inc(mix_ev, 1)
            tr_evac(TR_P1, uT, TOK, None, None)
            dve.wait_ge(gb_ev, 3)
            mixer_out(1, 3)
            moe(1)
            dve.wait_ge(s_lnw, 32 * 5)
            dve.wait_ge(ln_nrm, 8)
            for j in range(NT):
                if j % 2 == 0:
                    dve.wait_ge(nrm_act, 7 + j // 2)
                V_.tensor_tensor(H[:, j, :], H[:, j, :], LG[:, :], ALU.mult).then_inc(pgl, 1)

        @block.tensor
        def _(pe):
            mm = nc.tensor.matmul

            def weights(n):
                pe.wait_ge(w_in[n % RING], 16 * (n // RING + 1))

            def ada_rows(q, n):
                weights(n)
                if q > 4:
                    pe.wait_ge(ada_ev, q)
                w = slot_of(n).rearrange("p (k n) -> p k n", k=DC)
                bank = 4 + q if q < 4 else 7
                for kk in range(2):
                    for g in range(4):
                        k = 2 * g + kk
                        ins = mm(PS[32 * g:32 * g + 32, bank, :], silu_c[:, k, :], w[:, k, :],
                                 start=(kk == 0), stop=(kk == 1))
                ins.then_inc(ada_pe, 1)

            def ada_turn(q):
                pe.wait_ge(ar_ev, q + 1)
                src = arow[:, q, :] if q < 4 else arow1
                bank = 4 + q if q < 4 else 7
                for t in range(4):
                    ins = nc.tensor.transpose(PS[:, bank, t * P:(t + 1) * P], src[:, t * P:(t + 1) * P], ident[:, :])
                ins.then_inc(at_pe, 1)

            pe.wait_ge(s_const, 2)
            pe.wait_ge(s_small, 16 * 8)
            nc.tensor.transpose(PS[:, 0, 0:128], rows1, ident[:, :])
            nc.tensor.transpose(PS[:, 0, 128:168], rows2, ident[0:40, 0:40]).then_inc(s_bT_pe, 1)
            pe.wait_ge(s_silu, 1)

            n = 0
            for q in range(4):
                ada_rows(q, n)
                n += 1
                if q:
                    ada_turn(q - 1)
            ada_turn(3)

            def tr_items(first, srcs):
                for q in range(DC):
                    i = first + q
                    if i >= 4:
                        tr_wait(pe, i - 4)
                    for j, s in enumerate(srcs):
                        ins = nc.tensor.transpose(PS[:, i % 4, j * P:(j + 1) * P], s[:, q * P:(q + 1) * P], ident[:, :])
                    ins.then_inc(tr_pe, 1)

            pe.wait_ge(s_x, 16)
            pe.wait_ge(ada_ev, 1)
            tr_items(TR_X, [H[:, j, :] for j in range(NT)])
            pe.wait_ge(s_ctx, 16)
            tr_items(TR_C, [ctxn[:, j, :] for j in range(NX)])
            tr_wait(pe, TR_C + DC - 2)
            tr_wait(pe, TR_C + DC - 1)

            def qk_turn(i):
                nh = NKV if i < NKT else 4
                pe.wait_ge(rot_done, i + 1)
                if i >= 2:
                    pe.wait_ge(qk_ev, i - 1)
                for h in range(nh):
                    ins = nc.tensor.transpose(PS[:, i % 2, h * P:(h + 1) * P], rot[:, h * HD:(h + 1) * HD], ident[:, :])
                ins.then_inc(qkT_pe, 1)

            for i in range(14):
                ctx_item = i < NX
                if i in (0, NKT, NKT + NT):
                    weights(n)
                    w = slot_of(n).rearrange("p (k n) -> p k n", k=DC)
                if i >= 3:
                    pe.wait_ge(xn_done, i - 2)
                j = i if ctx_item else (i - NX) % NT
                a = ucT if ctx_item else uT
                for k in range(DC):
                    ins = mm(PS[:, 4 + i % 3, :], a[:, k, j * P:(j + 1) * P], w[:, k, :], start=(k == 0), stop=(k == DC - 1))
                ins.then_inc(qkv_pe, 1)
                if i in (NKT - 1, NKT + NT - 1, NKT + 2 * NT - 1):
                    n += 1
                if i:
                    qk_turn(i - 1)
            qk_turn(13)
            pe.wait_ge(qk_ev, 14)

            LAG = 2
            NU = NH * NT

            def pv(h):
                pe.wait_ge(pt_act, NT * (h + 1))
                pe.wait_ge(pt_dve, NT * (h + 1))
                if h:
                    pe.wait_ge(o_ev, h)
                kv = h // (NH // NKV)
                for k in range(NKT):
                    ins = mm(PS[:, 6, :], V[:, k, kv * HD:(kv + 1) * HD], PT[:, k, :], start=(k == 0), stop=(k == NKT - 1))
                ins.then_inc(pv_pe, 1)

            for u in range(NU + LAG):
                if u < NU:
                    h, qb = u // NT, u % NT
                    kv = h // (NH // NKV)
                    if u >= 2:
                        pe.wait_ge(exp_done, u - 1)
                    b = 2 * (u % 2)
                    q = qT[:, h, qb * P:(qb + 1) * P]
                    mm(PS[:, b, :], q, kT[:, kv, 0:512], start=True, stop=True)
                    mm(PS[:, b + 1, 0:NKT * P - 512], q, kT[:, kv, 512:NKT * P], start=True, stop=True).then_inc(s_pe, 1)
                v = u - LAG
                if 2 <= u <= 21:
                    ada_turn(u + 2)
                if v >= 0:
                    if v % NT == 0 and v:
                        pv(v // NT - 1)
                    pe.wait_ge(p_norm, v + 1)
                    if v:
                        pe.wait_ge(pt_act, v)
                        pe.wait_ge(pt_dve, v)
                    for k in range(NKT):
                        ins = nc.tensor.transpose(PS[:, 4 + k // 3, (k % 3) * P:(k % 3 + 1) * P],
                                                  Pb[:, v % 3, k * P:(k + 1) * P], ident[:, :])
                    ins.then_inc(t_pe, 1)
                if 1 <= u <= 20:
                    ada_rows(u + 3, n)
                    n += 1
            pv(NH - 1)
            pe.wait_ge(o_ev, NH)

            def gate_rows(k):
                pe.wait_ge(gc_rd, k + 1)
                for f in range(DC):
                    ins = mm(PS[:, 6 + f // 4, (f % 4) * P:(f % 4 + 1) * P], gcb[:, f, :], ident[:, :], start=True, stop=True)
                ins.then_inc(gb_pe, 1)
                pe.wait_ge(gb_ev, k + 1)

            def project(l, n):
                for half in range(2):
                    weights(n)
                    w = slot_of(n).rearrange("p (k n) -> p k n", k=DC)
                    for j in range(NT):
                        for k in range(DC):
                            ins = mm(PS[:, 4 * half + j, :], uT[:, k, j * P:(j + 1) * P], w[:, k, :],
                                     start=(k == 0), stop=(k == DC - 1))
                        ins.then_inc(y_pe[l], 1)
                    n += 1
                return n

            def moe(l):
                pe.wait_ge(nrm_act, 4 * l + 2)
                pe.wait_ge(ln_nrm, 4 * l + 2)
                tr_items(TR_R0 if l == 0 else TR_R1, [H[:, j, :] for j in range(NT)])
                last = (TR_R0 if l == 0 else TR_R1) + DC - 1
                tr_wait(pe, last - 1)
                tr_wait(pe, last)
                for kk in range(2):
                    for g in range(4):
                        k = 2 * g + kk
                        ins = mm(PS[32 * g:32 * g + 32, 4, :], wr[:, k, :], uT[:, k, :], start=(kk == 0), stop=(kk == 1))
                ins.then_inc(lr_pe, 1)
                pe.wait_ge(lr_ev, l + 1)
                for j in range(NT):
                    ins = nc.tensor.transpose(PS[:, 5, j * P:(j + 1) * P], lrow[:, j * P:(j + 1) * P], ident[:, :])
                ins.then_inc(lg_pe, 1)
                pe.wait_ge(gc_rd, 2 * l + 2)
                for f in range(DC):
                    half = f // 4
                    ins = mm(PS[BLK * half:BLK * half + BLK, 7, (f % 4) * P:(f % 4 + 1) * P], gcb[:, f, 0:BLK],
                             ident[:, :], start=True, stop=True)
                ins.then_inc(gb_pe, 1)
                pe.wait_ge(m_rd, l + 1)
                mflat = cand[:, :, :].rearrange("p t e -> p (t e)")
                mm(PS[:, 5, 0:64], tri[:, :], mflat, start=True, stop=False)
                mm(PS[:, 5, 0:64], ones[:, :], MP[:, 0:NT, :].rearrange("p t e -> p (t e)"), start=False, stop=True)
                mm(PS[:, 5, 64:80], ones[:, :], MP[:, NT, :], start=True, stop=True).then_inc(rk_pe, 1)

                def index():
                    for j in range(NT):
                        ins = mm(PS[0:BLK, 6, 0:1], oh[:, j, :], tokid[:, j:j + 1], start=(j == 0), stop=(j == NT - 1))
                    ins.then_inc(ix_pe[l], 1)

                def turn_x():
                    for f in range(DC):
                        ins = nc.tensor.transpose(PS[:, 2, f * BLK:(f + 1) * BLK], xg[:, f * P:(f + 1) * P],
                                                  ident[0:BLK, 0:BLK])
                    ins.then_inc(xt_pe[l], 1)

                pe.wait_ge(oh_rd[l], 1)
                index()
                pe.wait_ge(oh_rd[l], 2)
                pe.wait_ge(ix_rd[l], 1)
                index()
                pe.wait_ge(xg_in[l], 16)
                turn_x()
                base = base_moe[l]
                pe.wait_ge(tab_rd, l + 1)
                with pe.Fori(0, NE // 2) as pair:
                    for par in range(2):
                        lo = pe.value_load(table[l][0:1, bass.ds(pair * 2 + par, 1)], min_val=0, max_val=MAXB)
                        hi = pe.value_load(table[l][0:1, bass.ds(pair * 2 + (par + 1), 1)], min_val=1, max_val=MAXB)
                        nn = base + 3 * par

                        def landed(j):
                            pe.wait_ge(w_in[(nn + j) % RING], pair * 16 + 16 * ((nn + j) // RING + 1))

                        wg = slot_of(nn).rearrange("p (k n) -> p k n", k=DC)
                        wu = slot_of(nn + 1).rearrange("p (k n) -> p k n", k=DC)
                        wd = slot_of(nn + 2).rearrange("p (k n) -> p k n", k=FC)
                        with pe.Fori(lo, hi) as g:
                            pe.wait_ge(xT_rd[l], g + 1)
                            landed(0)
                            landed(1)
                            for h in range(2):
                                for k in range(DC):
                                    mm(PS[0:BLK, h, 0:256], xT[:, k, :], wg[:, k, 256 * h:256 * h + 256],
                                       start=(k == 0), stop=(k == DC - 1))
                                    ins = mm(PS[BLK:P, h, 0:256], xT[:, k, :], wu[:, k, 256 * h:256 * h + 256],
                                             start=(k == 0), stop=(k == DC - 1))
                                ins.then_inc(gu[l][h], 1)

                            def turn_hidden(h):
                                pe.wait_ge(hid_rd[l][h], g + 1)
                                pe.nop(nofuse=True)
                                for f in range(2):
                                    ins = nc.tensor.transpose(PS[:, 3 + h, f * BLK:(f + 1) * BLK],
                                                              hid[:, (2 * h + f) * P:(2 * h + f + 1) * P],
                                                              ident[0:BLK, 0:BLK])
                                ins.then_inc(ht_pe[l][h], 1)

                            turn_hidden(0)
                            pe.wait_ge(xg_in[l], g * 16 + 32)
                            pe.nop(nofuse=True)
                            turn_x()
                            landed(2)

                            def down(h):
                                pe.wait_ge(ht_rd[l][h], g + 1)
                                for k in (2 * h, 2 * h + 1):
                                    for half in range(2):
                                        ins = mm(PS[BLK * half:BLK * half + BLK, 5, :], hidT[:, k, :],
                                                 wd[:, k, 512 * half:512 * half + 512],
                                                 start=(k == 0), stop=(k == FC - 1))
                                return ins

                            down(0)
                            turn_hidden(1)
                            pe.wait_ge(oh_rd[l], g + 3)
                            pe.wait_ge(ix_rd[l], g + 2)
                            index()
                            down(1).then_inc(dn_pe[l], 1)

            gate_rows(0)
            n = project(0, n)
            moe(0)
            pe.wait_ge(nrm_act, 4)
            pe.wait_ge(ln_nrm, 4)
            tr_items(TR_M1, [H[:, j, :] for j in range(NT)])
            tr_wait(pe, TR_M1 + DC - 2)
            tr_wait(pe, TR_M1 + DC - 1)
            pe.wait_ge(s_ws, 16)
            for g in range(8):
                ins = nc.tensor.transpose(PS[:, g // 4, (g % 4) * P:(g % 4 + 1) * P], ws[:, g, :], ident[:, :])
            ins.then_inc(wsT_pe, 1)
            n = base_s1
            for i in range(16):
                if i % 4 == 0:
                    weights(n)
                    w = slot_of(n).rearrange("p (k n) -> p k n", k=DC)
                if i >= 4:
                    pe.wait_ge(z_ev, i - 3)
                j = i % 4
                for k in range(DC):
                    ins = mm(PS[:, 4 + i % 4, :], uT[:, k, j * P:(j + 1) * P], w[:, k, :], start=(k == 0), stop=(k == DC - 1))
                ins.then_inc(z_pe, 1)
                if i % 4 == 3:
                    n += 1
            pe.wait_ge(z_ev, 16)
            gate_rows(2)
            pe.wait_ge(wsT_ev, 1)
            pe.wait_ge(v_rd, NT)
            for g in range(8):
                if g >= 4:
                    pe.wait_ge(mix_ev, g - 3)
                mm(PS[:, g % 4, :], wsT[:, g, :], zv[:, :, g * P:(g + 1) * P], start=True, stop=True).then_inc(mix_pe, 1)
            pe.wait_ge(mix_ev, 8)
            tr_items(TR_P1, [zu[:, j, :] for j in range(NT)])
            tr_wait(pe, TR_P1 + DC - 2)
            tr_wait(pe, TR_P1 + DC - 1)
            n = project(1, n)
            moe(1)


_INS = ['x', 'c', 'ctx', 'c_ctx', 'w_ada', 'b_ada', 'ln_g', 'ln_b', 'a_wqkv', 'a_qg', 'a_kg', 'a_wo', 'b_win', 'b_vg',
        'b_vb', 'b_ws', 'b_bs', 'b_wout', 'w_router', 'router_bias', 'e_gate', 'e_up', 'e_down']
_OUT = ((1, 512, 1024), 'float32')
GRID_W, HEAD_DIM, ROPE_THETA = 64, 128, 10000.0


def rope_tables(n):
    import numpy as np
    half = HEAD_DIM // 2
    inv = (np.float32(1.0) / (np.float32(ROPE_THETA) ** (np.arange(0, half, 2, dtype=np.float32) / np.float32(half))))
    t = np.arange(n)
    ang = np.concatenate([(t // GRID_W).astype(np.float32)[:, None] * inv,
                          (t % GRID_W).astype(np.float32)[:, None] * inv], -1)
    cos, sin = np.cos(ang), np.sin(ang)
    return (np.repeat(cos, 2, axis=1).astype(np.float32),
            np.stack([-sin, sin], -1).reshape(n, HEAD_DIM).astype(np.float32))


def kernel(**inputs):
    import numpy as _np
    import concourse.bacc as _bacc
    from concourse import mybir as _mybir
    from concourse.bass_utils import run_bass_kernel_spmd as _run

    nc = _bacc.Bacc("TRN2", target_bir_lowering=False, num_devices=1)
    arrays, args = {}, []
    for name in _INS:
        a = _np.ascontiguousarray(inputs[name])
        arrays[f"in_{name}_dram"] = a
        args.append(nc.dram_tensor(f"in_{name}_dram", a.shape, _mybir.dt.from_np(a.dtype), kind="ExternalInput").ap())
    for name, a in zip(("rope_cos", "rope_sin"), rope_tables(512)):
        arrays[f"{name}_dram"] = a
        args.append(nc.dram_tensor(f"{name}_dram", a.shape, _mybir.dt.from_np(a.dtype), kind="ExternalInput").ap())
    shape, dtype = _OUT
    args.append(nc.dram_tensor("out_0_dram", shape, _mybir.dt.from_np(_np.dtype(dtype)), kind="ExternalOutput").ap())
    backbone(nc, *args)
    r = _run(nc, [arrays], core_ids=[0])
    return r.results[0]["out_0_dram"]
```

```python
from contextlib import ExitStack

import concourse.bass as bass
from concourse import mybir

ALU = mybir.AluOpType
ACT = mybir.ActivationFunctionType
AX = mybir.AxisListType
F32 = mybir.dt.float32
I32 = mybir.dt.int32

P = 128
EPS = 1e-6
RING = 6
BLK = 64
BIG = 1e30


def backbone(nc, x, c, ctx_tok, c_ctx, w_ada, b_ada, ln_g, ln_b, a_wqkv, a_qg, a_kg, a_wo, b_win, b_vg, b_vb, b_ws,
             b_bs, b_wout, w_router, router_bias, e_gate, e_up, e_down, rope_cos, rope_sin, out):
    D = x.shape[2]
    NT = x.shape[1] // P
    NX = ctx_tok.shape[1] // P
    DC = D // P
    DEPTH = w_ada.shape[0]
    ALPHA = float((2 * DEPTH) ** 0.25)
    HD = a_qg.shape[1]
    NH = a_wo.shape[1] // HD
    NKV = (a_wqkv.shape[2] // HD - NH) // 2
    NKT = NX + NT
    SCALE = float(HD) ** -0.5
    NE = w_router.shape[1]
    NG = 4
    PER = NE // NG
    FE = e_gate.shape[3]
    FC = FE // P
    TOK = NT * P
    MAXB = (NE + (2 * TOK - NE) // BLK + 1) // 2 * 2
    NTHR = TOK // BLK - 1
    SH1, SC1, G1, SH2, SC2, G2 = range(0, 6 * DC, DC)
    assert D == 1024 and NT == 4 and NX == 2 and HD == P and NH == 8 and NKV == 2 and FE == 512 and DEPTH == 2
    assert (MAXB - NE) * BLK == 2 * TOK

    hscr = [nc.dram_tensor(f"tokens_{l}", [TOK, D], F32).ap() for l in range(DEPTH)]
    yscr = [nc.dram_tensor(f"expert_rows_{l}", [MAXB * BLK, D], F32).ap() for l in range(DEPTH)]

    with ExitStack() as st:
        def sb(name, shape, dt=F32):
            return st.enter_context(nc.sbuf_tensor(name, shape, dt))

        def sem(name):
            return st.enter_context(nc.semaphore(name))

        ring = sb("ring", [P, RING, 4096])
        H = sb("H", [P, NT, D])
        uT = sb("uT", [P, DC, TOK])
        RD = sb("RD", [P, 4096])
        RE = sb("RE", [P, 4096])
        RFW = sb("RFW", [P, 6144])
        RF, RW = RFW[:, 0:3072], RFW[:, 3072:6144]
        LG = sb("LG", [P, D])
        LB = sb("LB", [P, D])
        G = sb("G", [P, D])
        ident = sb("ident", [P, P])
        ones = sb("ones", [P, P])
        tri = sb("tri", [P, P])
        ctxn = RD[:, 0:2048].rearrange("p (t d) -> p t d", t=NX)
        ucT = RD[:, 2048:4096].rearrange("p (c t) -> p c t", c=DC)
        PT = RD[:, 0:NKT * TOK].rearrange("p (k q) -> p k q", k=NKT)
        zu = RD[:, :].rearrange("p (t d) -> p t d", t=NT)
        yg = RD[:, :].rearrange("p (b k d) -> p b k d", b=2, k=2)
        qT = RE[:, :].rearrange("p (h q) -> p h q", h=NH)
        zv = RE[:, :].rearrange("p (t d) -> p t d", t=NT)
        kT = RF[:, 0:1536].rearrange("p (h k) -> p h k", h=NKV)
        V = RF[:, 1536:3072].rearrange("p (k d) -> p k d", k=NKT)
        ws = RF[:, 0:1024].rearrange("p (g s) -> p g s", g=8)
        wsT = RF[:, 1024:2048].rearrange("p (g s) -> p g s", g=8)
        xn, t1, t2, rot, junk = (RW[:, 512 * i:512 * i + 512] for i in range(5))
        Pb = RW[:, 0:2304].rearrange("p (b k) -> p b k", b=3)
        arow = RW[:, 0:2048].rearrange("p (q n) -> p q n", q=4)
        arow1 = RW[:, 2304:2816]
        lrow = RW[:, 1024:1536]
        gcb = RW[:, 0:1024].rearrange("p (c m) -> p c m", c=DC)
        lt = RW[:, 1024:3072].rearrange("p (b d) -> p b d", b=2)
        ropeC = LG[:, 0:512].rearrange("p (t d) -> p t d", t=NT)
        ropeS = LG[:, 512:1024].rearrange("p (t d) -> p t d", t=NT)
        xga = RE[0:BLK, 0:1024]
        xg = RW[0:BLK, 1024:2048]
        xT = RE[:, 1024:1536].rearrange("p (c s) -> p c s", c=DC)
        xTt = RE[:, 1536:2048].rearrange("p (c s) -> p c s", c=DC)
        gs = RE[0:BLK, 2048:2560]
        hid = RE[0:BLK, 2560:3072]
        hidT = RE[:, 3072:3328].rearrange("p (k s) -> p k s", k=FC)
        ysb = [RE[:, 3328:3840], RW[:, 2560:3072]]
        oh = RW[:, 2048:2304].rearrange("p (t s) -> p t s", t=NT)
        oh2t = RW[:, 2304:2560].rearrange("p (t s) -> p t s", t=NT)

        silu_c = sb("silu_c", [P, DC, 32])
        craw = sb("craw", [P, 2, DC])
        rows1 = RE[:, 0:P]
        rows2 = RE[0:40, P:2 * P]
        cols = sb("cols", [P, 168])
        badaT = cols[:, 0:96].rearrange("p (l m) -> p l m", l=2)
        lngT = cols[:, 96:128].rearrange("p (k c) -> p k c", k=4)
        lnbT = cols[:, 128:160].rearrange("p (k c) -> p k c", k=4)
        bsT = cols[:, 160:168]
        fsc = sb("fsc", [P, 3, DC])
        fsh = sb("fsh", [P, 3, DC])
        mod = [sb(f"mod{l}", [P, 48]) for l in range(DEPTH)]
        modc = sb("modc", [P, 16])
        qg = sb("qg", [P, HD])
        kg = sb("kg", [P, HD])
        wr = sb("wr", [P, DC, 32])
        atmp = sb("atmp", [P, 4, 2])
        rb = sb("rb", [P, NE])
        warm = sb("warm", [P, 1])
        ss = sb("ss", [P, 4])
        ms = sb("ms", [P, 4])
        rt = sb("rt", [P, 4])
        rs = sb("rs", [P, 4])
        nt = sb("nt", [P, 4])
        mx = sb("mx", [P, 4])
        nmx = sb("nmx", [P, 4])
        den = sb("den", [P, 4])
        rden = sb("rden", [P, 4])
        st6 = sb("st6", [P, NT, 12])
        mv = sb("mv", [P, NT, 2])
        nb = sb("nb", [P, NT])
        sc_ = sb("sc_", [P, NT, NE])
        sel = sb("sel", [P, NT, NE])
        s6 = sb("s6", [P, 16, 6])
        g4 = sb("g4", [P, NT, NG])
        gm1 = sb("gm1", [P, NT])
        gmask = sb("gmask", [P, NT, NG])
        cand = sb("cand", [P, NT, NE])
        o1 = sb("o1", [P, NT, NE])
        o2 = sb("o2", [P, NT, NE])
        MP = sb("MP", [P, NT + 1, NE])
        wts = sb("wts", [P, 2, NT])
        wsum = sb("wsum", [P, NT])
        gtn = sb("gtn", [P, NE, NTHR])
        gpr = sb("gpr", [P, MAXB // 2])
        nbk = sb("nbk", [P, NE])
        bs = sb("bs", [P, NE + 3])
        first_slot = sb("first_slot", [P, NE])
        smap = sb("smap", [P, NT, NE])
        slot = sb("slot", [P, 2, NT])
        srel = sb("srel", [P, 2, NT])
        yidx = sb("yidx", [P, 2, NT], I32)
        table = [sb(f"table{l}", [1, NE + 3], I32) for l in range(DEPTH)]
        gidx = sb("gidx", [P, 2], I32)
        at = {}
        for name, width in (("slot", BLK), ("dec16", NE), ("dec4", NG), ("token", NT), ("thr", NTHR), ("pair", MAXB // 2)):
            first = sum(b - a for a, b in at.values())
            at[name] = (first, first + width)
        ic = sb("ic", [P, first + width], I32)
        fc = sb("fc", [P, first + width])
        iota_s, dec16, dec4, tokid, thr, even = (fc[:, a:b] for a, b in at.values())

        PS = st.enter_context(nc.psum_tensor("PS", [P, 8, 512], F32))

        static0 = ([("ada", 0, q) for q in range(4)] + [("qkv", 0, n) for n in (2, 0, 1)]
                   + [("ada", 0, q) for q in range(4, 12)] + [("ada", 1, q) for q in range(12)]
                   + [("wo", 0, 0), ("wo", 0, 1)])
        static1 = [("win", 0, n) for n in (2, 3, 0, 1)] + [("wout", 0, 0), ("wout", 0, 1)]
        S0 = len(static0)
        slots = [ring[:, b, :] for b in range(RING)] + [uT[:, :, :].rearrange("p c t -> p (c t)"), RD[:, :], RFW[:, 0:4096]]
        nloads = [0] * len(slots)
        place, moe_place = [], []

        def plan(b, loads=1):
            nloads[b] += loads
            return b, nloads[b] - loads + 1

        place += [plan(i % RING) for i in range(S0)]
        for l in range(DEPTH):
            if l:
                place += [plan(moe_place[0][e % 3][j][0]) for e in (NE - 3, NE - 1) for j in range(3)]
            banks = [[b for b, _ in place[-6:-3]], [b for b, _ in place[-3:]], [RING, RING + 1, RING + 2]]
            moe_place.append([[plan(b, (NE - e + 2) // 3) for b in banks[e]] for e in range(3)])

        w_in = [sem(f"weights_in_{b}") for b in range(len(slots))]
        s_c = sem("cond_loaded")
        s_x = sem("x_loaded")
        s_ctx = sem("ctx_loaded")
        s_small = sem("small_loaded")
        s_rope = sem("rope_loaded")
        s_lnw = sem("ln_weights_loaded")
        s_ws = sem("spatial_weights_loaded")
        s_const = sem("constants_ready")
        s_ic = sem("iota_ready")
        s_silu = sem("silu_c_ready")
        s_bT_pe = sem("bias_rows_turned")
        ada_pe, ar_ev, at_pe, ada_ev = (sem("ada_rows_in_psum"), sem("ada_rows_ready"), sem("ada_cols_in_psum"),
                                        sem("ada_ready"))
        s_zero, s_fold, lr_pe, lr_ev, lg_rd = (sem("pads_zeroed"), sem("folded_ready"), sem("logit_rows_in_psum"),
                                               sem("logit_rows_ready"), sem("logits_ready"))
        ab_rd, lnw_sc = sem("norm_scale_ready"), sem("ln_rows_scaled")
        nrm_act = sem("ln_normed_by_act")
        tr_pe, tr_act, tr_dve = sem("turned_in_psum"), sem("turned_by_act"), sem("turned_by_dve")
        qkv_pe, sq_done, ms_done, sqrt_done = sem("qkv_in_psum"), sem("squares_done"), sem("meansq_ready"), sem("sqrt_ready")
        xn_done, t1_done, rot_done = sem("normed"), sem("rope_cos_part"), sem("rotated")
        qkT_pe, qk_ev = sem("qk_turned_in_psum"), sem("qkT_ready")
        s_pe, nm, exp_done, p_norm = sem("scores_in_psum"), sem("negmax_ready"), sem("exp_done"), sem("probs_ready")
        t_pe, pt_act, pt_dve = sem("probs_turned_in_psum"), sem("probsT_by_act"), sem("probsT_by_dve")
        pv_pe, o_ev = sem("attn_out_in_psum"), sem("attn_out_ready")
        gc_rd, gb_pe, gb_ev = sem("gate_cols_spread"), sem("gate_rows_in_psum"), sem("gate_rows_ready")
        y_pe = [sem(f"mixer_out_in_psum_{l}") for l in range(DEPTH)]
        var_rd, std_rd, ln_nrm, ln_rd = sem("ln_var_ready"), sem("ln_std_ready"), sem("ln_normed"), sem("ln_tile_ready")
        pgl = sem("ln_gain_applied")
        z_pe, z_ev = sem("mlp_in_psum"), sem("gelu_done")
        vn, vg1, v_rd = sem("v_normed"), sem("v_gain_applied"), sem("v_ready")
        wsT_pe, wsT_ev = sem("spatial_turned_in_psum"), sem("spatialT_ready")
        mix_pe, mix_ev = sem("mixed_in_psum"), sem("gated_ready")
        s_hw = [sem(f"tokens_stored_{l}") for l in range(DEPTH)]
        lg_pe, sig_rd, m_rd, rk_pe, tab_rd = (sem("logits_in_psum"), sem("scores_ready"), sem("choice_ready"),
                                              sem("ranks_in_psum"), sem("table_ready"))
        L = range(DEPTH)
        oh_rd = [sem(f"onehot_ready_{l}") for l in L]
        ix_pe = [sem(f"index_in_psum_{l}") for l in L]
        ix_rd = [sem(f"index_ready_{l}") for l in L]
        xg_in = [sem(f"gathered_{l}") for l in L]
        x0_in = [sem(f"block_0_gathered_{l}") for l in L]
        xg_rd = [sem(f"block_rows_ready_{l}") for l in L]
        xt_pe = [sem(f"gathered_turned_{l}") for l in L]
        xT_rd = [sem(f"block_xT_ready_{l}") for l in L]
        gu = [[sem(f"gate_up_{h}_in_psum_{l}") for h in range(2)] for l in L]
        silu_rd = [[sem(f"silu_{h}_ready_{l}") for h in range(2)] for l in L]
        hid_rd = [[sem(f"hidden_{h}_ready_{l}") for h in range(2)] for l in L]
        ht_pe = [[sem(f"hidden_{h}_turned_{l}") for h in range(2)] for l in L]
        ht_rd = [[sem(f"hiddenT_{h}_ready_{l}") for h in range(2)] for l in L]
        dn_pe = [sem(f"block_out_in_psum_{l}") for l in L]
        y_ev = [sem(f"block_out_ready_{l}") for l in L]
        y_st = [[sem(f"block_out_stored_{l}_{b}") for b in range(2)] for l in L]
        dlp = [sem(f"dve_loop_chain_{l}") for l in L]
        fg = [[sem(f"expert_rows_in_{l}_{b}") for b in range(2)] for l in L]
        fg_used = sem("expert_rows_used")
        out_rd, out0_rd = sem("out_tile_ready"), sem("out_tile_0_ready")
        s_out = sem("out_stored")
        chain = sem("dve_chain")
        pchain = sem("pool_chain")

        block = st.enter_context(nc.Block())

        def tr_wait(eng, i):
            eng.wait_ge(tr_dve if i % 2 else tr_act, i // 2 + 1)

        TR_X, TR_C, TR_R0, TR_M1, TR_P1, TR_R1 = 0, 8, 16, 24, 32, 40

        @block.sync
        def _(sp):
            wqkv = a_wqkv[0].rearrange("(k p) n -> p k n", p=P)
            wo = a_wo[0].rearrange("(k p) n -> p k n", p=P)
            win = b_win[0].rearrange("(k p) n -> p k n", p=P)
            wout = b_wout[0].rearrange("(k p) n -> p k n", p=P)
            ada = [w_ada[l].rearrange("(p k) n -> p k n", k=DC) for l in range(DEPTH)]
            view = {"qkv": wqkv, "wo": wo, "win": win, "wout": wout}

            def load_static(n, kind, l, q):
                src = (ada[l] if kind == "ada" else view[kind])[:, :, 512 * q:512 * q + 512]
                b = place[n][0]
                sp.dma_start(slots[b].rearrange("p (k n) -> p k n", k=DC), src).then_inc(w_in[b], 16)

            def load_expert(l, e, par, j):
                b = moe_place[l][par][j][0]
                dst = slots[b]
                if j < 2:
                    src = (e_gate, e_up)[j][l, e].rearrange("(k p) n -> p k n", p=P)
                    dst = dst.rearrange("p (k n) -> p k n", k=DC)
                else:
                    src = e_down[l, e].rearrange("(k p) n -> p k n", p=P)
                    dst = dst.rearrange("p (k n) -> p k n", k=FC)
                sp.dma_start(dst, src).then_inc(w_in[b], 16)

            def expert_in(l, par, j, turn):
                b, number = moe_place[l][par][j]
                sp.wait_ge(w_in[b], turn * 16 + 16 * number)

            def static_in(n):
                b, number = place[n]
                sp.wait_ge(w_in[b], 16 * number)

            def wait_used(ch):
                kind, l, q = ch
                if kind == "ada":
                    sp.wait_ge(ada_pe, 12 * l + q + 1)
                elif kind == "qkv":
                    sp.wait_ge(qkv_pe, {2: NKT, 0: NKT + NT, 1: NKT + 2 * NT}[q])
                elif kind == "win":
                    sp.wait_ge(z_pe, NT * ((q + 2) % 4 + 1))
                else:
                    sp.wait_ge(y_pe[0 if kind == "wo" else 1], NT * (q + 1))

            for l in range(DEPTH):
                if l == 0:
                    sp.dma_start(craw[:, 0, :], c[0].rearrange("(p k) -> p k", k=DC)).then_inc(s_c, 16)
                    sp.dma_start(craw[:, 1, :], c_ctx.rearrange("(p k) -> p k", k=DC)).then_inc(s_c, 16)
                    sp.dma_start(rows1[0:96, :], b_ada.rearrange("l (m p) -> (l m) p", p=P)).then_inc(s_small, 16)
                    sp.dma_start(rows1[96:128, :], ln_g.rearrange("l k (c p) -> (l k c) p", p=P)).then_inc(s_small, 16)
                    sp.dma_start(rows2[0:32, :], ln_b.rearrange("l k (c p) -> (l k c) p", p=P)).then_inc(s_small, 16)
                    for n, ch in enumerate(static0):
                        if n == 3:
                            sp.dma_start(H[:, :, :], x[0].rearrange("(t p) d -> p t d", p=P)).then_inc(s_x, 16)
                        if n == 4:
                            sp.dma_start(ctxn, ctx_tok[0].rearrange("(t p) d -> p t d", p=P)).then_inc(s_ctx, 16)
                        if n == 5:
                            sp.dma_start(ropeC, rope_cos.rearrange("(t p) d -> p t d", p=P)).then_inc(s_rope, 16)
                            sp.dma_start(ropeS, rope_sin.rearrange("(t p) d -> p t d", p=P)).then_inc(s_rope, 16)
                        if n >= RING:
                            wait_used(static0[n - RING])
                        load_static(n, *ch)
                    for m in range(DEPTH):
                        for par in range(2):
                            first = NE * BLK + par * TOK
                            sp.dma_start(yscr[m][first:first + TOK, :], x[0]).then_inc(y_st[m][par], 16)
                else:
                    for b in range(2):
                        sp.wait_ge(fg[l - 1][b], 32 * (NT // 2))
                    for i, ch in enumerate(static1):
                        if i:
                            static_in(S0 + i - 1)
                        load_static(S0 + i, *ch)
                for i in range(6):
                    wait_used((static0, static1)[l][i - 6])
                    if i < 2:
                        static_in(S0 + l * len(static1) - 2 + i)
                    else:
                        expert_in(l, (i - 2) // 3, (i - 2) % 3, 0)
                    load_expert(l, i // 3, i // 3, i % 3)
                sp.wait_ge(gb_pe, 2 * l + 2)
                for j in range(3):
                    if j < 2:
                        expert_in(l, 1, j + 1, 0)
                    else:
                        expert_in(l, 2, 0, 0)
                    load_expert(l, 2, 2, j)
                sp.wait_ge(tab_rd, l + 1)

                def follow(t, par, e):
                    col = bass.ds(t * 3 + (par - 2), 1) if e is None else slice(e - 2, e - 1)
                    last = sp.value_load(table[l][0:1, col], min_val=1, max_val=MAXB)
                    for j in range(3):
                        sp.wait_ge(dn_pe[l] if j == 2 else gu[l][1], last)
                        sp.nop(nofuse=True)
                        if j == 2:
                            expert_in(l, par, 0, t)
                        else:
                            expert_in(l, (par - 1) % 3, j + 1, t if par else t - 1)
                        load_expert(l, t * 3 + par if e is None else e, par, j)

                with sp.Fori(1, NE // 3) as t:
                    for par in range(3):
                        follow(t, par, None)
                follow(NE // 3, (NE - 1) % 3, NE - 1)

        @block.gpsimd
        def _(pool):
            nchain = [0]

            def link(ins):
                nchain[0] += 1
                ins.then_inc(pchain, 1)
                pool.wait_ge(pchain, nchain[0])

            nc.gpsimd.memset(silu_c[:, :, :], 0.0).then_inc(s_zero, 1)
            nc.gpsimd.memset(wr[:, :, :], 0.0).then_inc(s_zero, 1)
            nc.gpsimd.memset(ident[:, :], 0.0).then_inc(pchain, 1)
            nc.gpsimd.memset(ones[:, :], 1.0).then_inc(pchain, 1)
            nchain[0] = 2
            pool.wait_ge(pchain, 2)
            nc.gpsimd.affine_select(out=ident[:, :], in_=ident[:, :], compare_op=ALU.not_equal, fill=1.0, base=0,
                                    pattern=[[-1, P]], channel_multiplier=1).then_inc(s_const, 1)
            nc.gpsimd.affine_select(out=tri[:, :], in_=ones[:, :], compare_op=ALU.is_gt, fill=0.0, base=0,
                                    pattern=[[1, P]], channel_multiplier=-1).then_inc(s_const, 1)
            def iota(name, step, base, by_row):
                a, b = at[name]
                return nc.gpsimd.iota(ic[:, a:b], pattern=[[step, b - a]], base=base, channel_multiplier=by_row)

            iota("slot", 1, 0, 0)
            iota("dec16", -1, NE, 0)
            iota("dec4", -1, NG, 0)
            iota("token", P, 0, 1)
            iota("thr", BLK, BLK, 0)
            iota("pair", 2, 0, 0).then_inc(s_ic, 1)

            pool.wait_ge(s_rope, 32)
            for i in range(14):
                if i < NX:
                    continue
                nh = NKV if i < NKT else 4
                j = (i - NX) % NT
                pool.wait_ge(xn_done, i + 1)
                if i > NX:
                    pool.wait_ge(rot_done, i)
                nc.gpsimd.tensor_tensor(t1[:, 0:nh * HD].rearrange("p (h d) -> p h d", h=nh),
                                        xn[:, 0:nh * HD].rearrange("p (h d) -> p h d", h=nh),
                                        ropeC[:, j:j + 1, :].broadcast_to([P, nh, HD]), ALU.mult).then_inc(t1_done, 1)

            def ln_affine(k):
                for j in range(NT):
                    nc.gpsimd.tensor_tensor(H[:, j, :], H[:, j, :], LG[:, :], ALU.mult).then_inc(pgl, 1)
                for j in range(NT):
                    pool.wait_ge(pgl, NT * k + j + 1)
                    nc.gpsimd.tensor_tensor(H[:, j, :], H[:, j, :], LB[:, :], ALU.add).then_inc(ln_rd, 1)

            def moe(l):
                pool.wait_ge(s_hw[l], 16 * NT)
                pool.wait_ge(tr_pe, (TR_R0 if l == 0 else TR_R1) + DC)
                pool.wait_ge(lnw_sc, 2 if l == 0 else 6)
                ln_affine(2 * l)
                pool.wait_ge(tab_rd, l + 1)

                def gather(par, rows=xga, done=xg_in[l]):
                    nc.gpsimd.indirect_dma_start(
                        out=rows, out_offset=None, in_=hscr[l],
                        in_offset=bass.IndirectOffsetOnAxis(ap=gidx[0:BLK, par:par + 1], axis=0)).then_inc(done, 16)

                def hand_over():
                    nc.gpsimd.tensor_copy(xg, xga).then_inc(xg_rd[l], 1)

                pool.wait_ge(ix_rd[l], 1)
                gather(0, xg, x0_in[l])
                pool.wait_ge(ix_rd[l], 2)
                gather(1)
                pairs = pool.value_load(table[l][0:1, NE + 1:NE + 2], min_val=1, max_val=MAXB // 2)
                with pool.Fori(0, pairs) as gg:
                    for par in range(2):
                        g = gg * 2 + par
                        pool.wait_ge(xg_in[l], g * 16 + 16)
                        pool.wait_ge(xt_pe[l], g + 1)
                        pool.nop(nofuse=True)
                        hand_over()
                        pool.wait_ge(ix_rd[l], g + 3)
                        pool.nop(nofuse=True)
                        pool.wait_ge(xg_rd[l], g + 1)
                        pool.nop(nofuse=True)
                        gather(par)
                pairs = pool.value_load(table[l][0:1, NE + 1:NE + 2], min_val=1, max_val=MAXB // 2)
                for par in range(2):
                    pool.wait_ge(y_st[l][par], pairs * 16 + 16)
                    pool.nop(nofuse=True)
                pool.wait_ge(xg_in[l], pairs * 32 + 16)
                pool.nop(nofuse=True)
                for j in range(NT):
                    if l * NT + j >= 2:
                        pool.wait_ge(fg_used, l * NT + j - 1)
                    for k in range(2):
                        nc.gpsimd.indirect_dma_start(
                            out=yg[:, j % 2, k, :], out_offset=None, in_=yscr[l],
                            in_offset=bass.IndirectOffsetOnAxis(ap=yidx[:, k, j:j + 1], axis=0),
                        ).then_inc(fg[l][j % 2], 16)

            moe(0)
            pool.wait_ge(tr_pe, TR_M1 + DC)
            pool.wait_ge(lnw_sc, 4)
            ln_affine(1)
            pool.wait_ge(s_lnw, 32 * 3)
            for j in range(NT):
                pool.wait_ge(vn, j + 1)
                nc.gpsimd.tensor_tensor(zv[:, j, :], zv[:, j, :], LG[:, :], ALU.mult).then_inc(vg1, 1)
                pool.wait_ge(vg1, j + 1)
                nc.gpsimd.tensor_tensor(zv[:, j, :], zv[:, j, :], LB[:, :], ALU.add).then_inc(v_rd, 1)
            moe(1)
            pool.wait_ge(s_lnw, 32 * 5)
            pool.wait_ge(nrm_act, 7)
            link(nc.gpsimd.tensor_tensor(H[:, 0, :], H[:, 0, :], LG[:, :], ALU.mult))
            nc.gpsimd.tensor_tensor(H[:, 0, :], H[:, 0, :], LB[:, :], ALU.add).then_inc(out0_rd, 1)

        @block.scalar
        def _(act):
            A = nc.scalar.activation
            act.dma_start(rows2[32:40, :], b_bs[0]).then_inc(s_small, 16)
            act.dma_start(qg[:, :], a_qg[0:1, :].broadcast_to([P, HD])).then_inc(s_small, 16)
            act.dma_start(kg[:, :], a_kg[0:1, :].broadcast_to([P, HD])).then_inc(s_small, 16)
            act.dma_start(rb[:, :], router_bias.rearrange("(o n) -> o n", o=1).broadcast_to([P, NE])).then_inc(s_small, 16)
            act.wait_ge(s_zero, 2)
            act.dma_start(wr[:, :, 0:NE], w_router.rearrange("(k p) n -> p k n", p=P)).then_inc(s_small, 16)
            act.wait_ge(s_c, 32)
            A(silu_c[:, :, 0:2], craw[:, :, :].rearrange("p v k -> p k v"), ACT.Silu).then_inc(s_silu, 1)
            for q in range(4):
                act.wait_ge(ada_pe, q + 1)
                A(arow[:, q, :], PS[:, 4 + q, :], ACT.Copy).then_inc(ar_ev, 1)
            act.wait_ge(s_small, 16 * 8)

            nload = [0]

            def load_rows(g, b, scaled):
                nload[0] += 1
                act.dma_start(LG[:, :], g.broadcast_to([P, D])).then_inc(s_lnw, 16)
                act.dma_start(LB[:, :], b.broadcast_to([P, D])).then_inc(s_lnw, 16)
                if scaled:
                    act.wait_ge(s_lnw, 32 * nload[0])
                    A(LG[:, :], LG[:, :], ACT.Copy, scale=ALPHA).then_inc(lnw_sc, 1)
                    A(LB[:, :], LB[:, :], ACT.Copy, scale=ALPHA).then_inc(lnw_sc, 1)

            def tr_evac(first, dst, src_n, sc, sh):
                for q in range(0, DC, 2):
                    i = first + q
                    act.wait_ge(tr_pe, i + 1)
                    src = PS[:, i % 4, 0:src_n]
                    if sc is None:
                        A(dst[:, q, :], src, ACT.Copy).then_inc(tr_act, 1)
                    else:
                        A(dst[:, q, :], src, ACT.Identity, bias=sh[:, q:q + 1], scale=sc[:, q:q + 1]).then_inc(tr_act, 1)

            def m(t, o):
                return t[:, o:o + DC]

            act.wait_ge(ada_ev, 4)
            tr_evac(TR_X, uT, TOK, m(mod[0], SC1), m(mod[0], SH1))
            tr_evac(TR_C, ucT, NX * P, m(modc, SC1), m(modc, SH1))

            def qk_evac(i):
                act.wait_ge(qkT_pe, i + 1)
                if i < NKT:
                    A(kT[:, :, i * P:(i + 1) * P], PS[:, i % 2, 0:NKV * P].rearrange("p (h q) -> p h q", h=NKV),
                      ACT.Copy).then_inc(qk_ev, 1)
                else:
                    h0, j = 4 * ((i - NKT) // NT), (i - NKT) % NT
                    A(qT[:, h0:h0 + 4, j * P:(j + 1) * P], PS[:, i % 2, :].rearrange("p (h q) -> p h q", h=4),
                      ACT.Copy).then_inc(qk_ev, 1)

            for i in range(14):
                bank = PS[:, 4 + i % 3, :]
                nh = NKV if i < NKT else 4
                act.wait_ge(qkv_pe, i + 1)
                if i < NKT:
                    A(V[:, i, :], bank[:, NKV * HD:2 * NKV * HD], ACT.Copy)
                if i:
                    act.wait_ge(ms_done, i)
                for h in range(nh):
                    ins = A(junk[:, h * HD:(h + 1) * HD], bank[:, h * HD:(h + 1) * HD], ACT.Square, accum_out=ss[:, h:h + 1])
                ins.then_inc(sq_done, 1)
                act.wait_ge(ms_done, i + 1)
                A(rt[:, 0:nh], ms[:, 0:nh], ACT.Sqrt).then_inc(sqrt_done, 1)
                if i:
                    qk_evac(i - 1)
            qk_evac(13)
            A(warm[:, :], ones[:, 0:1], ACT.Exp)

            LAG = 2
            NU = NH * NT
            for u in range(NU + LAG):
                if u < NU:
                    act.wait_ge(nm, u + 1)
                    if u >= 3:
                        act.wait_ge(t_pe, u - 2)
                    if u >= 4:
                        act.wait_ge(p_norm, u - 3)
                    A(Pb[:, u % 3, :], PS[:, 2 * (u % 2):2 * (u % 2) + 2, :].rearrange("p b n -> p (b n)")[:, 0:NKT * P],
                      ACT.Exp, bias=nmx[:, u % 4:u % 4 + 1], scale=SCALE, accum_out=den[:, u % 4:u % 4 + 1]
                      ).then_inc(exp_done, 1)
                v = u - LAG
                if v >= 0:
                    if v % NT == 0 and v:
                        h = v // NT - 1
                        act.wait_ge(pv_pe, h + 1)
                        A(uT[:, h, :], PS[:, 6, :], ACT.Copy).then_inc(o_ev, 1)
                    act.wait_ge(t_pe, v + 1)
                    qb = v % NT
                    A(PT[:, 0:3, qb * P:(qb + 1) * P], PS[:, 4, 0:3 * P].rearrange("p (k q) -> p k q", k=3),
                      ACT.Copy).then_inc(pt_act, 1)
                if 1 <= u <= 20:
                    act.wait_ge(ada_pe, u + 4)
                    if u > 1:
                        act.wait_ge(at_pe, u + 3)
                    A(arow1, PS[:, 7, :], ACT.Copy).then_inc(ar_ev, 1)
            act.wait_ge(pv_pe, NH)
            A(uT[:, NH - 1, :], PS[:, 6, :], ACT.Copy).then_inc(o_ev, 1)

            def gate_rows(n):
                act.wait_ge(gb_pe, n + 1)
                A(G[:, :], PS[:, 6:8, :].rearrange("p b n -> p (b n)"), ACT.Copy).then_inc(gb_ev, 1)

            def norm_part(k, tiles, t):
                act.wait_ge(var_rd, k + 1)
                A(rt[:, 0:NT], ms[:, 0:NT], ACT.Sqrt).then_inc(std_rd, 1)
                act.wait_ge(ab_rd, k + 1)
                for j in tiles:
                    A(t[:, j, :], t[:, j, :], ACT.Identity, bias=nb[:, j:j + 1], scale=rs[:, j:j + 1]).then_inc(nrm_act, 1)

            def moe(l):
                act.wait_ge(nrm_act, 4 * l + 2)
                for j in (0, 2):
                    act.dma_start(hscr[l][j * P:(j + 1) * P, :], H[:, j, :]).then_inc(s_hw[l], 16)
                act.wait_ge(ln_nrm, 4 * l + 2)
                for j in (1, 3):
                    act.dma_start(hscr[l][j * P:(j + 1) * P, :], H[:, j, :]).then_inc(s_hw[l], 16)
                tr_evac(TR_R0 if l == 0 else TR_R1, uT, TOK, fsc[:, 2 * l, :], fsh[:, 2 * l, :])
                act.wait_ge(lr_pe, l + 1)
                A(lrow, PS[:, 4, :], ACT.Copy).then_inc(lr_ev, 1)
                A(warm[:, :], ones[:, 0:1], ACT.Sigmoid)
                act.wait_ge(lg_rd, l + 1)
                A(sc_[:, :, :], sel[:, :, :], ACT.Sigmoid).then_inc(sig_rd, 1)
                act.wait_ge(gb_pe, 2 * l + 2)
                A(G[:, 0:512], PS[:, 7, :], ACT.Copy).then_inc(gb_ev, 1)
                act.wait_ge(ln_rd, NT * (2 * l + 1))
                load_rows(ln_g[l, 1:2, :], ln_b[l, 1:2, :], l == 0)
                act.wait_ge(tab_rd, l + 1)
                pairs = act.value_load(table[l][0:1, NE + 1:NE + 2], min_val=1, max_val=MAXB // 2)
                with act.Fori(0, pairs) as gg:
                    A(warm[:, :], ones[:, 0:1], ACT.Silu)
                    for par in range(2):
                        g = gg * 2 + par
                        for h in range(2):
                            act.wait_ge(gu[l][h], g + 1)
                            A(gs[:, 256 * h:256 * h + 256], PS[0:BLK, h, 0:256], ACT.Silu).then_inc(silu_rd[l][h], 1)
                            act.wait_ge(ht_pe[l][h], g + 1)
                            A(hidT[:, 2 * h:2 * h + 2, :], PS[:, 3 + h, 0:2 * BLK].rearrange("p (k s) -> p k s", k=2),
                              ACT.Copy).then_inc(ht_rd[l][h], 1)
                        act.wait_ge(y_ev[l], g + 1)
                        act.nop(nofuse=True)
                        act.dma_start(yscr[l][bass.ds(g * BLK, BLK), :].rearrange("s (q d) -> q s d", q=2),
                                      ysb[par]).then_inc(y_st[l][par], 16)
                norm_part((1, 4)[l], ((0, 2), (0,))[l], H)

            gate_rows(0)
            load_rows(ln_g[0, 0:1, :], ln_b[0, 0:1, :], True)
            norm_part(0, (0, 2), H)
            moe(0)
            act.dma_start(ws, b_ws[0].rearrange("g t s -> t g s")).then_inc(s_ws, 16)
            tr_evac(TR_M1, uT, TOK, fsc[:, 1, :], fsh[:, 1, :])
            act.wait_ge(ln_rd, 2 * NT)
            load_rows(b_vg[0:1, :], b_vb[0:1, :], False)
            for i in range(16):
                half, n, j = i // 8, (i // 4) % 2, i % 4
                act.wait_ge(z_pe, i + 1)
                dst = (zv, zu)[half]
                A(dst[:, j, 512 * n:512 * n + 512], PS[:, 4 + i % 4, :], ACT.Gelu_apprx_tanh).then_inc(z_ev, 1)
                if i == 8:
                    norm_part(2, (), zv)
            gate_rows(2)
            act.wait_ge(v_rd, NT)
            load_rows(ln_g[1, 0:1, :], ln_b[1, 0:1, :], True)
            tr_evac(TR_P1, uT, TOK, None, None)
            norm_part(3, (0, 2), H)
            moe(1)
            for j in (1, 2, 0, 3):
                if j:
                    act.wait_ge(out_rd, j)
                else:
                    act.wait_ge(out0_rd, 1)
                act.dma_start(out[0, j * P:(j + 1) * P, :], H[:, j, :]).then_inc(s_out, 16)
            act.wait_ge(s_out, 16 * NT)

        @block.vector
        def _(dve):
            V_ = nc.vector
            nchain = [0]

            def link(ins):
                nchain[0] += 1
                ins.then_inc(chain, 1)
                dve.wait_ge(chain, nchain[0])

            def rsqrt(n, wait_sem, wait_val):
                dve.wait_ge(wait_sem, wait_val)
                link(V_.reciprocal(rs[:, 0:n], rt[:, 0:n]))
                link(V_.tensor_tensor(nt[:, 0:n], rs[:, 0:n], rs[:, 0:n], ALU.mult))
                link(V_.tensor_tensor(nt[:, 0:n], nt[:, 0:n], ms[:, 0:n], ALU.mult))
                link(V_.tensor_scalar(nt[:, 0:n], nt[:, 0:n], -0.5, 1.5, ALU.mult, ALU.add))
                link(V_.tensor_tensor(rs[:, 0:n], rs[:, 0:n], nt[:, 0:n], ALU.mult))

            dve.wait_ge(s_ic, 1)
            link(V_.tensor_copy(fc[:, :], ic[:, :]))
            dve.wait_ge(s_bT_pe, 1)
            link(V_.tensor_copy(cols[:, :], PS[:, 0, 0:168]))
            for l in range(DEPTH):
                for o in (SC1, SC2):
                    link(V_.tensor_scalar(badaT[:, l, o:o + DC], badaT[:, l, o:o + DC], 1.0, None, ALU.add))

            def ada_evac(q):
                dve.wait_ge(at_pe, q + 1)
                l, qq = divmod(q, 12)
                ps = PS[:, 4 + q if q < 4 else 7, :].rearrange("p (t g v) -> p t v g", t=4, g=4)
                nv = 2 if q < 4 else 1
                link(V_.tensor_reduce(atmp[:, :, 0:nv], ps[:, :, 0:nv, :], AX.X, ALU.add))
                if q < 4:
                    V_.tensor_tensor(modc[:, 4 * q:4 * q + 4], atmp[:, :, 1], badaT[:, 0, 4 * q:4 * q + 4], ALU.add)
                V_.tensor_tensor(mod[l][:, 4 * qq:4 * qq + 4], atmp[:, :, 0],
                                 badaT[:, l, 4 * qq:4 * qq + 4], ALU.add).then_inc(ada_ev, 1)
                dve.wait_ge(ada_ev, q + 1)

            for q in range(4):
                ada_evac(q)

            def tr_evac(first, dst, src_n, sc, sh):
                for q in range(1, DC, 2):
                    i = first + q
                    dve.wait_ge(tr_pe, i + 1)
                    src = PS[:, i % 4, 0:src_n]
                    if sc is None:
                        V_.tensor_copy(dst[:, q, :], src).then_inc(tr_dve, 1)
                    else:
                        V_.tensor_scalar(dst[:, q, :], src, sc[:, q:q + 1], sh[:, q:q + 1], ALU.mult,
                                         ALU.add).then_inc(tr_dve, 1)

            def m(t, o):
                return t[:, o:o + DC]

            tr_evac(TR_X, uT, TOK, m(mod[0], SC1), m(mod[0], SH1))
            tr_evac(TR_C, ucT, NX * P, m(modc, SC1), m(modc, SH1))

            dve.wait_ge(s_small, 16 * 8)
            dve.wait_ge(s_rope, 32)
            for i in range(14):
                bank = PS[:, 4 + i % 3, :]
                nh = NKV if i < NKT else 4
                gain = kg if i < NKT else qg
                dve.wait_ge(sq_done, i + 1)
                V_.tensor_scalar(ms[:, 0:nh], ss[:, 0:nh], 1.0 / HD, EPS, ALU.mult, ALU.add).then_inc(ms_done, 1)
                rsqrt(nh, sqrt_done, i + 1)
                to = rot if i < NX else xn
                if i and i < NX:
                    dve.wait_ge(qkT_pe, i)
                for h in range(nh):
                    ins = V_.scalar_tensor_tensor(out=to[:, h * HD:(h + 1) * HD], in0=bank[:, h * HD:(h + 1) * HD],
                                                  scalar=rs[:, h:h + 1], in1=gain[:, :], op0=ALU.mult, op1=ALU.mult)
                if i < NX:
                    link(ins)
                    V_.tensor_copy(nt[:, 0:1], rs[:, 0:1]).then_inc(xn_done, 1)
                    V_.tensor_copy(nt[:, 1:2], rs[:, 0:1]).then_inc(rot_done, 1)
                    continue
                ins.then_inc(xn_done, 1)
                dve.wait_ge(xn_done, i + 1)
                j = (i - NX) % NT
                xv = xn[:, 0:nh * HD].rearrange("p (h d) -> p h d", h=nh)
                tv = t2[:, 0:nh * HD].rearrange("p (h d) -> p h d", h=nh)
                for par in range(2):
                    ins = V_.tensor_tensor(tv[:, :, par::2], xv[:, :, 1 - par::2],
                                           ropeS[:, j:j + 1, par::2].broadcast_to([P, nh, HD // 2]), ALU.mult)
                link(ins)
                dve.wait_ge(t1_done, i - NX + 1)
                dve.wait_ge(qkT_pe, i)
                V_.tensor_tensor(rot[:, 0:nh * HD], t1[:, 0:nh * HD], t2[:, 0:nh * HD], ALU.add).then_inc(rot_done, 1)

            LAG = 2
            NU = NH * NT
            for u in range(NU + LAG):
                if u < NU:
                    dve.wait_ge(s_pe, u + 1)
                    if u == 0:
                        dve.wait_ge(qkT_pe, 14)
                    link(V_.tensor_reduce(mx[:, u % 4:u % 4 + 1],
                                          PS[:, 2 * (u % 2):2 * (u % 2) + 2, :].rearrange("p b n -> p (b n)")[:, 0:NKT * P],
                                          AX.X, ALU.max))
                    if u >= 4:
                        dve.wait_ge(exp_done, u - 3)
                    V_.tensor_scalar(nmx[:, u % 4:u % 4 + 1], mx[:, u % 4:u % 4 + 1], -SCALE, None,
                                     ALU.mult).then_inc(nm, 1)
                if 2 <= u <= 21:
                    ada_evac(u + 2)
                v = u - LAG
                if v >= 0:
                    dve.wait_ge(t_pe, v + 1)
                    qb = v % NT
                    V_.tensor_copy(PT[:, 3:6, qb * P:(qb + 1) * P],
                                   PS[:, 5, 0:3 * P].rearrange("p (k q) -> p k q", k=3)).then_inc(pt_dve, 1)
                w = u - 1
                if 0 <= w < NU:
                    dve.wait_ge(exp_done, w + 1)
                    link(V_.reciprocal(rden[:, w % 4:w % 4 + 1], den[:, w % 4:w % 4 + 1]))
                    V_.tensor_scalar(Pb[:, w % 3, :], Pb[:, w % 3, :], rden[:, w % 4:w % 4 + 1], None,
                                     ALU.mult).then_inc(p_norm, 1)
            for k, (l, o_sc, o_sh) in enumerate(((0, SC2, SH2), (1, SC1, SH1), (1, SC2, SH2))):
                sc, sh = mod[l][:, o_sc:o_sc + DC], mod[l][:, o_sh:o_sh + DC]
                V_.tensor_tensor(fsc[:, k, :], lngT[:, k, :], sc, ALU.mult)
                link(V_.tensor_tensor(fsh[:, k, :], lnbT[:, k, :], sc, ALU.mult))
                V_.tensor_tensor(fsh[:, k, :], fsh[:, k, :], sh, ALU.add).then_inc(s_fold, 1)
            dve.wait_ge(s_fold, 3)

            def gate_cols(col, n):
                V_.tensor_copy(gcb, col.unsqueeze(2).broadcast_to([P, DC, P])).then_inc(gc_rd, 1)

            def norm_stats(j, r):
                V_.bn_stats(st6[:, j, 0:6], r[:, 0:512])
                link(V_.bn_stats(st6[:, j, 6:12], r[:, 512:1024]))

            def norm_scale(k):
                for j in range(NT):
                    ins = V_.bn_aggr(mv[:, j, :], st6[:, j, :])
                link(ins)
                V_.tensor_scalar(ms[:, 0:NT], mv[:, :, 1], EPS, None, ALU.add).then_inc(var_rd, 1)
                rsqrt(NT, std_rd, k + 1)
                V_.scalar_tensor_tensor(out=nb[:, :], in0=mv[:, :, 0], scalar=-1.0, in1=rs[:, 0:NT], op0=ALU.mult,
                                        op1=ALU.mult).then_inc(ab_rd, 1)

            def norm_tile(t, j, done):
                V_.tensor_scalar(t[:, j, :], t[:, j, :], mv[:, j, 0:1], rs[:, j:j + 1], ALU.subtract,
                                 ALU.mult).then_inc(done, 1)

            def mixer_out(l, k):
                if l:
                    dve.wait_ge(ln_rd, 2 * NT)
                for n in range(2):
                    cut = slice(512 * n, 512 * n + 512)
                    for j in range(NT):
                        r, h = lt[:, j % 2, cut], H[:, j, cut]
                        dve.wait_ge(y_pe[l], NT * n + j + 1)
                        link(V_.tensor_tensor(r, PS[:, 4 * n + j, :], G[:, cut], ALU.mult))
                        link(V_.scalar_tensor_tensor(out=h, in0=h, scalar=ALPHA if l == 0 else 1.0, in1=r,
                                                     op0=ALU.mult, op1=ALU.add))
                        ins = V_.bn_stats(st6[:, j, 6 * n:6 * n + 6], h)
                link(ins)
                norm_scale(k)
                for j in (1, 3):
                    norm_tile(H, j, ln_nrm)

            def first_max(one, v, tmp, dec, mx1, n):
                link(V_.tensor_reduce(mx1, v, AX.X, ALU.max))
                link(V_.tensor_tensor(tmp, v, mx1.unsqueeze(2).broadcast_to([P, NT, n]), ALU.is_equal))
                link(V_.tensor_tensor(tmp, tmp, dec.unsqueeze(1).broadcast_to([P, NT, n]), ALU.mult))
                link(V_.tensor_reduce(mx1, tmp, AX.X, ALU.max))
                link(V_.tensor_tensor(one, tmp, mx1.unsqueeze(2).broadcast_to([P, NT, n]), ALU.is_equal))

            def moe(l):
                tr_evac(TR_R0 if l == 0 else TR_R1, uT, TOK, fsc[:, 2 * l, :], fsh[:, 2 * l, :])
                gate_cols(m(mod[l], G2), 2 * l + 1)
                dve.wait_ge(lg_pe, l + 1)
                V_.tensor_reduce(sel[:, :, :], PS[:, 5, :].rearrange("p (t g e) -> p t e g", t=NT, g=4)[:, :, 0:NE, :],
                                 AX.X, ALU.add).then_inc(lg_rd, 1)
                dve.wait_ge(sig_rd, l + 1)
                link(V_.tensor_tensor(sel[:, :, :], sc_[:, :, :], rb[:, :].unsqueeze(1).broadcast_to([P, NT, NE]), ALU.add))
                sv = sel[:, :, :].rearrange("p t (g e) -> p (t g) e", g=NG)
                V_.tensor_tensor(s6[:, :, 0:2], sv[:, :, 0:4:2], sv[:, :, 1:4:2], ALU.add)
                V_.tensor_tensor(s6[:, :, 2:4], sv[:, :, 0:2], sv[:, :, 2:4], ALU.add)
                V_.tensor_tensor(s6[:, :, 4:5], sv[:, :, 0:1], sv[:, :, 3:4], ALU.add)
                link(V_.tensor_tensor(s6[:, :, 5:6], sv[:, :, 1:2], sv[:, :, 2:3], ALU.add))
                link(V_.tensor_reduce(g4[:, :, :].rearrange("p t g -> p (t g)"), s6[:, :, :], AX.X, ALU.max))
                first_max(gmask[:, :, :], g4[:, :, :], cand[:, :, 0:NG], dec4, gm1[:, :], NG)
                link(V_.tensor_scalar(g4[:, :, :], gmask[:, :, :], BIG, -BIG, ALU.mult, ALU.add))
                pv = g4[:, :, :].rearrange("p t g -> p (t g)").unsqueeze(2).broadcast_to([P, NT * NG, PER])
                link(V_.tensor_tensor(sv, sv, pv, ALU.add))
                first_max(o1[:, :, :], sel[:, :, :], cand[:, :, :], dec16, gm1[:, :], NE)
                link(V_.scalar_tensor_tensor(out=sel[:, :, :], in0=o1[:, :, :], scalar=-3e38, in1=sel[:, :, :],
                                             op0=ALU.mult, op1=ALU.add))
                first_max(o2[:, :, :], sel[:, :, :], cand[:, :, :], dec16, gm1[:, :], NE)
                V_.memset(MP[:, 0, :], 0.0)
                link(V_.tensor_tensor(cand[:, :, :], o1[:, :, :], o2[:, :, :], ALU.add))
                link(V_.tensor_copy(MP[:, 1, :], cand[:, 0, :]))
                for j in range(1, NT):
                    ins = V_.tensor_tensor(MP[:, j + 1, :], MP[:, j, :], cand[:, j, :], ALU.add)
                    if j < NT - 1:
                        link(ins)
                ins.then_inc(m_rd, 1)
                for k, o in enumerate((o1, o2)):
                    link(V_.tensor_tensor(smap[:, :, :], sc_[:, :, :], o[:, :, :], ALU.mult))
                    link(V_.tensor_reduce(wts[:, k, :], smap[:, :, :], AX.X, ALU.add))
                link(V_.tensor_tensor(wsum[:, :], wts[:, 0, :], wts[:, 1, :], ALU.add))
                link(V_.reciprocal(wsum[:, :], wsum[:, :]))
                link(V_.tensor_tensor(wts[:, :, :], wts[:, :, :], wsum[:, :].unsqueeze(1).broadcast_to([P, 2, NT]), ALU.mult))
                dve.wait_ge(rk_pe, l + 1)
                link(V_.tensor_tensor(gtn[:, :, :], PS[:, 5, 64:80].unsqueeze(2).broadcast_to([P, NE, NTHR]),
                                      thr.unsqueeze(1).broadcast_to([P, NE, NTHR]), ALU.is_gt))
                link(V_.tensor_reduce(nbk[:, :], gtn[:, :, :], AX.X, ALU.add))
                link(V_.tensor_scalar(nbk[:, :], nbk[:, :], 1.0, None, ALU.add))
                V_.memset(bs[:, 0:1], 0.0)
                link(V_.tensor_tensor_scan(bs[:, 1:NE + 1], ones[:, 0:NE], nbk[:, :], 0.0, ALU.mult, ALU.add))
                link(V_.tensor_tensor(gpr[:, :], bs[:, NE:NE + 1].broadcast_to([P, MAXB // 2]), even, ALU.is_gt))
                link(V_.tensor_reduce(bs[:, NE + 1:NE + 2], gpr[:, :], AX.X, ALU.add))
                V_.tensor_scalar(first_slot[:, :], bs[:, 0:NE], float(BLK), None, ALU.mult)
                link(V_.tensor_scalar(bs[:, NE + 2:NE + 3], bs[:, NE + 1:NE + 2], 2.0, None, ALU.mult))
                V_.tensor_copy(table[l][:, :], bs[0:1, :]).then_inc(tab_rd, 1)
                link(V_.tensor_tensor(smap[:, :, :], PS[:, 5, 0:64].rearrange("p (t e) -> p t e", t=NT),
                                      first_slot[:, 0:NE].unsqueeze(1).broadcast_to([P, NT, NE]), ALU.add))
                for k, o in enumerate((o1, o2)):
                    link(V_.tensor_tensor(cand[:, :, :], smap[:, :, :], o[:, :, :], ALU.mult))
                    link(V_.tensor_reduce(slot[:, k, :], cand[:, :, :], AX.X, ALU.add))
                V_.tensor_copy(yidx[:, :, :], slot[:, :, :])
                link(V_.tensor_copy(srel[:, :, :], slot[:, :, :]))

                loop = dlp[l]

                def onehot(lnk):
                    it = iota_s.unsqueeze(1).broadcast_to([P, NT, BLK])
                    V_.tensor_tensor(oh, srel[:, 0, :].unsqueeze(2).broadcast_to([P, NT, BLK]), it, ALU.is_equal)
                    lnk(V_.tensor_tensor(oh2t, srel[:, 1, :].unsqueeze(2).broadcast_to([P, NT, BLK]), it, ALU.is_equal))
                    V_.tensor_tensor(oh, oh, oh2t, ALU.add).then_inc(oh_rd[l], 1)
                    lnk(V_.tensor_scalar(srel[:, :, :], srel[:, :, :], -float(BLK), None, ALU.add))

                def index(par):
                    V_.tensor_copy(gidx[0:BLK, par:par + 1], PS[0:BLK, 6, 0:1]).then_inc(ix_rd[l], 1)

                def x_evac(lnk):
                    lnk(V_.tensor_tensor(xTt, PS[:, 2, :].rearrange("p (c s) -> p c s", c=DC),
                                         fsc[:, 2 * l, :].unsqueeze(2).broadcast_to([P, DC, BLK]), ALU.mult))
                    V_.tensor_tensor(xT, xTt, fsh[:, 2 * l, :].unsqueeze(2).broadcast_to([P, DC, BLK]),
                                     ALU.add).then_inc(xT_rd[l], 1)

                onehot(link)
                for b in range(3):
                    if b == 2:
                        dve.wait_ge(x0_in[l], 16)
                    dve.wait_ge(ix_pe[l], b + 1)
                    index(b % 2)
                    onehot(link)
                dve.wait_ge(xt_pe[l], 1)
                x_evac(link)
                dve.wait_ge(gb_ev, 2 * l + 2)
                pairs = dve.value_load(table[l][0:1, NE + 1:NE + 2], min_val=1, max_val=MAXB // 2)
                with dve.Fori(0, pairs) as gg:
                    k = [0]

                    def lnk(ins):
                        k[0] += 1
                        ins.then_inc(loop, 1)
                        dve.wait_ge(loop, gg * 6 + k[0])

                    for par in range(2):
                        g = gg * 2 + par
                        for h in range(2):
                            dve.wait_ge(silu_rd[l][h], g + 1)
                            V_.tensor_tensor(hid[:, 256 * h:256 * h + 256], gs[:, 256 * h:256 * h + 256],
                                             PS[BLK:P, h, 0:256], ALU.mult).then_inc(hid_rd[l][h], 1)
                        dve.wait_ge(xt_pe[l], g + 2)
                        x_evac(lnk)
                        dve.wait_ge(xg_in[l], g * 16 + 16)
                        dve.wait_ge(ix_pe[l], g + 4)
                        index(1 - par)
                        onehot(lnk)
                        dve.wait_ge(y_st[l][par], gg * 16 + 16)
                        dve.wait_ge(dn_pe[l], g + 1)
                        V_.tensor_tensor(ysb[par], PS[:, 5, :], G[:, 0:512], ALU.mult).then_inc(y_ev[l], 1)
                    assert k[0] == 6

                dve.wait_ge(ln_rd, NT * (2 * l + 1))
                for j in range(NT):
                    h = H[:, j, :]
                    dve.wait_ge(fg[l][j % 2], 32 * (j // 2 + 1))
                    link(V_.scalar_tensor_tensor(out=h, in0=yg[:, j % 2, 0, :], scalar=wts[:, 0, j:j + 1], in1=h,
                                                 op0=ALU.mult, op1=ALU.add))
                    V_.scalar_tensor_tensor(out=h, in0=yg[:, j % 2, 1, :], scalar=wts[:, 1, j:j + 1], in1=h,
                                            op0=ALU.mult, op1=ALU.add).then_inc(fg_used, 1)
                    dve.wait_ge(fg_used, l * NT + j + 1)
                    norm_stats(j, h)
                norm_scale((1, 4)[l])
                if l < DEPTH - 1:
                    for j in (1, 3):
                        norm_tile(H, j, ln_nrm)
                    return
                dve.wait_ge(s_lnw, 32 * 5)
                for j in range(1, NT):
                    h = H[:, j, :]
                    link(V_.scalar_tensor_tensor(out=h, in0=h, scalar=mv[:, j, 0:1], in1=LG[:, :], op0=ALU.subtract,
                                                 op1=ALU.mult))
                    V_.scalar_tensor_tensor(out=h, in0=h, scalar=rs[:, j:j + 1], in1=LB[:, :], op0=ALU.mult,
                                            op1=ALU.add).then_inc(out_rd, 1)

            dve.wait_ge(pv_pe, NH)
            gate_cols(m(mod[0], G1), 0)
            dve.wait_ge(gb_ev, 1)
            mixer_out(0, 0)
            moe(0)
            tr_evac(TR_M1, uT, TOK, fsc[:, 1, :], fsh[:, 1, :])
            gate_cols(m(mod[1], G1), 2)
            dve.wait_ge(wsT_pe, 1)
            V_.tensor_copy(wsT, PS[:, 0:2, :].rearrange("p b (g t) -> p (b g) t", g=4)).then_inc(wsT_ev, 1)
            for j in range(NT):
                dve.wait_ge(z_ev, 4 + j + 1)
                norm_stats(j, zv[:, j, :])
            norm_scale(2)
            for j in range(NT):
                norm_tile(zv, j, vn)
            dve.wait_ge(z_ev, 16)
            for g in range(8):
                dve.wait_ge(mix_pe, g + 1)
                o = zu[:, :, g * P:(g + 1) * P]
                V_.scalar_tensor_tensor(out=o, in0=PS[:, g % 4, :].rearrange("p (t d) -> p t d", t=NT),
                                        scalar=bsT[:, g:g + 1], in1=o, op0=ALU.add, op1=ALU.mult).then_inc(mix_ev, 1)
            tr_evac(TR_P1, uT, TOK, None, None)
            dve.wait_ge(gb_ev, 3)
            mixer_out(1, 3)
            moe(1)

        @block.tensor
        def _(pe):
            mm = nc.tensor.matmul

            def weights(n):
                b, number = place[n]
                pe.wait_ge(w_in[b], 16 * number)
                return slots[b].rearrange("p (k n) -> p k n", k=DC)

            def ada_rows(q, n):
                w = weights(n)
                if q > 4:
                    pe.wait_ge(ada_ev, q)
                bank = 4 + q if q < 4 else 7
                for kk in range(2):
                    for g in range(4):
                        k = 2 * g + kk
                        ins = mm(PS[32 * g:32 * g + 32, bank, :], silu_c[:, k, :], w[:, k, :],
                                 start=(kk == 0), stop=(kk == 1))
                ins.then_inc(ada_pe, 1)

            def ada_turn(q):
                pe.wait_ge(ar_ev, q + 1)
                src = arow[:, q, :] if q < 4 else arow1
                bank = 4 + q if q < 4 else 7
                for t in range(4):
                    ins = nc.tensor.transpose(PS[:, bank, t * P:(t + 1) * P], src[:, t * P:(t + 1) * P], ident[:, :])
                ins.then_inc(at_pe, 1)

            pe.wait_ge(s_const, 2)
            pe.wait_ge(s_small, 16 * 8)
            nc.tensor.transpose(PS[:, 0, 0:128], rows1, ident[:, :])
            nc.tensor.transpose(PS[:, 0, 128:168], rows2, ident[0:40, 0:40]).then_inc(s_bT_pe, 1)
            pe.wait_ge(s_silu, 1)

            n = 0
            for q in range(4):
                ada_rows(q, n)
                n += 1
                if q:
                    ada_turn(q - 1)
            ada_turn(3)

            def tr_items(first, srcs):
                for q in range(DC):
                    i = first + q
                    if i >= 4:
                        tr_wait(pe, i - 4)
                    for j, s in enumerate(srcs):
                        ins = nc.tensor.transpose(PS[:, i % 4, j * P:(j + 1) * P], s[:, q * P:(q + 1) * P], ident[:, :])
                    ins.then_inc(tr_pe, 1)

            pe.wait_ge(s_x, 16)
            pe.wait_ge(ada_ev, 1)
            tr_items(TR_X, [H[:, j, :] for j in range(NT)])
            pe.wait_ge(s_ctx, 16)
            tr_items(TR_C, [ctxn[:, j, :] for j in range(NX)])
            tr_wait(pe, TR_C + DC - 2)
            tr_wait(pe, TR_C + DC - 1)

            def qk_turn(i):
                nh = NKV if i < NKT else 4
                pe.wait_ge(rot_done, i + 1)
                if i >= 2:
                    pe.wait_ge(qk_ev, i - 1)
                for h in range(nh):
                    ins = nc.tensor.transpose(PS[:, i % 2, h * P:(h + 1) * P], rot[:, h * HD:(h + 1) * HD], ident[:, :])
                ins.then_inc(qkT_pe, 1)

            for i in range(14):
                ctx_item = i < NX
                if i in (0, NKT, NKT + NT):
                    w = weights(n)
                if i >= 3:
                    pe.wait_ge(xn_done, i - 2)
                j = i if ctx_item else (i - NX) % NT
                a = ucT if ctx_item else uT
                for k in range(DC):
                    ins = mm(PS[:, 4 + i % 3, :], a[:, k, j * P:(j + 1) * P], w[:, k, :], start=(k == 0), stop=(k == DC - 1))
                ins.then_inc(qkv_pe, 1)
                if i in (NKT - 1, NKT + NT - 1, NKT + 2 * NT - 1):
                    n += 1
                if i:
                    qk_turn(i - 1)
            qk_turn(13)
            pe.wait_ge(qk_ev, 14)

            LAG = 2
            NU = NH * NT

            def pv(h):
                pe.wait_ge(pt_act, NT * (h + 1))
                pe.wait_ge(pt_dve, NT * (h + 1))
                if h:
                    pe.wait_ge(o_ev, h)
                kv = h // (NH // NKV)
                for k in range(NKT):
                    ins = mm(PS[:, 6, :], V[:, k, kv * HD:(kv + 1) * HD], PT[:, k, :], start=(k == 0), stop=(k == NKT - 1))
                ins.then_inc(pv_pe, 1)

            for u in range(NU + LAG):
                if u < NU:
                    h, qb = u // NT, u % NT
                    kv = h // (NH // NKV)
                    if u >= 2:
                        pe.wait_ge(exp_done, u - 1)
                    b = 2 * (u % 2)
                    q = qT[:, h, qb * P:(qb + 1) * P]
                    mm(PS[:, b, :], q, kT[:, kv, 0:512], start=True, stop=True)
                    mm(PS[:, b + 1, 0:NKT * P - 512], q, kT[:, kv, 512:NKT * P], start=True, stop=True).then_inc(s_pe, 1)
                v = u - LAG
                if 2 <= u <= 21:
                    ada_turn(u + 2)
                if v >= 0:
                    if v % NT == 0 and v:
                        pv(v // NT - 1)
                    pe.wait_ge(p_norm, v + 1)
                    if v:
                        pe.wait_ge(pt_act, v)
                        pe.wait_ge(pt_dve, v)
                    for k in range(NKT):
                        ins = nc.tensor.transpose(PS[:, 4 + k // 3, (k % 3) * P:(k % 3 + 1) * P],
                                                  Pb[:, v % 3, k * P:(k + 1) * P], ident[:, :])
                    ins.then_inc(t_pe, 1)
                if 1 <= u <= 20:
                    ada_rows(u + 3, n)
                    n += 1
            pv(NH - 1)
            pe.wait_ge(o_ev, NH)

            def gate_rows(k):
                pe.wait_ge(gc_rd, k + 1)
                for f in range(DC):
                    ins = mm(PS[:, 6 + f // 4, (f % 4) * P:(f % 4 + 1) * P], gcb[:, f, :], ident[:, :], start=True, stop=True)
                ins.then_inc(gb_pe, 1)
                pe.wait_ge(gb_ev, k + 1)

            def project(l, n):
                for half in range(2):
                    w = weights(n)
                    for j in range(NT):
                        for k in range(DC):
                            ins = mm(PS[:, 4 * half + j, :], uT[:, k, j * P:(j + 1) * P], w[:, k, :],
                                     start=(k == 0), stop=(k == DC - 1))
                        ins.then_inc(y_pe[l], 1)
                    n += 1
                return n

            def moe(l):
                pe.wait_ge(nrm_act, 4 * l + 2)
                pe.wait_ge(ln_nrm, 4 * l + 2)
                tr_items(TR_R0 if l == 0 else TR_R1, [H[:, j, :] for j in range(NT)])
                last = (TR_R0 if l == 0 else TR_R1) + DC - 1
                tr_wait(pe, last - 1)
                tr_wait(pe, last)
                for kk in range(2):
                    for g in range(4):
                        k = 2 * g + kk
                        ins = mm(PS[32 * g:32 * g + 32, 4, :], wr[:, k, :], uT[:, k, :], start=(kk == 0), stop=(kk == 1))
                ins.then_inc(lr_pe, 1)
                pe.wait_ge(lr_ev, l + 1)
                for j in range(NT):
                    ins = nc.tensor.transpose(PS[:, 5, j * P:(j + 1) * P], lrow[:, j * P:(j + 1) * P], ident[:, :])
                ins.then_inc(lg_pe, 1)
                pe.wait_ge(gc_rd, 2 * l + 2)
                for f in range(DC):
                    half = f // 4
                    ins = mm(PS[BLK * half:BLK * half + BLK, 7, (f % 4) * P:(f % 4 + 1) * P], gcb[:, f, 0:BLK],
                             ident[:, :], start=True, stop=True)
                ins.then_inc(gb_pe, 1)
                pe.wait_ge(m_rd, l + 1)
                mflat = cand[:, :, :].rearrange("p t e -> p (t e)")
                mm(PS[:, 5, 0:64], tri[:, :], mflat, start=True, stop=False)
                mm(PS[:, 5, 0:64], ones[:, :], MP[:, 0:NT, :].rearrange("p t e -> p (t e)"), start=False, stop=True)
                mm(PS[:, 5, 64:80], ones[:, :], MP[:, NT, :], start=True, stop=True).then_inc(rk_pe, 1)

                def index():
                    for j in range(NT):
                        ins = mm(PS[0:BLK, 6, 0:1], oh[:, j, :], tokid[:, j:j + 1], start=(j == 0), stop=(j == NT - 1))
                    ins.then_inc(ix_pe[l], 1)

                def turn_x():
                    for f in range(DC):
                        ins = nc.tensor.transpose(PS[:, 2, f * BLK:(f + 1) * BLK], xg[:, f * P:(f + 1) * P],
                                                  ident[0:BLK, 0:BLK])
                    ins.then_inc(xt_pe[l], 1)

                for b in range(3):
                    pe.wait_ge(oh_rd[l], b + 1)
                    if b:
                        pe.wait_ge(ix_rd[l], b)
                    index()
                pe.wait_ge(x0_in[l], 16)
                turn_x()
                pe.wait_ge(tab_rd, l + 1)

                def expert(t, par, e):
                    col = lambda o: bass.ds(t * 3 + (par + o), 1) if e is None else slice(e + o, e + o + 1)
                    lo = pe.value_load(table[l][0:1, col(0)], min_val=0, max_val=MAXB)
                    hi = pe.value_load(table[l][0:1, col(1)], min_val=1, max_val=MAXB)

                    def landed(j):
                        b, number = moe_place[l][par][j]
                        pe.wait_ge(w_in[b], t * 16 + 16 * number)

                    wg, wu, wd = (slots[b].rearrange("p (k n) -> p k n", k=kt)
                                  for (b, _), kt in zip(moe_place[l][par], (DC, DC, FC)))
                    with pe.Fori(lo, hi) as g:
                        pe.wait_ge(xT_rd[l], g + 1)
                        landed(0)
                        landed(1)
                        for h in range(2):
                            for k in range(DC):
                                mm(PS[0:BLK, h, 0:256], xT[:, k, :], wg[:, k, 256 * h:256 * h + 256],
                                   start=(k == 0), stop=(k == DC - 1))
                                ins = mm(PS[BLK:P, h, 0:256], xT[:, k, :], wu[:, k, 256 * h:256 * h + 256],
                                         start=(k == 0), stop=(k == DC - 1))
                            ins.then_inc(gu[l][h], 1)

                        def turn_hidden(h):
                            pe.wait_ge(hid_rd[l][h], g + 1)
                            pe.nop(nofuse=True)
                            for f in range(2):
                                ins = nc.tensor.transpose(PS[:, 3 + h, f * BLK:(f + 1) * BLK],
                                                          hid[:, (2 * h + f) * P:(2 * h + f + 1) * P],
                                                          ident[0:BLK, 0:BLK])
                            ins.then_inc(ht_pe[l][h], 1)

                        turn_hidden(0)
                        pe.wait_ge(xg_rd[l], g + 1)
                        pe.nop(nofuse=True)
                        turn_x()
                        landed(2)

                        def down(h):
                            pe.wait_ge(ht_rd[l][h], g + 1)
                            for k in (2 * h, 2 * h + 1):
                                for half in range(2):
                                    ins = mm(PS[BLK * half:BLK * half + BLK, 5, :], hidT[:, k, :],
                                             wd[:, k, 512 * half:512 * half + 512],
                                             start=(k == 0), stop=(k == FC - 1))
                            return ins

                        down(0)
                        turn_hidden(1)
                        pe.wait_ge(oh_rd[l], g + 4)
                        pe.wait_ge(ix_rd[l], g + 3)
                        index()
                        down(1).then_inc(dn_pe[l], 1)

                with pe.Fori(0, NE // 3) as t:
                    for par in range(3):
                        expert(t, par, None)
                expert(NE // 3, 0, NE - 1)
                total = pe.value_load(table[l][0:1, NE:NE + 1], min_val=1, max_val=MAXB)
                filled = pe.value_load(table[l][0:1, NE + 2:NE + 3], min_val=1, max_val=MAXB)
                with pe.If(total < filled):
                    g = total

                    def hand_on(sem, *waits):
                        for w, v in waits:
                            pe.wait_ge(w, v)
                            pe.nop(nofuse=True)
                        pe.nop(nofuse=True).then_inc(sem, 1)

                    hand_on(gu[l][0], (xT_rd[l], g + 1))
                    hand_on(gu[l][1])
                    hand_on(ht_pe[l][0], (hid_rd[l][0], g + 1))
                    hand_on(xt_pe[l], (xg_rd[l], g + 1))
                    hand_on(ht_pe[l][1], (ht_rd[l][0], g + 1), (hid_rd[l][1], g + 1))
                    hand_on(ix_pe[l], (oh_rd[l], g + 4), (ix_rd[l], g + 3))
                    hand_on(dn_pe[l], (ht_rd[l][1], g + 1))

            gate_rows(0)
            n = project(0, n)
            moe(0)
            pe.wait_ge(nrm_act, 4)
            pe.wait_ge(ln_nrm, 4)
            tr_items(TR_M1, [H[:, j, :] for j in range(NT)])
            tr_wait(pe, TR_M1 + DC - 2)
            tr_wait(pe, TR_M1 + DC - 1)
            pe.wait_ge(s_ws, 16)
            for g in range(8):
                ins = nc.tensor.transpose(PS[:, g // 4, (g % 4) * P:(g % 4 + 1) * P], ws[:, g, :], ident[:, :])
            ins.then_inc(wsT_pe, 1)
            n = S0
            for i in range(16):
                if i % 4 == 0:
                    w = weights(n)
                if i >= 4:
                    pe.wait_ge(z_ev, i - 3)
                j = i % 4
                for k in range(DC):
                    ins = mm(PS[:, 4 + i % 4, :], uT[:, k, j * P:(j + 1) * P], w[:, k, :], start=(k == 0), stop=(k == DC - 1))
                ins.then_inc(z_pe, 1)
                if i % 4 == 3:
                    n += 1
            pe.wait_ge(z_ev, 16)
            gate_rows(2)
            pe.wait_ge(wsT_ev, 1)
            pe.wait_ge(v_rd, NT)
            for g in range(8):
                if g >= 4:
                    pe.wait_ge(mix_ev, g - 3)
                mm(PS[:, g % 4, :], wsT[:, g, :], zv[:, :, g * P:(g + 1) * P], start=True, stop=True).then_inc(mix_pe, 1)
            pe.wait_ge(mix_ev, 8)
            tr_items(TR_P1, [zu[:, j, :] for j in range(NT)])
            tr_wait(pe, TR_P1 + DC - 2)
            tr_wait(pe, TR_P1 + DC - 1)
            n = project(1, n)
            moe(1)


_INS = ['x', 'c', 'ctx', 'c_ctx', 'w_ada', 'b_ada', 'ln_g', 'ln_b', 'a_wqkv', 'a_qg', 'a_kg', 'a_wo', 'b_win', 'b_vg',
        'b_vb', 'b_ws', 'b_bs', 'b_wout', 'w_router', 'router_bias', 'e_gate', 'e_up', 'e_down']
_OUT = ((1, 512, 1024), 'float32')
GRID_W, HEAD_DIM, ROPE_THETA = 64, 128, 10000.0


def rope_tables(n):
    import numpy as np
    half = HEAD_DIM // 2
    inv = (np.float32(1.0) / (np.float32(ROPE_THETA) ** (np.arange(0, half, 2, dtype=np.float32) / np.float32(half))))
    t = np.arange(n)
    ang = np.concatenate([(t // GRID_W).astype(np.float32)[:, None] * inv,
                          (t % GRID_W).astype(np.float32)[:, None] * inv], -1)
    cos, sin = np.cos(ang), np.sin(ang)
    return (np.repeat(cos, 2, axis=1).astype(np.float32),
            np.stack([-sin, sin], -1).reshape(n, HEAD_DIM).astype(np.float32))


def kernel(**inputs):
    import numpy as _np
    import concourse.bacc as _bacc
    from concourse import mybir as _mybir
    from concourse.bass_utils import run_bass_kernel_spmd as _run

    nc = _bacc.Bacc("TRN2", target_bir_lowering=False, num_devices=1)
    arrays, args = {}, []
    for name in _INS:
        a = _np.ascontiguousarray(inputs[name])
        arrays[f"in_{name}_dram"] = a
        args.append(nc.dram_tensor(f"in_{name}_dram", a.shape, _mybir.dt.from_np(a.dtype), kind="ExternalInput").ap())
    for name, a in zip(("rope_cos", "rope_sin"), rope_tables(512)):
        arrays[f"{name}_dram"] = a
        args.append(nc.dram_tensor(f"{name}_dram", a.shape, _mybir.dt.from_np(a.dtype), kind="ExternalInput").ap())
    shape, dtype = _OUT
    args.append(nc.dram_tensor("out_0_dram", shape, _mybir.dt.from_np(_np.dtype(dtype)), kind="ExternalOutput").ap())
    backbone(nc, *args)
    r = _run(nc, [arrays], core_ids=[0])
    return r.results[0]["out_0_dram"]
```
